# Optimizing a Trainium2 kernel written in Bass

```python
import jax, jax.numpy as jnp
from jax import lax
import numpy as np

D_MODEL = 1024
BATCH = 1
SEQ = 1024
DEPTH = 1
DEC_BATCH = 8
DEC_SEQ = 1
PAST_LEN = 2048
PAGE_SIZE = 128

N_HEADS = 8
HEAD_DIM = 64
N_KV_HEADS = 2
GROUP = N_HEADS // N_KV_HEADS
ROT_DIM = HEAD_DIM // 4
ROPE_THETA = 500000.0
CMP_BLOCK = 32
CMP_STRIDE = 16
CMP_HIDDEN = 64
SEL_BLOCK = 64
N_SEL = 16
SEL_FORCE = 1.0e6
WINDOW = 512
Q_BLOCK = 128
D_RNN = D_MODEL
RNN_BLOCKS = 8
RNN_BW = D_RNN // RNN_BLOCKS
CONV_W = 4
RG_C = 8.0
N_EXPERTS = 64
TOP_K = 6
D_EXPERT = 256
D_SHARED = 256
ROUTED_SCALE = 2.5
MOE_BLOCK = 128
DN_ALPHA = (2.0 * DEPTH) ** 0.25
DN_BETA = (8.0 * DEPTH) ** -0.25
LN_EPS = 1e-5
Q_WIDTH = N_HEADS * HEAD_DIM
KV_WIDTH = 2 * N_KV_HEADS * HEAD_DIM
IN_SPLITS = (Q_WIDTH, KV_WIDTH, KV_WIDTH, KV_WIDTH, 3 * N_HEADS, D_RNN, D_RNN, D_MODEL, D_MODEL)
N_IN = sum(IN_SPLITS)
F32 = jnp.float32

kernel_name = 'hybrid_nsa_rglru_moe_deepnorm_step'

def layer_norm(x, g, b):
    xf = x.astype(F32)
    mu = jnp.mean(xf, axis=-1, keepdims=True)
    var = jnp.mean(jnp.square(xf - mu), axis=-1, keepdims=True)
    return ((xf - mu) * lax.rsqrt(var + LN_EPS) * g + b).astype(x.dtype)

def masked_softmax(s, mask):
    s = jnp.where(mask, s.astype(F32), -jnp.inf)
    m = jnp.max(s, axis=-1, keepdims=True)
    m = jnp.where(jnp.isfinite(m), m, 0.0)
    e = jnp.exp(s - m)
    return e / jnp.maximum(jnp.sum(e, axis=-1, keepdims=True), 1e-30)

def rope_partial(x, pos):
    half = ROT_DIM // 2
    inv = ROPE_THETA ** (-(jnp.arange(half, dtype=F32) * (2.0 / ROT_DIM)))
    ang = pos.astype(F32)[:, None] * inv[None, :]
    cos = jnp.cos(ang)[None, :, None, :]
    sin = jnp.sin(ang)[None, :, None, :]
    xf = x.astype(F32)
    x1, x2 = xf[..., :half], xf[..., half:ROT_DIM]
    out = jnp.concatenate([x1 * cos - x2 * sin, x2 * cos + x1 * sin, xf[..., ROT_DIM:]], axis=-1)
    return out.astype(x.dtype)

def rope_keys(kv, pos):
    return jnp.stack([rope_partial(kv[:, :, 0], pos), kv[:, :, 1]], axis=2)

def mixer_inputs(x, pos, w_in):
    B, T, _ = x.shape
    offs = [int(o) for o in np.cumsum(IN_SPLITS)[:-1]]
    uq, ukc, uks, ukw, ug_nsa, u_rnn, u_gate, g_a, g_b = jnp.split(
        jnp.einsum('btd,dn->btn', x, w_in), offs, axis=-1)
    q = uq.reshape(B, T, N_HEADS, HEAD_DIM)
    q_rot = rope_partial(q, pos).reshape(B, T, N_KV_HEADS, GROUP, HEAD_DIM)
    q = q.reshape(B, T, N_KV_HEADS, GROUP, HEAD_DIM)
    kv_shape = (B, T, 2, N_KV_HEADS, HEAD_DIM)
    kv_c = ukc.reshape(kv_shape)
    kv_s = rope_keys(uks.reshape(kv_shape), pos)
    kv_w = rope_keys(ukw.reshape(kv_shape), pos)
    gates = jax.nn.sigmoid(ug_nsa.astype(F32)).reshape(B, T, N_KV_HEADS, GROUP, 3)
    return q, q_rot, kv_c, kv_s, kv_w, gates, u_rnn, u_gate, g_a, g_b

def compress(rows, pos_emb, w1, w2):
    B, T = rows.shape[:2]
    n_chunk = T // CMP_STRIDE
    parts = CMP_BLOCK // CMP_STRIDE
    n_cmp = n_chunk - parts + 1
    ch = rows[:, :n_chunk * CMP_STRIDE].reshape(B, n_chunk, CMP_STRIDE, N_KV_HEADS, HEAD_DIM)
    w1p = w1.reshape(parts, CMP_STRIDE, HEAD_DIM, CMP_HIDDEN)
    pep = pos_emb.reshape(parts, CMP_STRIDE, HEAD_DIM)
    hid = 0.0
    for m in range(parts):
        part = jnp.einsum('bnshd,sdf->bnhf', ch, w1p[m]) + jnp.einsum('sd,sdf->f', pep[m], w1p[m])
        hid = hid + part[:, m:m + n_cmp]
    return jnp.einsum('bnhf,fd->bnhd', jax.nn.gelu(hid), w2)

def sel_map(n_cmp, n_sel):
    ratio = SEL_BLOCK // CMP_STRIDE
    d = jnp.arange(n_cmp)[:, None] - ratio * jnp.arange(n_sel)[None, :]
    return sum(((d + n >= 0) & (d + n < ratio)).astype(F32) for n in range(CMP_BLOCK // CMP_STRIDE))

def nsa_core(q, q_rot, q_pos, kc, vc, c_end, fetch_sel, n_sel_blocks, kv_w, w_pos, gates):
    B, Tq = q.shape[:2]
    scale = HEAD_DIM ** -0.5
    s_c = jnp.einsum('bqhgd,bchd->bhgqc', q, kc).astype(F32) * scale
    p_c = masked_softmax(s_c, c_end[None, :] <= q_pos[:, None])
    o_c = jnp.einsum('bhgqc,bchd->bqhgd', p_c, vc.astype(F32))
    imp = jnp.einsum('bhgqc,cs->bhqs', p_c, sel_map(kc.shape[1], n_sel_blocks))
    blk = jnp.arange(n_sel_blocks)[None, :]
    cur = (q_pos // SEL_BLOCK)[:, None]
    forced = (blk == 0) | (blk == cur) | (blk == cur - 1)
    score = jnp.where(blk > cur, -jnp.inf, jnp.where(forced, SEL_FORCE, imp))
    n = min(N_SEL, n_sel_blocks)
    _, idx = lax.top_k(score, n)
    idx = idx.transpose(0, 2, 1, 3)
    kv_s = fetch_sel(idx)
    k_s = kv_s[..., 0, :].reshape(B, Tq, N_KV_HEADS, n * SEL_BLOCK, HEAD_DIM)
    v_s = kv_s[..., 1, :].reshape(B, Tq, N_KV_HEADS, n * SEL_BLOCK, HEAD_DIM)
    pos_s = (idx[..., None] * SEL_BLOCK + jnp.arange(SEL_BLOCK)).reshape(B, Tq, N_KV_HEADS, n * SEL_BLOCK)
    m_s = (pos_s <= q_pos[None, :, None, None]).transpose(0, 2, 1, 3)[:, :, None]
    s_s = jnp.einsum('bqhgd,bqhkd->bhgqk', q_rot, k_s).astype(F32) * scale
    o_s = jnp.einsum('bhgqk,bqhkd->bqhgd', masked_softmax(s_s, m_s), v_s.astype(F32))
    diff = q_pos[:, None] - w_pos[None, :]
    m_w = (diff >= 0) & (diff <= WINDOW) & (w_pos[None, :] >= 0)
    s_w = jnp.einsum('bqhgd,bkhd->bhgqk', q_rot, kv_w[:, :, 0]).astype(F32) * scale
    o_w = jnp.einsum('bhgqk,bkhd->bqhgd', masked_softmax(s_w, m_w), kv_w[:, :, 1].astype(F32))
    o = gates[..., 0:1] * o_c + gates[..., 1:2] * o_s + gates[..., 2:3] * o_w
    return o.reshape(B, Tq, Q_WIDTH).astype(q.dtype)

def nsa_prompt(q, q_rot, kv_c, kv_s, kv_w, gates, p):
    B, T = q.shape[:2]
    kc = compress(kv_c[:, :, 0], p['cmp_pos_k'], p['w_cmp_k1'], p['w_cmp_k2'])
    vc = compress(kv_c[:, :, 1], p['cmp_pos_v'], p['w_cmp_v1'], p['w_cmp_v2'])
    c_end = jnp.arange(kc.shape[1], dtype=jnp.int32) * CMP_STRIDE + (CMP_BLOCK - 1)
    n_sel_blocks = T // SEL_BLOCK
    kv_blocks = kv_s.reshape(B, n_sel_blocks, SEL_BLOCK, 2, N_KV_HEADS, HEAD_DIM)
    bb = jnp.arange(B)[:, None, None, None]
    hh = jnp.arange(N_KV_HEADS)[None, None, :, None]

    def fetch(idx):
        return kv_blocks[bb, idx, :, :, hh, :]

    kv_w_pad = jnp.pad(kv_w, ((0, 0), (WINDOW, 0), (0, 0), (0, 0), (0, 0)))

    def one_block(i):
        s0 = i * Q_BLOCK
        take = lambda a: lax.dynamic_slice_in_dim(a, s0, Q_BLOCK, axis=1)
        q_pos = s0 + jnp.arange(Q_BLOCK, dtype=jnp.int32)
        w_rows = lax.dynamic_slice_in_dim(kv_w_pad, s0, WINDOW + Q_BLOCK, axis=1)
        w_pos = s0 - WINDOW + jnp.arange(WINDOW + Q_BLOCK, dtype=jnp.int32)
        return nsa_core(take(q), take(q_rot), q_pos, kc, vc, c_end, fetch, n_sel_blocks,
                        w_rows, w_pos, take(gates))

    o = lax.map(one_block, jnp.arange(T // Q_BLOCK, dtype=jnp.int32))
    return o.transpose(1, 0, 2, 3).reshape(B, T, Q_WIDTH)

def nsa_sample(q, q_rot, kv_c, kv_s, kv_w, gates, pool_c, pool_s, win_buf, page_table, p):
    Bd, S = q.shape[:2]
    q_pos = PAST_LEN + jnp.arange(S, dtype=jnp.int32)
    past_c = pool_c[page_table].reshape(Bd, PAST_LEN, 2, N_KV_HEADS, HEAD_DIM)
    rows_c = jnp.concatenate([past_c, kv_c.astype(past_c.dtype)], axis=1)
    kc = compress(rows_c[:, :, 0], p['cmp_pos_k'], p['w_cmp_k1'], p['w_cmp_k2'])
    vc = compress(rows_c[:, :, 1], p['cmp_pos_v'], p['w_cmp_v1'], p['w_cmp_v2'])
    c_end = jnp.arange(kc.shape[1], dtype=jnp.int32) * CMP_STRIDE + (CMP_BLOCK - 1)
    ns_past = PAST_LEN // SEL_BLOCK
    ns_new = -(-S // SEL_BLOCK)
    per_page = PAGE_SIZE // SEL_BLOCK
    pool_blocks = pool_s.reshape(pool_s.shape[0], per_page, SEL_BLOCK, 2, N_KV_HEADS, HEAD_DIM)
    tail = jnp.pad(kv_s, ((0, 0), (0, ns_new * SEL_BLOCK - S), (0, 0), (0, 0), (0, 0)))
    tail = tail.reshape(Bd, ns_new, SEL_BLOCK, 2, N_KV_HEADS, HEAD_DIM)
    bb = jnp.arange(Bd)[:, None, None, None]
    hh = jnp.arange(N_KV_HEADS)[None, None, :, None]

    def fetch(idx):
        jp = jnp.minimum(idx, ns_past - 1)
        page = page_table[bb, jp // per_page]
        past = pool_blocks[page, jp % per_page, :, :, hh, :]
        new = tail[bb, jnp.clip(idx - ns_past, 0, ns_new - 1), :, :, hh, :]
        return jnp.where((idx < ns_past)[..., None, None, None], past, new.astype(past.dtype))

    rows_w = jnp.concatenate([win_buf, kv_w.astype(win_buf.dtype)], axis=1)
    n_buf = win_buf.shape[1]
    w_pos = PAST_LEN - n_buf + jnp.arange(n_buf + S, dtype=jnp.int32)
    o = nsa_core(q, q_rot, q_pos, kc, vc, c_end, fetch, ns_past + ns_new, rows_w, w_pos, gates)
    return o, rows_w[:, S:]

def rglru_branch(u, u_gate, conv_buf, h0, p):
    B, T, _ = u.shape
    up = jnp.concatenate([conv_buf.astype(u.dtype), u], axis=1)
    xc = p['conv_b'] + sum(up[:, k:k + T] * p['conv_w'][k] for k in range(CONV_W))
    xb = xc.reshape(B, T, RNN_BLOCKS, RNN_BW)
    r = jax.nn.sigmoid((jnp.einsum('btnc,ncd->btnd', xb, p['w_rg_a']).reshape(B, T, D_RNN) + p['b_rg_a']).astype(F32))
    i = jax.nn.sigmoid((jnp.einsum('btnc,ncd->btnd', xb, p['w_rg_i']).reshape(B, T, D_RNN) + p['b_rg_i']).astype(F32))
    log_a = -RG_C * r * jax.nn.softplus(-p['lru_lambda'].astype(F32))
    a = jnp.exp(log_a)
    b = jnp.sqrt(-jnp.expm1(2.0 * log_a)) * (i * xc.astype(F32))

    def step(h, ab):
        h = ab[0] * h + ab[1]
        return h, h

    h_last, hs = lax.scan(step, h0.astype(F32), (a.transpose(1, 0, 2), b.transpose(1, 0, 2)))
    y = hs.transpose(1, 0, 2) * jax.nn.gelu(u_gate.astype(F32))
    return y.astype(u.dtype), up[:, -(CONV_W - 1):], h_last

def swiglu(x, wg, wu, wd):
    return (jax.nn.silu(x @ wg) * (x @ wu)) @ wd

def moe(x, p):
    N, D = x.shape
    scores = jax.nn.sigmoid(jnp.einsum('nd,de->ne', x, p['w_router']).astype(F32))
    _, e_idx = lax.top_k(scores + p['router_bias'].astype(F32), TOP_K)
    w = jnp.take_along_axis(scores, e_idx, axis=1)
    w = w / jnp.sum(w, axis=-1, keepdims=True) * ROUTED_SCALE
    nk = N * TOP_K
    e_flat = e_idx.reshape(nk)
    order = jnp.argsort(e_flat)
    e_sorted = e_flat[order]
    tok_sorted = (order // TOP_K).astype(jnp.int32)
    w_sorted = w.reshape(nk)[order]
    blk = MOE_BLOCK if nk >= MOE_BLOCK * N_EXPERTS else 8
    counts = jnp.bincount(e_flat, length=N_EXPERTS)
    padded = (counts + blk - 1) // blk * blk
    end_pad = jnp.cumsum(padded)
    start_pad = end_pad - padded
    start = jnp.cumsum(counts) - counts
    dest = start_pad[e_sorted] + jnp.arange(nk) - start[e_sorted]
    n_blocks = -(-nk // blk) + N_EXPERTS
    rows = n_blocks * blk
    row_tok = jnp.full((rows,), N, jnp.int32).at[dest].set(tok_sorted)
    row_w = jnp.zeros((rows,), F32).at[dest].set(w_sorted)
    blk_expert = jnp.minimum(jnp.searchsorted(end_pad, jnp.arange(n_blocks) * blk, side='right'), N_EXPERTS - 1)
    x_rows = jnp.concatenate([x, jnp.zeros((1, D), x.dtype)], axis=0)[row_tok].reshape(n_blocks, blk, D)

    def expert_block(args):
        xb, e = args
        return swiglu(xb, p['w_exp_gate'][e], p['w_exp_up'][e], p['w_exp_down'][e])

    y_rows = lax.map(expert_block, (x_rows, blk_expert)).reshape(rows, D)
    routed = jax.ops.segment_sum(y_rows.astype(F32) * row_w[:, None], row_tok, num_segments=N + 1)[:N]
    shared = swiglu(x, p['w_sh_gate'], p['w_sh_up'], p['w_sh_down']).astype(F32)
    return (routed + shared).astype(x.dtype)

def block_tail(x, o_attn, y_rnn, g_a, g_b, p):
    merged = (jax.nn.sigmoid(g_a.astype(F32)) * (o_attn @ p['w_branch_attn'])
              + jax.nn.sigmoid(g_b.astype(F32)) * (y_rnn @ p['w_branch_rnn']))
    mix = merged.astype(x.dtype) @ p['w_out']
    x = layer_norm(DN_ALPHA * x + mix, p['ln1_g'], p['ln1_b'])
    B, T, D = x.shape
    ffn = moe(x.reshape(B * T, D), p).reshape(B, T, D)
    return layer_norm(DN_ALPHA * x + ffn, p['ln2_g'], p['ln2_b'])

def setup_inputs(seed: int = 0) -> dict:
    key = jax.random.key(seed)
    keys = jax.random.split(key, 40)
    cnt = iter(range(40))
    nrm = lambda shape, s: jax.random.normal(keys[next(cnt)], shape, F32) * s
    L = DEPTH
    n_pages = PAST_LEN // PAGE_SIZE
    n_pool = (5 * DEC_BATCH * n_pages + 3) // 4
    w_buf = min(WINDOW, PAST_LEN)
    a0 = jax.random.uniform(keys[next(cnt)], (L, D_RNN), F32, 0.9, 0.999) ** (1.0 / RG_C)
    perm = jax.random.permutation(keys[next(cnt)], n_pool)[:DEC_BATCH * n_pages]
    return {
        'x_prompt': nrm((BATCH, SEQ, D_MODEL), 1.0),
        'x_sample': nrm((DEC_BATCH, DEC_SEQ, D_MODEL), 1.0),
        'cache_cmp_kv': nrm((L, n_pool, PAGE_SIZE, 2, N_KV_HEADS, HEAD_DIM), 1.0),
        'cache_sel_kv': nrm((L, n_pool, PAGE_SIZE, 2, N_KV_HEADS, HEAD_DIM), 1.0),
        'cache_win_kv': nrm((L, DEC_BATCH, w_buf, 2, N_KV_HEADS, HEAD_DIM), 1.0),
        'state_conv': nrm((L, DEC_BATCH, CONV_W - 1, D_RNN), 1.0),
        'state_rnn': nrm((L, DEC_BATCH, D_RNN), 0.5),
        'page_table': perm.reshape(DEC_BATCH, n_pages).astype(jnp.int32),
        'w_in': nrm((L, D_MODEL, N_IN), D_MODEL ** -0.5),
        'conv_w': nrm((L, CONV_W, D_RNN), CONV_W ** -0.5),
        'conv_b': nrm((L, D_RNN), 0.01),
        'w_rg_a': nrm((L, RNN_BLOCKS, RNN_BW, RNN_BW), RNN_BW ** -0.5),
        'b_rg_a': nrm((L, D_RNN), 0.01),
        'w_rg_i': nrm((L, RNN_BLOCKS, RNN_BW, RNN_BW), RNN_BW ** -0.5),
        'b_rg_i': nrm((L, D_RNN), 0.01),
        'lru_lambda': jnp.log(a0) - jnp.log1p(-a0),
        'cmp_pos_k': nrm((L, CMP_BLOCK, HEAD_DIM), 0.1),
        'cmp_pos_v': nrm((L, CMP_BLOCK, HEAD_DIM), 0.1),
        'w_cmp_k1': nrm((L, CMP_BLOCK, HEAD_DIM, CMP_HIDDEN), (CMP_BLOCK * HEAD_DIM) ** -0.5),
        'w_cmp_k2': nrm((L, CMP_HIDDEN, HEAD_DIM), CMP_HIDDEN ** -0.5),
        'w_cmp_v1': nrm((L, CMP_BLOCK, HEAD_DIM, CMP_HIDDEN), (CMP_BLOCK * HEAD_DIM) ** -0.5),
        'w_cmp_v2': nrm((L, CMP_HIDDEN, HEAD_DIM), CMP_HIDDEN ** -0.5),
        'w_branch_attn': nrm((L, Q_WIDTH, D_MODEL), Q_WIDTH ** -0.5),
        'w_branch_rnn': nrm((L, D_RNN, D_MODEL), D_RNN ** -0.5),
        'w_out': nrm((L, D_MODEL, D_MODEL), DN_BETA * D_MODEL ** -0.5),
        'ln1_g': 1.0 + nrm((L, D_MODEL), 0.02),
        'ln1_b': nrm((L, D_MODEL), 0.02),
        'w_router': nrm((L, D_MODEL, N_EXPERTS), D_MODEL ** -0.5),
        'router_bias': nrm((L, N_EXPERTS), 0.01),
        'w_exp_gate': nrm((L, N_EXPERTS, D_MODEL, D_EXPERT), D_MODEL ** -0.5),
        'w_exp_up': nrm((L, N_EXPERTS, D_MODEL, D_EXPERT), D_MODEL ** -0.5),
        'w_exp_down': nrm((L, N_EXPERTS, D_EXPERT, D_MODEL), DN_BETA * D_EXPERT ** -0.5),
        'w_sh_gate': nrm((L, D_MODEL, D_SHARED), D_MODEL ** -0.5),
        'w_sh_up': nrm((L, D_MODEL, D_SHARED), D_MODEL ** -0.5),
        'w_sh_down': nrm((L, D_SHARED, D_MODEL), DN_BETA * D_SHARED ** -0.5),
        'ln2_g': 1.0 + nrm((L, D_MODEL), 0.02),
        'ln2_b': nrm((L, D_MODEL), 0.02),
    }

def reference(x_prompt, x_sample, cache_cmp_kv, cache_sel_kv, cache_win_kv, state_conv, state_rnn,
              page_table, w_in, conv_w, conv_b, w_rg_a, b_rg_a, w_rg_i, b_rg_i, lru_lambda,
              cmp_pos_k, cmp_pos_v, w_cmp_k1, w_cmp_k2, w_cmp_v1, w_cmp_v2, w_branch_attn,
              w_branch_rnn, w_out, ln1_g, ln1_b, w_router, router_bias, w_exp_gate, w_exp_up,
              w_exp_down, w_sh_gate, w_sh_up, w_sh_down, ln2_g, ln2_b):
    B, T, _ = x_prompt.shape
    Bd, S, _ = x_sample.shape
    pos_p = jnp.arange(T, dtype=jnp.int32)
    pos_s = PAST_LEN + jnp.arange(S, dtype=jnp.int32)
    xp, xs = x_prompt, x_sample
    cmp_p, cmp_s, sel_p, sel_s, win_p, win_s = [], [], [], [], [], []
    conv_p, conv_s, rnn_p, rnn_s = [], [], [], []
    for l in range(DEPTH):
        p = dict(w_in=w_in[l], conv_w=conv_w[l], conv_b=conv_b[l], w_rg_a=w_rg_a[l], b_rg_a=b_rg_a[l],
                 w_rg_i=w_rg_i[l], b_rg_i=b_rg_i[l], lru_lambda=lru_lambda[l], cmp_pos_k=cmp_pos_k[l],
                 cmp_pos_v=cmp_pos_v[l], w_cmp_k1=w_cmp_k1[l], w_cmp_k2=w_cmp_k2[l], w_cmp_v1=w_cmp_v1[l],
                 w_cmp_v2=w_cmp_v2[l], w_branch_attn=w_branch_attn[l], w_branch_rnn=w_branch_rnn[l],
                 w_out=w_out[l], ln1_g=ln1_g[l], ln1_b=ln1_b[l], w_router=w_router[l],
                 router_bias=router_bias[l], w_exp_gate=w_exp_gate[l], w_exp_up=w_exp_up[l],
                 w_exp_down=w_exp_down[l], w_sh_gate=w_sh_gate[l], w_sh_up=w_sh_up[l],
                 w_sh_down=w_sh_down[l], ln2_g=ln2_g[l], ln2_b=ln2_b[l])
        q, q_rot, kv_c, kv_s, kv_w, gates, u_rnn, u_gate, g_a, g_b = mixer_inputs(xp, pos_p, p['w_in'])
        o_attn = nsa_prompt(q, q_rot, kv_c, kv_s, kv_w, gates, p)
        y_rnn, conv_new, h_new = rglru_branch(u_rnn, u_gate, jnp.zeros((B, CONV_W - 1, D_RNN), xp.dtype),
                                              jnp.zeros((B, D_RNN), F32), p)
        xp = block_tail(xp, o_attn, y_rnn, g_a, g_b, p)
        cmp_p.append(kv_c)
        sel_p.append(kv_s)
        win_p.append(kv_w[:, -min(WINDOW, T):])
        conv_p.append(conv_new)
        rnn_p.append(h_new)
        q, q_rot, kv_c, kv_s, kv_w, gates, u_rnn, u_gate, g_a, g_b = mixer_inputs(xs, pos_s, p['w_in'])
        o_attn, win_new = nsa_sample(q, q_rot, kv_c, kv_s, kv_w, gates, cache_cmp_kv[l], cache_sel_kv[l],
                                     cache_win_kv[l], page_table, p)
        y_rnn, conv_new, h_new = rglru_branch(u_rnn, u_gate, state_conv[l], state_rnn[l], p)
        xs = block_tail(xs, o_attn, y_rnn, g_a, g_b, p)
        cmp_s.append(kv_c)
        sel_s.append(kv_s)
        win_s.append(win_new)
        conv_s.append(conv_new)
        rnn_s.append(h_new)
    return (xp, xs, jnp.stack(cmp_p), jnp.stack(cmp_s), jnp.stack(sel_p), jnp.stack(sel_s),
            jnp.stack(win_p), jnp.stack(win_s), jnp.stack(conv_p), jnp.stack(conv_s),
            jnp.stack(rnn_p), jnp.stack(rnn_s))


_drawn_inputs = setup_inputs


def setup_inputs(seed=0):
    import zlib

    import numpy as np

    out = dict(_drawn_inputs(seed))
    spreads = {}
    factors = {'cache_cmp_kv': 5.141,
     'b_rg_a': 23.413,
     'b_rg_i': 8.0,
     'cmp_pos_k': 7.64,
     'ln2_g': 8.69,
     'ln2_b': 7.922}
    for name, (base, spread) in spreads.items():
        noise = np.random.default_rng([zlib.crc32(name.encode()), seed]).standard_normal(out[name].shape)
        drawn = base * np.exp(spread * noise) if base else spread * noise
        out[name] = __import__('jax').numpy.asarray(drawn.astype(out[name].dtype))
    for name, factor in factors.items():
        out[name] = (out[name] * factor).astype(out[name].dtype)
    return out
```

```python
from contextlib import ExitStack

import numpy as np

import concourse.bass as bass
from concourse import mybir

F32 = mybir.dt.float32
I32 = mybir.dt.int32
U32 = mybir.dt.uint32
ALU = mybir.AluOpType
ACT = mybir.ActivationFunctionType
AX = mybir.AxisListType.X

P = 128
D = 1024
KT = D // P
SEQ = 1024
BD = 8
NTOK = SEQ + BD
NT = SEQ // P + 1
PAST = 2048
PAGE = 128
NPG = PAST // PAGE
NPOOL = 160
HD = 64
NH = 8
KV = 2 * 2 * HD
QW = NH * HD
TOKW = QW + 3 * KV + 3 * NH
C_U = TOKW
C_G = C_U + D
C_A = C_G + D
C_B = C_A + D
CH = NTOK // 3
WINDOW = 512
NE = 64
TOPK = 6
DE = 256
USED = NTOK * TOPK // P
NBLK = 112
SCALE = HD ** -0.5
ALPHA = 2.0 ** 0.25
EPS = 1e-5
NEG = -1e30
ROUTED_SCALE = 2.5


def constants():
    p = np.arange(P, dtype=np.float64)[:, None]
    c = np.arange(P, dtype=np.float64)[None, :]
    parts = {}
    parts["ident"] = (p == c) * 1.0
    parts["diag"] = np.where(c <= p, 0.0, NEG)
    parts["edge"] = np.where(c >= p, 0.0, NEG)
    end = 16.0 * np.arange(63)[None, None, :] + 31
    parts["cmpm"] = np.where(end <= p[:, :, None] + 128.0 * np.arange(8)[None, :, None], 0.0, NEG).reshape(P, 504)
    inv = np.float32(500000.0) ** (-(np.arange(8, dtype=np.float32) * np.float32(2.0 / 16)))
    pos = np.full((P, NT), float(PAST), np.float32)
    pos[:, :8] = (np.arange(8)[None, :] * P + np.arange(P)[:, None])
    ang = pos[:, :, None] * inv.astype(np.float32)[None, None, :]
    parts["cos"] = np.cos(ang.astype(np.float32)).reshape(P, NT * 8)
    parts["sin"] = np.sin(ang.astype(np.float32)).reshape(P, NT * 8)
    parts["before"] = (p < c) * 1.0
    parts["ones"] = np.ones((P, P))
    parts["group"] = ((p // 4) == (np.arange(64)[None, :] // 4)) * 1.0
    parts["own"] = ((p // 8) == np.arange(8)[None, :]) * 1.0
    s = np.arange(33)
    parts["lower"] = np.broadcast_to((s[None, :] < s[:, None]).reshape(1, 33 * 33), (P, 33 * 33)) * 1.0
    parts["force"] = np.broadcast_to(np.where((s == 0) | (s >= 31), 1e6, 0.0)[None, :], (P, 33))
    parts["free"] = np.broadcast_to(np.where((s == 0) | (s >= 31), 0.0, 1.0)[None, :], (P, 33))
    parts["tokid"] = p + 128.0 * np.arange(NT)[None, :]
    parts["exp"] = np.broadcast_to(np.arange(64.0)[None, :], (P, 64))
    parts["row"] = p
    where, at = {}, 0
    for k, v in parts.items():
        where[k] = (at, v.shape[1])
        at += v.shape[1]
    return np.ascontiguousarray(np.concatenate([np.asarray(v, np.float32) for v in parts.values()], 1)), where


CONSTS, CWHERE = constants()
NCONST = CONSTS.shape[1]


class Engine:

    def __init__(self, eng, chain, met, others):
        self.eng, self.chain, self.met, self.others = eng, chain, met, others
        self.count, self.last, self.meets = {}, None, 0

    def do(self, ins, sem=None):
        sem = self.chain if sem is None else sem
        ins.then_inc(sem, 1)
        self.count[sem.name] = self.count.get(sem.name, 0) + 1
        self.last = (sem, self.count[sem.name])

    def settle(self):
        if self.last:
            self.eng.wait_ge(*self.last)

    def step(self, ins, sem=None):
        self.do(ins, sem)
        self.settle()

    def meet(self):
        self.settle()
        self.eng.nop().then_inc(self.met, 1)
        self.meets += 1
        for o in self.others:
            self.eng.wait_ge(o, self.meets)


def attention_plan():
    units, n, nv, heads = [], 0, 0, []
    for i in range(8):
        for j in range(4):
            for g in range(2):
                for kind in "sw":
                    if kind == "s":
                        t0 = 0
                        groups = [[("s", t, t * P) for t in range(a, min(a + 4, i + 1))] for a in range(0, i + 1, 4)]
                    else:
                        t0 = max(0, i - 4)
                        tiles = [("w", t, (t - t0) * P) for t in range(t0, i + 1)] + [("c", 0, 640)]
                        groups = [tiles[a:a + 4] for a in range(0, len(tiles), 4)]
                    units.append(dict(i=i, j=j, g=g, kind=kind, t0=t0, groups=groups, first=n, vfirst=nv))
                    n += len(groups)
                    nv += len(groups)
                    if len(units) > 16 and len(units) % 16 == 4:
                        heads.append(n)
                        n += 1
    return units, heads + [n]


UNITS, HEADS = attention_plan()


def build(nc, a, o, x1_dram, tab_dram, y_dram):
    ctx = ExitStack()
    with ctx:
        arena = ctx.enter_context(nc.sbuf_tensor("arena", [P, 52400], F32))
        PS = ctx.enter_context(nc.psum_tensor("PS", [P, 8, 512], F32))
        names = {}

        def sem(name):
            if name not in names:
                names[name] = ctx.enter_context(nc.semaphore(name))
            return names[name]

        def isb(name, shape, dt=I32):
            return ctx.enter_context(nc.sbuf_tensor(name, shape, dt))

        def at(off, *shape):
            n = int(np.prod(shape))
            assert off + n <= 52400, (off, shape)
            v = arena[:, off:off + n]
            if len(shape) == 2:
                v = v.rearrange("p (a b) -> p a b", a=shape[0])
            elif len(shape) == 3:
                v = v.rearrange("p (a b c) -> p a b c", a=shape[0], b=shape[1])
            return v

        def const(name, n=P):
            w, k = CWHERE[name]
            return arena[0:n, w:w + k]
        assert NCONST <= 3500
        ident = arena[:, 0:P]
        gate = at(3500, NT, 24)
        negb = at(3720, 2, 2)
        sums = at(3724, 2, 3)
        coef = at(3730, 3)
        mx = at(3734, 4)
        posT = at(3740, 2, 32)
        cbias = at(3804, 2)
        small = at(3810, 100)
        wfin = at(3910, NT, TOPK)
        xT = at(4000, KT, NTOK)
        AT = at(12256, 4, NTOK)
        W1 = at(16384, 2, 32, P)
        W2 = at(24576, 2, P)
        wtm = at(12256, KT, TOKW)
        assert 12256 + KT * TOKW <= 24576
        kvT = at(24832, 4, NTOK)
        kvraw = at(28960, NT, 3 * KV)
        qT = at(35872, 4, NTOK)
        qrT = at(40000, 4, NTOK)
        TMP = 44128

        def kvtok(t):
            return kvraw[:, (t + 1) % NT, :]

        xin = at(TMP, 3, D)
        qtok = at(TMP + 3072, 2, QW)
        qrtok = at(TMP + 4096, 2, QW)
        rt = at(TMP + 5120, 4, 64)
        Pb = at(TMP, 2, D)
        PTs = at(TMP + 2048, 2, 512)
        atok = at(TMP + 3072, 2, QW)
        gh = at(TMP + 4096, 2, 127)
        kcp = at(TMP + 4352, 63)
        vcp = at(TMP + 4416, P)
        zrow = at(TMP + 4832, D)
        possb = at(TMP + 4544, 4 * HD)
        DB = 28960 + 768
        wKV = at(DB, BD, 4, KV)
        cpg = at(DB, 2, NPG, KV)
        spg = at(DB, 2, NPG, 2 * HD)
        kvTb = at(DB + 8192, 2, PAST)
        kcs = at(DB + 12288, BD, 127)
        vcs = at(DB + 13304, BD, P)
        SS = at(DB + 14328, 2052)
        PTb = at(DB + 16380, NPG, 64)
        pself = at(DB + 17404, 3, 64)
        rank = at(DB + 17596, 2, 33 * 33)
        ghs = at(DB + 19774, 2, 127)
        sm = at(DB + 20028, 8, 36)
        gsel = at(DB + 20316, 4)
        selmask = at(DB + 20320, 33)
        zc = at(DB + 20360, 132)
        qz = at(51000, 2, BD, 64)
        Pc = at(52024, 127)
        assert DB + 20492 <= 51000
        ring = at(16384, 6, KT, P)
        EB = 16384 + 6144
        RT = at(EB, KT, NTOK)
        mT = at(EB + 8256, KT, NTOK)
        E0 = EB + 8256
        ucb = at(E0, 1028)
        ucs = at(E0 + 1028, BD, 4)
        xc = at(E0 + 1060, NTOK)
        gg = at(E0 + 2092, 2, NTOK)
        rr, aa, th, ii, vv, hs = (at(E0 + 4156 + k * NTOK, NTOK) for k in range(6))
        vec = at(E0 + 10348, KT, 40)
        vrows = at(E0 + 10668, D)
        orows = at(E0 + 11692, D)
        wra = at(E0 + 12716, KT, P)
        wri = at(E0 + 13740, KT, P)
        stg = at(E0 + 14764, 20)
        lam = at(E0 + 14784, 8, KT)
        assert E0 + 14848 <= 52400
        sg = at(E0 + 8256, 2, NTOK)
        m1 = at(E0 + 8256 + 2064, NTOK)
        wout = at(4000, KT, D)
        xr = at(12192, 2, D)
        yy = at(14240, 2, D)
        lnw = at(16288, 4, D)
        st = at(20384, 2, 16)
        x1tok = at(39042, NT, D)
        x1T = at(20500, KT, NTOK)
        assert E0 == 30784 and E0 + 8256 <= 39042 and 20500 + 8256 <= E0
        wrt = at(4000, KT, NE)
        wsg = at(4512, KT, DE)
        wsu = at(6560, KT, DE)
        wsd = at(8608, 2, D)
        shT = at(10656, 2, NTOK)
        sil = at(12720, NTOK)
        HB = 30784
        sc = at(HB, NT, NE)
        Mm = at(HB + 576, NT, NE)
        idxf = at(HB + 1152, NT, 8)
        oh = at(HB + 1224, TOPK, NE)
        sel8 = at(HB + 1608, 8)
        rb = at(HB + 1616, NE)
        selv = at(HB + 1680, NE)
        dstf = at(HB + 1744, NT, TOPK)
        cs = at(HB + 1800, NE)
        nbl = at(HB + 1864, NE)
        base = at(HB + 1928, NE)
        pos = at(HB + 1992, NE)
        tmp6 = at(HB + 2056, TOPK, NE)
        trow = at(HB + 2440, P)
        trowT = at(HB + 2568, P)
        wk = at(HB + 2700, 8)
        ridx = at(HB + 2720, NE)
        wexg = at(16288 + 4096 + 100, 2, KT, DE)
        wexu = at(24580, 2, KT, DE)
        wexd = at(28676, 2, 2, D)
        xg = at(4000, 2, D)
        xgT = at(6048, 2, KT, P)
        hsl = at(8096, 2, DE)
        hh_ = at(8608, 2, DE)
        hT = at(9120, 2, 2, P)
        ysb = at(9632, 2, D)
        assert 28676 + 4096 <= 39042
        yg = at(20484, 6, D)
        fin = at(4000, 2, D)

        ptab = isb("ptab", [1, P])
        i8 = isb("i8", [P, 8], U32)
        dsti = isb("dsti", [P, NT, TOPK])
        tokid = isb("tokid", [P, NT])
        ztab = isb("ztab", [NBLK, P])
        idxall = isb("idxall", [P, P])
        idxs = isb("idxs", [P, 2])
        izero = isb("izero", [P, 1])
        pause = isb("pause", [P, 2])
        blke = isb("blke", [1, P])
        nblk = isb("nblk", [1, 4])

        met = [sem("pe_met"), sem("act_met"), sem("dve_met")]

        s_const = sem("const_in")
        s_xin = [sem(f"xin{k}") for k in range(3)]
        s_wtm = sem("wtm_in")
        x_turned = sem("x_turned")
        xT_ready = sem("xT_ready")
        tok_mm = sem("tok_mm")
        tok_ev = sem("tok_ev")
        rope_done = sem("rope_done")
        tok_turned = sem("tok_turned")
        tokT_ready = sem("tokT_ready")
        out_done = sem("out_done")
        w1_zero = sem("w1_zero")
        s_w1 = sem("w1_in")
        cmp_mm = sem("cmp_mm")
        cmp_ev = sem("cmp_ev")
        qk_done = sem("qk_done")
        mx_done = sem("mx_done")
        exp_done = sem("exp_done")
        pt_done = sem("pt_done")
        pt_ev = sem("pt_ev")
        pv_done = sem("pv_done")
        o_ev = sem("o_ev")
        for name in ("gu_mm", "gu_free", "wex", "wexd", "xg", "xgT_mm", "xgT_ev", "yd", "ix", "pg"):
            sem(name + "0"), sem(name + "1")
        for name in ("y_zero", "y_mm", "y_ev", "y_ev2", "hT_mm", "hT_ev", "sl_done"):
            sem(name)

        block = ctx.enter_context(nc.Block())
        G_CMP = BD + 2
        G_SEL = G_CMP + 8 * BD + 1
        GP = [slice(0, 64), slice(64, 128)]

        def rows_of(t):
            return P if t < NT - 1 else BD

        stream = []
        for n in range(KT):
            stream += [("in", C_U + n * P), ("in", C_G + n * P)]
        for n in range(KT):
            stream += [("in", C_A + n * P), ("wa", n * P), ("in", C_B + n * P), ("wb", n * P)]
        RING = 6
        due, filled = [], [0] * RING
        for b, (kind, _) in enumerate(stream):
            filled[b % RING] += 32 if kind == "wa" else 16
            due.append(filled[b % RING])
        s_ring = [sem(f"ring{k}") for k in range(RING)]
        w_used = sem("w_used")

        @block.sync
        def _(sp):
            sp.dma_start(arena[:, 0:NCONST], a["consts"]).then_inc(s_const, 16)
            sp.dma_start(ptab[:, :], a["page_table"].rearrange("(u b) c -> u (b c)", u=1)).then_inc(s_const, 16)
            for t in range(NT):
                n = rows_of(t)
                if t >= 3:
                    sp.wait_ge(x_turned, 2 * (t - 2))
                src = a["x_prompt"][t * P:(t + 1) * P, :] if n == P else a["x_sample"]
                sp.dma_start(xin[0:n, t % 3, :], src).then_inc(s_xin[t % 3], 16)
                if t == 2:
                    for k in range(KT):
                        sp.dma_start(wtm[:, k, :], a["w_in"][k * P:(k + 1) * P, 0:TOKW]).then_inc(s_wtm, 16)
            sp.dma_start(o["win_s"][:, 0:WINDOW - 1, :], a["win"][:, 1:WINDOW, :]).then_inc(out_done, 16)
            sp.dma_start(o["conv_s"][:, 0:2, :], a["state_conv"][:, 1:3, :]).then_inc(out_done, 16)
            sp.wait_ge(rope_done, NT)
            sp.dma_start(o["cmp_p"].rearrange("(t p) c -> p t c", p=P), kvraw[:, 1:9, 0:KV]).then_inc(out_done, 16)
            sp.dma_start(o["sel_p"].rearrange("(t p) c -> p t c", p=P), kvraw[:, 1:9, KV:2 * KV]).then_inc(out_done, 16)
            sp.dma_start(o["win_p"].rearrange("(t p) c -> p t c", p=P), kvraw[:, 5:9, 2 * KV:3 * KV]).then_inc(out_done, 16)
            sp.dma_start(o["cmp_s"], kvraw[0:BD, 0, 0:KV]).then_inc(out_done, 16)
            sp.dma_start(o["sel_s"], kvraw[0:BD, 0, KV:2 * KV]).then_inc(out_done, 16)
            sp.dma_start(o["win_s"][:, WINDOW - 1, :], kvraw[0:BD, 0, 2 * KV:3 * KV]).then_inc(out_done, 16)
            for m in met:
                sp.wait_ge(m, 1)
            sp.wait_ge(w1_zero, 1)
            for kv in range(2):
                for g in range(2):
                    sp.dma_start(W1[GP[g], kv, :, g * 64:g * 64 + 64],
                                 a["w1k" if kv == 0 else "w1v"].rearrange("s d f -> d s f")).then_inc(s_w1, 16)
                    sp.dma_start(W2[GP[g], kv, g * 64:g * 64 + 64], a["w2k" if kv == 0 else "w2v"]).then_inc(s_w1, 16)
            sp.dma_start(y_dram[USED:NBLK, :, :].rearrange("b p d -> p b d"),
                         zrow.unsqueeze(1).broadcast_to([P, NBLK - USED, D])).then_inc(sem("y_zero"), 16)
            for k in range(4):
                sp.dma_start(possb[0:32, k * HD:(k + 1) * HD], a["posk" if k < 2 else "posv"]).then_inc(s_w1, 16)

            for m in met:
                sp.wait_ge(m, 3)
            sp.wait_ge(out_done, 8 * 16)
            sp.wait_ge(sem("y_zero"), 16)
            for b in range(BD):
                sp.dma_start(wKV[:, b, :, :], a["win"][b].rearrange("(t p) c -> p t c", p=P)).then_inc(sem("win_in"), 16)

            def pages(pool, dst, half, free, free0, per):
                for b in range(BD):
                    if b >= 2:
                        sp.wait_ge(free, free0 + per * (b - 1))
                    with sp.Fori(0, NPG) as k:
                        pg = sp.value_load(ptab[0:1, bass.ds(k + b * NPG, 1)], min_val=0, max_val=NPOOL - 1)
                        src = pool[bass.ds(pg, 1), :, :] if half is None else pool[bass.ds(pg, 1), :, half * 2 * HD:(half + 1) * 2 * HD]
                        sp.dma_start(dst[:, b % 2, bass.ds(k, 1), :].rearrange("p a c -> p (a c)"),
                                     src.rearrange("a p c -> (a p) c")).then_inc(sem(f"pg{b % 2}"), 16)
            sp.wait_ge(sem("win_pv"), 1)
            pages(a["cmp"], cpg, None, sem("dt_done"), G_CMP, 8)
            sp.wait_ge(sem("dt_done"), G_CMP + 8 * BD)
            pages(a["sel"], spg, 0, sem("dt_done"), G_SEL, 4)
            sp.wait_ge(sem("dt_done"), G_SEL + 4 * BD)
            pages(a["sel"], spg, 1, sem("spv_used"), 0, 1)

            for m in met:
                sp.wait_ge(m, 4)
            sv = sem("vec_in")
            sp.dma_start(vrows[0:24, :], a["state_conv"].rearrange("b r c -> (b r) c")).then_inc(sv, 16)
            sp.dma_start(vrows[24:32, :], a["state_rnn"]).then_inc(sv, 16)
            sp.dma_start(vrows[32:36, :], a["conv_w"]).then_inc(sv, 16)
            for k, nm in enumerate(("conv_b", "b_rg_a", "b_rg_i", "lru_lambda")):
                sp.dma_start(vrows[36 + k:37 + k, :], a[nm]).then_inc(sv, 16)
            sp.dma_start(wra, a["w_rg_a"].rearrange("n c d -> c n d")).then_inc(sv, 16)
            sp.dma_start(wri, a["w_rg_i"].rearrange("n c d -> c n d")).then_inc(sv, 16)
            for b, (kind, c0) in enumerate(stream):
                if b >= RING:
                    sp.wait_ge(w_used, b - RING + 1)
                s = b % RING
                if kind == "wa":
                    for g in range(2):
                        sp.dma_start(ring[GP[g], s, 0:4, :],
                                     a["w_branch_attn"].rearrange("(g j d) n -> g d j n", g=2, j=4)[g, :, :, c0:c0 + P]).then_inc(s_ring[s], 16)
                else:
                    w = a["w_in"] if kind == "in" else a["w_branch_rnn"]
                    sp.dma_start(ring[:, s, :, :], w[:, c0:c0 + P].rearrange("(k p) n -> p k n", p=P)).then_inc(s_ring[s], 16)
                if b == 2 * KT:
                    sp.wait_ge(sem("rows_ready"), 1)
                    sp.dma_start(o["conv_p"], orows[0:3, :]).then_inc(out_done, 16)
                    sp.dma_start(o["conv_s"][:, 2, :], orows[3:11, :]).then_inc(out_done, 16)
                    sp.dma_start(o["rnn_p"], orows[11:12, :]).then_inc(out_done, 16)
                    sp.dma_start(o["rnn_s"], orows[12:20, :]).then_inc(out_done, 16)
                    sp.wait_ge(out_done, 12 * 16)
                    sp.sem_inc(sem("rows_out"), 1)

            for m in met:
                sp.wait_ge(m, 6)
            sp.dma_start(wout, a["w_out"].rearrange("(k p) n -> p k n", p=P)).then_inc(sem("wout_in"), 16)
            for k, nm in enumerate(("ln1_g", "ln1_b", "ln2_g", "ln2_b")):
                sp.dma_start(lnw[:, k, :], a[nm].broadcast_to([P, D])).then_inc(sem("ln_in"), 16)
            for t in range(NT):
                n = rows_of(t)
                if t >= 2:
                    sp.wait_ge(sem("xr_used"), t - 1)
                src = a["x_prompt"][t * P:(t + 1) * P, :] if n == P else a["x_sample"]
                sp.dma_start(xr[0:n, t % 2, :], src).then_inc(s_xin[t % 2], 16)
            sp.wait_ge(sem("x1_done"), NT)
            sp.dma_start(x1_dram[0:SEQ, :].rearrange("(t p) d -> p t d", p=P), x1tok[:, 0:8, :]).then_inc(sem("x1_out"), 16)
            sp.dma_start(x1_dram[SEQ:NTOK, :], x1tok[0:BD, 8, :]).then_inc(sem("x1_out"), 16)
            for m in met:
                sp.wait_ge(m, 7)
            sp.dma_start(wrt, a["w_router"].rearrange("(k p) n -> p k n", p=P)).then_inc(sem("wrt_in"), 16)
            sp.dma_start(rb, a["router_bias"].broadcast_to([P, NE])).then_inc(sem("wrt_in"), 16)
            sp.dma_start(wsg, a["w_sh_gate"].rearrange("(k p) n -> p k n", p=P)).then_inc(sem("wsh_in"), 16)
            sp.dma_start(wsu, a["w_sh_up"].rearrange("(k p) n -> p k n", p=P)).then_inc(sem("wsh_in"), 16)
            sp.dma_start(wsd, a["w_sh_down"].rearrange("(k p) n -> p k n", p=P)).then_inc(sem("wsh_in"), 16)
            sp.wait_ge(sem("ztab_set"), 1)
            sp.dma_start(tab_dram.rearrange("(b p) u -> b (p u)", p=P), ztab[:, :]).then_inc(sem("tab_zero"), 16)
            sp.wait_ge(sem("tab_full"), 16 * NT * TOPK)
            sp.dma_start(ztab[:, :], tab_dram.rearrange("(b p) u -> b (p u)", p=P)).then_inc(sem("tab_in"), 16)
            for m in met:
                sp.wait_ge(m, 8)
            turns = sp.value_load(nblk[0:1, 0:1], min_val=1, max_val=NBLK // 2)
            with sp.Fori(0, NBLK // 2) as i:
                with sp.If(i < turns):
                    for s in range(2):
                        e = sp.value_load(blke[0:1, bass.ds(i * 2 + s, 1)], min_val=0, max_val=NE - 1)
                        sp.wait_ge(sem(f"gu_mm{s}"), i + 1)
                        for w, name in ((wexg, "w_exp_gate"), (wexu, "w_exp_up")):
                            sp.dma_start(w[:, s, :, :].rearrange("p k n -> p (k n)"),
                                         a[name][bass.ds(e, 1), :, :].rearrange("u (p k) n -> (u p) (k n)", p=P)).then_inc(sem(f"wex{s}"), 16)
                        sp.wait_ge(sem("y_mm"), i * 2 + s + 1)
                        sp.dma_start(wexd[:, s, :, :].rearrange("p k n -> p (k n)"),
                                     a["w_exp_down"][bass.ds(e, 1), :, :].rearrange("u (p k) n -> (u p) (k n)", p=P)).then_inc(sem(f"wexd{s}"), 16)
            for t in range(NT):
                n = rows_of(t)
                sp.wait_ge(sem("fin_done"), t + 1)
                dst = o["y_p"][t * P:(t + 1) * P, :] if n == P else o["y_s"]
                sp.dma_start(dst, fin[0:n, t % 2, :]).then_inc(sem(f"y_out{t % 2}"), 16)
            sp.wait_ge(sem("y_out0"), 16 * 5)
            sp.wait_ge(sem("y_out1"), 16 * 4)
            sp.wait_ge(out_done, 12 * 16)

        @block.tensor
        def _(pe):
            E = Engine(pe, sem("pe_chain"), met[0], met[1:])
            mm = nc.tensor.matmul

            def turn(out, in_, n):
                return nc.tensor.transpose(out, in_, ident[0:n, 0:n])

            pe.wait_ge(s_const, 32)
            for t in range(NT):
                n = rows_of(t)
                pe.wait_ge(s_xin[t % 3], 16 * (t // 3 + 1))
                for hf in range(2):
                    gi = 2 * t + hf
                    if gi >= 4:
                        pe.wait_ge(xT_ready, gi - 3)
                    for k in range(4):
                        ins = turn(PS[:, gi % 4, k * P:k * P + n], xin[0:n, t % 3, (hf * 4 + k) * P:(hf * 4 + k + 1) * P], n)
                    E.do(ins, x_turned)
            pe.wait_ge(s_wtm, 16 * KT)
            pe.wait_ge(xT_ready, 2 * NT)
            COLS = [(0, 512), (512, 1024), (1024, TOKW)]

            def turn_tile(t):
                n = rows_of(t)
                pe.wait_ge(rope_done, t + 1)
                for g3 in range(3):
                    gi = 3 * t + g3
                    if gi >= 2:
                        pe.wait_ge(tokT_ready, gi - 1)
                    for k in range(4):
                        if g3 < 2:
                            src = (qtok, qrtok)[g3][0:n, t % 2, k * P:(k + 1) * P]
                        else:
                            c = (0, 128, 256, 512)[k]
                            src = kvtok(t)[0:n, c:c + P]
                        ins = turn(PS[:, 6 + gi % 2, k * P:k * P + n], src, n)
                    E.do(ins, tok_turned)

            for t in range(NT):
                n = rows_of(t)
                if t >= 2:
                    pe.wait_ge(tok_ev, t - 1)
                for c, (c0, c1) in enumerate(COLS):
                    for k in range(KT):
                        ins = mm(PS[0:n, 3 * (t % 2) + c, 0:c1 - c0], xT[:, k, t * P:t * P + n], wtm[:, k, c0:c1], start=k == 0, stop=k == KT - 1)
                E.do(ins, tok_mm)
                if t:
                    turn_tile(t - 1)
            turn_tile(NT - 1)
            E.meet()

            pe.wait_ge(s_w1, 12 * 16)

            def hidden(kv, src, ncols, bank, c0):
                for s in range(32):
                    ins = mm(PS[:, bank, c0:c0 + ncols], W1[:, kv, s, :], src[:, s:s + 16 * (ncols - 1) + 1:16], start=s == 0, stop=s == 31)
                return ins

            turn(PS[:, 7, 0:32], possb[0:32, 0:128], 32)
            E.do(turn(PS[:, 7, 32:64], possb[0:32, 128:256], 32), cmp_mm)
            pe.wait_ge(cmp_ev, 1)
            for kv in range(2):
                for s in range(32):
                    ins = mm(PS[:, 7, 64 + kv:65 + kv], W1[:, kv, s, :], posT[:, kv, s:s + 1], start=s == 0, stop=s == 31)
            E.do(ins, cmp_mm)
            for kv in range(2):
                ins = hidden(kv, kvT[:, kv, :], 63, 6, 256 * kv)
            E.do(ins, cmp_mm)
            pe.wait_ge(cmp_ev, 3)
            mm(PS[:, 5, 0:63], W2[:, 0, :], gh[:, 0, 0:63], start=True, stop=True)
            E.do(mm(PS[0:63, 5, 256:384], gh[:, 1, 0:63], W2[:, 1, :], start=True, stop=True), cmp_mm)
            E.meet()
            pe.wait_ge(cmp_ev, 4)

            def scores(k):
                u = UNITS[k]
                i, j, g = u["i"], u["j"], u["g"]
                if k >= 2:
                    pe.wait_ge(exp_done, k - 1)
                q = slice(i * P, (i + 1) * P)
                end = (i + 1) * P
                for c0 in range(u["t0"] * P, end, 512):
                    c1 = min(c0 + 512, end)
                    b = 2 * (k % 2) + (c0 - u["t0"] * P) // 512
                    ins = mm(PS[:, b, 0:c1 - c0], qrT[GP[g], j, q], kvT[GP[g], 2 if u["kind"] == "s" else 3, c0:c1], start=True, stop=True)
                if u["kind"] == "w":
                    ins = mm(PS[:, 2 * (k % 2) + 1, 128:191], qT[GP[g], j, q], kcp[GP[g], :], start=True, stop=True)
                E.do(ins, qk_done)

            pend = []

            def values():
                k, gi, vi, grp = pend.pop(0)
                u = UNITS[k]
                hh = k // 2
                pe.wait_ge(pt_ev, gi + 1)
                if u["kind"] == "s" and gi == u["first"] and hh >= 2:
                    pe.wait_ge(o_ev, hh - 1)
                for c, (kind, t, _) in enumerate(grp):
                    oc = 64 * "swc".index(kind)
                    out = PS[:, 6 + hh % 2, oc:oc + 64]
                    g = u["g"]
                    if kind == "c":
                        ins = mm(out, PTs[0:63, vi % 2, c * P:(c + 1) * P], vcp[0:63, g * 64:g * 64 + 64], start=True, stop=True)
                    else:
                        v = kvtok(t)[:, (384 if kind == "s" else 640) + g * 64:(384 if kind == "s" else 640) + g * 64 + 64]
                        ins = mm(out, PTs[:, vi % 2, c * P:(c + 1) * P], v, start=t == u["t0"], stop=t == u["i"])
                E.do(ins, pv_done)

            def turn_probs(k):
                u = UNITS[k]
                pe.wait_ge(exp_done, k + 1)
                for n, grp in enumerate(u["groups"]):
                    gi = u["first"] + n
                    if gi >= 2:
                        pe.wait_ge(pt_ev, gi - 1)
                    for c, (kind, t, off) in enumerate(grp):
                        w = 63 if kind == "c" else P
                        ins = turn(PS[0:w, 4 + gi % 2, c * P:(c + 1) * P], Pb[:, k % 2, off:off + w], P)
                    E.do(ins, pt_done)
                    if pend:
                        values()
                    pend.append((k, gi, u["vfirst"] + n, grp))

            def turn_heads(i):
                pe.wait_ge(o_ev, 8 * (i + 1))
                pe.wait_ge(pt_ev, HEADS[i] - 1)
                for j in range(4):
                    ins = turn(PS[:, 4 + HEADS[i] % 2, j * P:(j + 1) * P], atok[:, i % 2, j * P:(j + 1) * P], P)
                E.do(ins, pt_done)

            for k in range(len(UNITS)):
                scores(k)
                if k:
                    turn_probs(k - 1)
                if k >= 16 and k % 16 == 4:
                    turn_heads(k // 16 - 1)
            turn_probs(len(UNITS) - 1)
            while pend:
                values()
            turn_heads(7)
            E.meet()

            grp_n = [0]

            def turn4(src, nparts, width, name, per=4):
                gi = grp_n[0]
                grp_n[0] += 1
                if gi >= 2:
                    pe.wait_ge(sem("dt_ev" if (gi - 2) % 2 == 0 else "dt_ev2"), (gi - 2) // 2 + 1)
                for c, s in enumerate(src):
                    ins = turn(PS[0:width, 5 + gi % 2, c * (512 // per):c * (512 // per) + nparts], s, nparts)
                E.do(ins, sem("dt_done"))
                return gi

            def turned(gi):
                pe.wait_ge(sem("dt_ev" if gi % 2 == 0 else "dt_ev2"), gi // 2 + 1)

            pe.wait_ge(sem("win_in"), 16 * BD)
            for b in range(BD):
                gi = turn4([wKV[:, b, t, 0:P] for t in range(4)], P, P, "w")
                turned(gi)
                ins = mm(PS[0:64, 0, 0:512], qz[:, 1, b, :], kvTb[:, b % 2, 0:512], start=b == 0, stop=b == BD - 1)
                E.do(ins, sem("dk_used"))
            for c, col in ((0, 3), (1, 2)):
                for b in range(BD):
                    ins = mm(PS[0:64, 4, c:c + 1], qz[:, 1, b, :], kvT[:, col, SEQ + b:SEQ + b + 1], start=b == 0, stop=b == BD - 1)
            E.do(ins, sem("ds_done"))

            def own_key(slot, cols, first):
                gi = turn4([pself[0:64, slot, 0:8]], 64, 8, "self")
                turned(gi)
                ins = mm(PS[:, 7, 0:64], kvtok(8)[0:BD, cols:cols + P], PTs_self(slot), start=first, stop=False, skip_group_check=True)
                return ins

            def PTs_self(slot):
                return pself[0:8, 2, 0:64] if slot else sm_self

            sm_self = at(DB + 20492 - 0, 64)[0:8, :]

            pe.wait_ge(sem("dp_ready"), 1)
            own_key(0, 640, True)
            gi = turn4([SS[0:64, t * P:(t + 1) * P] for t in range(4)], 64, P, "p", per=8)
            turned(gi)
            for b in range(BD):
                for t in range(4):
                    ins = mm(PS[:, 7, b * 8:b * 8 + 8], wKV[:, b, t, P:2 * P], PTb[:, t, b * 8:b * 8 + 8], start=False, stop=False, skip_group_check=True)
            E.do(ins, sem("win_pv"))

            def compressed(b):
                pe.wait_ge(sem("dg_done"), b + 1)
                if b:
                    pe.wait_ge(sem("dkc_ev"), b)
                mm(PS[:, 3, 0:127], W2[:, 0, :], ghs[:, 0, :], start=True, stop=True)
                E.do(mm(PS[0:127, 3, 256:384], ghs[:, 1, :], W2[:, 1, :], start=True, stop=True), sem("dkc_done"))

            for b in range(BD):
                pe.wait_ge(sem(f"pg{b % 2}"), 16 * NPG * (b // 2 + 1))
                for t4 in range(4):
                    for kv in range(2):
                        gi = turn4([cpg[:, b % 2, t4 * 4 + c, kv * P:(kv + 1) * P] for c in range(4)], P, P, "c")
                if b:
                    compressed(b - 1)
                turned(gi - 1)
                turned(gi)
                if b:
                    pe.wait_ge(sem("dg_done"), b)
                hidden(0, kvTb[:, 0, :], 127, 4, 0)
                E.do(hidden(1, kvTb[:, 1, :], 127, 4, 256), sem("dh_done"))
            compressed(BD - 1)
            pe.wait_ge(sem("dkc_ev"), BD)
            for b in range(BD):
                ins = mm(PS[0:64, 2, 0:127], qz[:, 0, b, :], kcs[:, b, :], start=b == 0, stop=b == BD - 1)
            E.do(ins, sem("ds_done"))
            pe.wait_ge(sem("dp_ready"), 2)
            E.do(mm(PS[0:64, 4, 0:127], const("group", 64), Pc[0:64, :], start=True, stop=True), sem("ds_done"))
            pe.wait_ge(sem("dp_ready"), 3)
            gi = turn4([SS[0:64, 0:127]], 64, 127, "pc")
            turned(gi)
            for b in range(BD):
                ins = mm(PS[:, 7, b * 8:b * 8 + 8], vcs[0:127, b, :], PTb[0:127, 0, b * 8:b * 8 + 8], start=False, stop=False, skip_group_check=True)
            E.step(ins)
            for b in range(BD):
                pe.wait_ge(sem(f"pg{b % 2}"), 16 * NPG * (b // 2 + 5))
                gis = []
                for t4 in range(4):
                    gi = turn4([spg[:, b % 2, t4 * 4 + c, :] for c in range(4)], P, P, "k")
                    gis.append(gi)
                    if t4:
                        turned(gi - 1)
                        mm(PS[0:64, t4 - 1, :], qz[:, 1, b, :], kvTb[:, b % 2, (t4 - 1) * 512:t4 * 512], start=b == 0, stop=b == BD - 1)
                turned(gi)
                E.do(mm(PS[0:64, 3, :], qz[:, 1, b, :], kvTb[:, b % 2, 1536:2048], start=b == 0, stop=b == BD - 1), sem("dk2_used"))
            pe.wait_ge(sem("dp_ready"), 4)
            own_key(1, 384, False)
            for h8 in range(2):
                gi = turn4([SS[0:64, (h8 * 8 + c) * P:(h8 * 8 + c + 1) * P] for c in range(8)], 64, P, "p", per=8)
            turned(gi - 1)
            turned(gi)
            for b in range(BD):
                pe.wait_ge(sem(f"pg{b % 2}"), 16 * NPG * (b // 2 + 9))
                for t in range(NPG):
                    ins = mm(PS[:, 7, b * 8:b * 8 + 8], spg[:, b % 2, t, :], PTb[:, t, b * 8:b * 8 + 8], start=False, stop=b == BD - 1 and t == NPG - 1, skip_group_check=True)
                E.do(ins, sem("spv_used"))
            E.meet()

            pe.wait_ge(sem("vec_in"), 9 * 16)
            for n in range(KT):
                ins = turn(PS[:, 7, n * 40:(n + 1) * 40], vrows[0:40, n * P:(n + 1) * P], 40)
            E.do(ins, sem("vec_T"))

            def product(b, bank, rhs, kts):
                s = b % RING
                pe.wait_ge(s_ring[s], due[b])
                for c in range(3):
                    for k in range(kts):
                        ins = mm(PS[:, bank + c, 0:CH], ring[:, s, k, :], rhs[:, k, c * CH:(c + 1) * CH], start=k == 0, stop=k == kts - 1)
                E.do(ins, w_used)

            for n in range(KT):
                if n:
                    pe.wait_ge(sem("r_ev"), n)
                product(2 * n, 0, xT, KT)
                if n:
                    pe.wait_ge(sem("i_ev"), n)
                product(2 * n + 1, 3, xT, KT)
                if n:
                    pe.wait_ge(sem("stg_done"), n)
                    if n > 1:
                        pe.wait_ge(sem("stg_ev"), n - 1)
                    E.do(turn(PS[0:20, 6, 0:P], stg[:, :], P), sem("stg_T"))
                pe.wait_ge(sem("xc_done"), n + 1)
                for c in range(3):
                    ins = mm(PS[:, c, 0:CH], wra[:, n, :], xc[:, c * CH:(c + 1) * CH], start=True, stop=True)
                E.do(ins, sem("r_mm"))
                pe.wait_ge(sem("g_ev"), n + 1)
                for c in range(3):
                    ins = mm(PS[:, 3 + c, 0:CH], wri[:, n, :], xc[:, c * CH:(c + 1) * CH], start=True, stop=True)
                E.do(ins, sem("i_mm"))
            pe.wait_ge(sem("stg_done"), KT)
            pe.wait_ge(sem("stg_ev"), KT - 1)
            E.do(turn(PS[0:20, 6, 0:P], stg[:, :], P), sem("stg_T"))
            E.meet()

            for n in range(KT):
                b = 2 * KT + 4 * n
                if n:
                    pe.wait_ge(sem("sg_done"), 2 * n)
                product(b, 0, xT, KT)
                if n:
                    pe.wait_ge(sem("mg_done"), 2 * n)
                product(b + 1, 3, AT, 4)
                pe.wait_ge(sem("sg_done"), 2 * n + 1)
                product(b + 2, 0, xT, KT)
                pe.wait_ge(sem("mg_done"), 2 * n + 1)
                product(b + 3, 3, RT, KT)
            E.meet()

            pe.wait_ge(sem("wout_in"), 16)

            def turn_x1(t):
                n = rows_of(t)
                pe.wait_ge(sem("x1_done"), t + 1)
                for hf in range(2):
                    gi = 2 * t + hf
                    if gi >= 2:
                        pe.wait_ge(sem("x1T_ev"), gi - 1)
                    for k in range(4):
                        ins = turn(PS[:, 4 + gi % 2, k * P:k * P + n], x1tok[0:n, t, (hf * 4 + k) * P:(hf * 4 + k + 1) * P], n)
                    E.do(ins, sem("x1_T"))

            for t in range(NT):
                n = rows_of(t)
                if t >= 2:
                    pe.wait_ge(sem("xr_used"), t - 1)
                for c in range(2):
                    for k in range(KT):
                        ins = mm(PS[0:n, 2 * (t % 2) + c, :], mT[:, k, t * P:t * P + n], wout[:, k, c * 512:(c + 1) * 512], start=k == 0, stop=k == KT - 1)
                E.do(ins, sem("mix_mm"))
                if t >= 2:
                    turn_x1(t - 2)
            turn_x1(NT - 2)
            turn_x1(NT - 1)
            E.meet()
            pe.wait_ge(sem("wrt_in"), 32)
            for t in range(NT):
                n = rows_of(t)
                if t >= 2:
                    pe.wait_ge(sem("lg_ev"), t - 1)
                for k in range(KT):
                    ins = mm(PS[0:n, 6 + t % 2, 0:NE], x1T[:, k, t * P:t * P + n], wrt[:, k, :], start=k == 0, stop=k == KT - 1)
                E.do(ins, sem("lg_mm"))
            pe.wait_ge(sem("wsh_in"), 48)
            for hb in range(2):
                for bank, w in ((0, wsg), (3, wsu)):
                    if hb:
                        pe.wait_ge(sem("sil_done" if bank == 0 else "shT_done"), 1)
                    for c in range(3):
                        for k in range(KT):
                            ins = mm(PS[:, bank + c, 0:CH], w[:, k, hb * P:(hb + 1) * P], x1T[:, k, c * CH:(c + 1) * CH], start=k == 0, stop=k == KT - 1)
                    E.do(ins, sem("sh_mm"))
            pe.wait_ge(sem("M_done"), NT)
            pe.wait_ge(sem("lg_ev"), NT)
            for t in range(NT):
                n = rows_of(t)
                ins = mm(PS[:, 6, 0:NE], const("ones", n), Mm[0:n, t, :], start=t == 0, stop=t == NT - 1)
            E.do(ins, sem("table_mm"))
            pe.wait_ge(sem("shT_done"), 2)
            for t in range(NT):
                n = rows_of(t)
                if t >= 2:
                    pe.wait_ge(sem("acc_done"), t - 1)
                for c in range(2):
                    for hb in range(2):
                        ins = mm(PS[0:n, 2 * (t % 2) + c, :], shT[:, hb, t * P:t * P + n], wsd[:, hb, c * 512:(c + 1) * 512], start=hb == 0, stop=hb == 1)
                E.do(ins, sem("shd_mm"))
                if t >= 2:
                    pe.wait_ge(sem("dst_done"), t - 1)
                ins = mm(PS[0:n, 4 + t % 2, 0:NE], const("before", n)[:, 0:n], Mm[0:n, t, :], start=True, stop=t == 0)
                for u in range(t):
                    ins = mm(PS[0:n, 4 + t % 2, 0:NE], const("ones")[:, 0:n], Mm[:, u, :], start=False, stop=u == t - 1)
                E.do(ins, sem("rk_mm"))
            pe.wait_ge(sem("table_step"), 1)
            E.do(turn(PS[0:1, 7, 0:P], ridx[:, 0:1], P), sem("table_mm"))
            pe.wait_ge(sem("table_step"), 2)
            E.do(turn(PS[:, 7, 128:128 + NBLK], trow[0:NBLK, :], NBLK), sem("table_mm"))
            for name, n in (("gu_mm0", 1), ("gu_mm1", 1), ("y_mm", 2), ("xgT_mm1", 2)):
                pe.nop().then_inc(sem(name), n)
            E.meet()
            turns = pe.value_load(nblk[0:1, 0:1], min_val=1, max_val=NBLK // 2)
            with pe.Fori(0, NBLK // 2) as i:
                with pe.If(i < turns):
                    for s in range(2):
                        pe.wait_ge(sem(f"xg{s}"), 16 * i + 16)
                        for hf in range(2):
                            pe.wait_ge(sem(f"xgT_ev{hf}"), 2 * i + s + 1)
                            for k in range(4):
                                ins = turn(PS[:, hf, k * P:(k + 1) * P], xg[:, s, hf * 4 + k::8], P)
                            ins.then_inc(sem(f"xgT_mm{hf}"), 1)
                    for s in range(2):
                        pe.wait_ge(sem("xgT_ev0"), 2 * i + s + 2)
                        pe.wait_ge(sem("xgT_ev1"), 2 * i + s + 2)
                        pe.wait_ge(sem(f"wex{s}"), 32 * i + 32)
                        pe.wait_ge(sem(f"gu_free{s}"), i + 1)
                        for h, w in ((0, wexg), (1, wexu)):
                            for k in range(KT):
                                ins = mm(PS[:, 2 + s, h * DE:(h + 1) * DE], xgT[:, s, k, :], w[:, s, k, :], start=k == 0, stop=k == KT - 1)
                        ins.then_inc(sem(f"gu_mm{s}"), 1)
                    for s in range(2):
                        pe.wait_ge(sem(f"gu_free{s}"), i + 2)
                        pe.wait_ge(sem("hT_ev"), 2 * i + s + 1)
                        for k in range(2):
                            ins = turn(PS[:, 4, k * P:(k + 1) * P], hh_[:, s, k::2], P)
                        ins.then_inc(sem("hT_mm"), 1)
                        pe.wait_ge(sem("hT_ev"), 2 * i + s + 2)
                        pe.wait_ge(sem(f"wexd{s}"), 16 * i + 16)
                        pe.wait_ge(sem("y_ev"), 2 * i + s + 1)
                        pe.wait_ge(sem("y_ev2"), 2 * i + s + 1)
                        for c in range(2):
                            for k in range(2):
                                ins = mm(PS[:, 5 + c, :], hT[:, s, k, :], wexd[:, s, k, c * 512:(c + 1) * 512], start=k == 0, stop=k == 1)
                        ins.then_inc(sem("y_mm"), 1)

        @block.scalar
        def _(act):
            E = Engine(act, sem("act_chain"), met[1], (met[0], met[2]))
            fn = nc.scalar.activation

            def copy(out, in_):
                return fn(out, in_, ACT.Copy)

            for t in range(NT):
                n = rows_of(t)
                for hf in range(2):
                    gi = 2 * t + hf
                    act.wait_ge(x_turned, gi + 1)
                    E.do(copy(xT[:, hf * 4:hf * 4 + 4, t * P:t * P + n],
                              PS[:, gi % 4, :].rearrange("p (k c) -> p k c", k=4)[:, :, 0:n]), xT_ready)

            def tok_T(t):
                n = rows_of(t)
                for g3 in range(3):
                    gi = 3 * t + g3
                    act.wait_ge(tok_turned, gi + 1)
                    E.do(copy((qT, qrT, kvT)[g3][:, :, t * P:t * P + n],
                              PS[:, 6 + gi % 2, :].rearrange("p (k c) -> p k c", k=4)[:, :, 0:n]), tokT_ready)

            for t in range(NT):
                n = rows_of(t)
                b0 = 3 * (t % 2)
                act.wait_ge(tok_mm, t + 1)
                if t >= 2:
                    act.wait_ge(tok_turned, 3 * (t - 1))
                E.do(copy(qtok[0:n, t % 2, :].rearrange("p (j g d) -> p g j d", j=4, g=2),
                          PS[0:n, b0, :].rearrange("p (g j d) -> p g j d", g=2, j=4)))
                E.do(copy(kvtok(t)[0:n, 0:512], PS[0:n, b0 + 1, :]))
                E.do(copy(kvtok(t)[0:n, 512:768], PS[0:n, b0 + 2, 0:256]))
                E.do(fn(gate[0:n, t, :], PS[0:n, b0 + 2, 256:280], ACT.Sigmoid), tok_ev)
                if t:
                    tok_T(t - 1)
            tok_T(NT - 1)
            E.meet()
            act.wait_ge(cmp_mm, 1)
            E.do(copy(posT.rearrange("p a b -> p (a b)"), PS[:, 7, 0:64]), cmp_ev)
            act.wait_ge(cmp_mm, 2)
            E.step(copy(cbias, PS[:, 7, 64:66]), cmp_ev)
            act.wait_ge(cmp_mm, 3)
            E.do(fn(gh[:, 0, 0:63], PS[:, 6, 0:63], ACT.Gelu_apprx_tanh, bias=cbias[:, 0:1]))
            E.do(fn(gh[:, 1, 0:63], PS[:, 6, 256:319], ACT.Gelu_apprx_tanh, bias=cbias[:, 1:2]), cmp_ev)
            act.wait_ge(cmp_mm, 4)
            E.do(copy(kcp, PS[:, 5, 0:63]))
            E.do(copy(vcp[0:63, :], PS[0:63, 5, 256:384]), cmp_ev)
            E.meet()

            def probs(k):
                u = UNITS[k]
                hh = k // 2
                act.wait_ge(mx_done, k + 1)
                if k >= 2:
                    act.wait_ge(pt_done, UNITS[k - 1]["first"])
                if hh >= 2:
                    act.wait_ge(o_ev, hh - 1)
                n = (u["i"] + 1 - u["t0"]) * P
                S = PS[:, 2 * (k % 2):2 * (k % 2) + 2, :].rearrange("p a b -> p (a b)")
                if u["kind"] == "s":
                    E.do(fn(Pb[:, k % 2, 0:n], S[:, 0:n], ACT.Exp, bias=negb[:, k % 2, 0:1], scale=SCALE, accum_out=sums[:, hh % 2, 0:1]), exp_done)
                else:
                    E.do(fn(Pb[:, k % 2, 640:703], S[:, 640:703], ACT.Exp, bias=negb[:, k % 2, 1:2], scale=SCALE, accum_out=sums[:, hh % 2, 2:3]))
                    E.do(fn(Pb[:, k % 2, 0:n], S[:, 0:n], ACT.Exp, bias=negb[:, k % 2, 0:1], scale=SCALE, accum_out=sums[:, hh % 2, 1:2]), exp_done)

            def take_turned(k):
                u = UNITS[k]
                for n, grp in enumerate(u["groups"]):
                    gi = u["first"] + n
                    act.wait_ge(pt_done, gi + 1)
                    vi = u["vfirst"] + n
                    if vi >= 2:
                        act.wait_ge(pv_done, vi - 1)
                    w = len(grp) - (grp[-1][0] == "c")
                    c_last = grp[-1][0] == "c"
                    if w:
                        ins = copy(PTs[:, vi % 2, 0:w * P], PS[:, 4 + gi % 2, 0:w * P])
                        if c_last:
                            E.do(ins)
                    if c_last:
                        ins = copy(PTs[0:63, vi % 2, w * P:(w + 1) * P], PS[0:63, 4 + gi % 2, w * P:(w + 1) * P])
                    E.do(ins, pt_ev)

            def heads_T(i):
                act.wait_ge(pt_done, HEADS[i] + 1)
                E.do(copy(AT[:, :, i * P:(i + 1) * P], PS[:, 4 + HEADS[i] % 2, :].rearrange("p (k c) -> p k c", k=4)), pt_ev)

            for k in range(len(UNITS)):
                if k:
                    take_turned(k - 1)
                probs(k)
                if k >= 16 and k % 16 == 4:
                    heads_T(k // 16 - 1)
            take_turned(len(UNITS) - 1)
            heads_T(7)
            E.meet()

            dt_ev = sem("dt_ev")
            gi = 0
            for b in range(BD):
                if gi % 2 == 0:
                    act.wait_ge(sem("dt_done"), gi + 1)
                    if b >= 2:
                        act.wait_ge(sem("dk_used"), b - 1)
                    E.do(copy(kvTb[:, b % 2, 0:512], PS[:, 5 + gi % 2, :]), dt_ev)
                gi += 1

            def softmax_exp(n, slot):
                act.wait_ge(sem("dmx_done"), slot + 1)
                E.step(fn(SS[0:64, 0:n], SS[0:64, 0:n], ACT.Exp, bias=sm[0:64, slot, 1:2], scale=SCALE, accum_out=sm[0:64, slot, 2:3]), sem("dexp_done"))

            softmax_exp(513, 0)
            act.wait_ge(sem("dt_done"), gi + 1)
            E.do(copy(at(DB + 20492, 64)[0:8, :], PS[0:8, 5 + gi % 2, 0:64]), dt_ev)
            gi += 2
            for b in range(BD):
                for t4 in range(4):
                    act.wait_ge(sem("dt_done"), gi + 1)
                    if t4 == 0 and b:
                        act.wait_ge(sem("dh_done"), b)
                    E.do(copy(kvTb[:, 0, t4 * 512:(t4 + 1) * 512], PS[:, 5 + gi % 2, :]), dt_ev)
                    gi += 2
                act.wait_ge(sem("dh_done"), b + 1)
                if b:
                    act.wait_ge(sem("dkc_done"), b)
                for kv in range(2):
                    E.do(fn(ghs[:, kv, :], PS[:, 4, 256 * kv:256 * kv + 127], ACT.Gelu_apprx_tanh, bias=cbias[:, kv:kv + 1]), sem("dg_done") if kv else None)
                if b:
                    E.do(copy(kcs[:, b - 1, :], PS[:, 3, 0:127]))
                    E.do(copy(vcs[0:127, b - 1, :], PS[0:127, 3, 256:384]), sem("dkc_ev"))
            act.wait_ge(sem("dkc_done"), BD)
            E.do(copy(kcs[:, BD - 1, :], PS[:, 3, 0:127]))
            E.do(copy(vcs[0:127, BD - 1, :], PS[0:127, 3, 256:384]), sem("dkc_ev"))
            softmax_exp(127, 1)
            act.wait_ge(sem("dt_done"), gi + 1)
            E.do(copy(PTb[0:127, 0, :], PS[0:127, 5 + gi % 2, 0:64]), dt_ev)
            gi += 1
            for b in range(BD):
                for t4 in range(4):
                    if gi % 2 == 0:
                        act.wait_ge(sem("dt_done"), gi + 1)
                        if b >= 2:
                            act.wait_ge(sem("dk2_used"), b - 1)
                        E.do(copy(kvTb[:, b % 2, t4 * 512:(t4 + 1) * 512], PS[:, 5 + gi % 2, :]), dt_ev)
                    gi += 1
            softmax_exp(2049, 2)
            gi += 1
            act.wait_ge(sem("dt_done"), gi + 1)
            E.do(copy(PTb[:, 0:8, :], PS[:, 5 + gi % 2, :].rearrange("p (k c) -> p k c", k=8)), dt_ev)
            E.meet()

            act.wait_ge(sem("vec_T"), 1)
            E.step(copy(vec.rearrange("p a b -> p (a b)"), PS[:, 7, 0:320]), sem("vec_ev"))
            act.wait_ge(sem("lam_step"), 1)
            E.do(fn(lam[:, 1, :], lam[:, 0, :], ACT.Exp, scale=-1.0), sem("lam_exp"))
            act.wait_ge(sem("lam_step"), 2)

            def rows_T(n):
                act.wait_ge(sem("stg_T"), n + 1)
                E.do(copy(orows[0:20, n * P:(n + 1) * P], PS[0:20, 6, 0:P]), sem("stg_ev"))

            for n in range(KT):
                act.wait_ge(w_used, 2 * n + 1)
                if n:
                    act.wait_ge(sem("xc_done"), n)
                E.do(copy(ucb[:, 3:691].rearrange("p (a b) -> p a b", a=2), PS[:, 0:2, 0:CH]))
                E.do(copy(ucb[:, 691:1027], PS[:, 2, 0:336]))
                E.do(copy(ucs[:, :, 3], PS[:, 2, 336:344]), sem("u_ev"))
                act.wait_ge(w_used, 2 * n + 2)
                if n >= 2:
                    act.wait_ge(sem("stg_done"), n - 1)
                E.do(fn(gg[:, n % 2, :].rearrange("p (a b) -> p a b", a=3), PS[:, 3:6, 0:CH], ACT.Gelu_apprx_tanh), sem("g_ev"))
                act.wait_ge(sem("r_mm"), n + 1)
                if n:
                    act.wait_ge(sem("stg_done"), n)
                E.step(fn(rr.rearrange("p (a b) -> p a b", a=3), PS[:, 0:3, 0:CH], ACT.Sigmoid, bias=vec[:, n, 37:38]), sem("r_ev"))
                act.wait_ge(sem("i_mm"), n + 1)
                E.do(fn(ii.rearrange("p (a b) -> p a b", a=3), PS[:, 3:6, 0:CH], ACT.Sigmoid, bias=vec[:, n, 38:39]), sem("i_ev"))
                E.do(fn(aa, rr, ACT.Exp, scale=lam[:, 3, n:n + 1]))
                E.do(fn(th, rr, ACT.Tanh, scale=lam[:, 4, n:n + 1]), sem("a_done"))
                act.wait_ge(sem("v_done"), n + 1)
                E.do(fn(vv, vv, ACT.Sqrt), sem("sq_done"))
                if n:
                    rows_T(n - 1)
            rows_T(KT - 1)
            E.settle()
            act.nop().then_inc(sem("rows_ready"), 1)
            act.wait_ge(sem("rows_out"), 1)
            E.meet()
            for n in range(KT):
                for h in range(2):
                    act.wait_ge(w_used, 2 * KT + 4 * n + 2 * h + 1)
                    if n:
                        act.wait_ge(sem("mg_done"), 2 * (n - 1) + h + 1)
                    E.do(fn(sg[:, h, :].rearrange("p (a b) -> p a b", a=3), PS[:, 0:3, 0:CH], ACT.Sigmoid), sem("sg_done"))
            E.meet()

            def x1_T(t):
                n = rows_of(t)
                for hf in range(2):
                    gi = 2 * t + hf
                    act.wait_ge(sem("x1_T"), gi + 1)
                    E.do(copy(x1T[:, hf * 4:hf * 4 + 4, t * P:t * P + n],
                              PS[:, 4 + gi % 2, :].rearrange("p (k c) -> p k c", k=4)[:, :, 0:n]), sem("x1T_ev"))

            for t in range(NT):
                n = rows_of(t)
                act.wait_ge(sem("var_done"), t + 1)
                E.do(fn(st[0:n, t % 2, 14:15], st[0:n, t % 2, 13:14], ACT.Sqrt), sem("std_done"))
                if t >= 2:
                    x1_T(t - 2)
            x1_T(NT - 2)
            x1_T(NT - 1)
            E.meet()
            for t in range(NT):
                n = rows_of(t)
                act.wait_ge(sem("lg_mm"), t + 1)
                E.do(fn(sc[0:n, t, :], PS[0:n, 6 + t % 2, 0:NE], ACT.Sigmoid), sem("lg_ev"))
            for hb in range(2):
                act.wait_ge(sem("sh_mm"), 2 * hb + 1)
                if hb:
                    act.wait_ge(sem("shT_done"), 1)
                E.do(fn(sil.rearrange("p (a b) -> p a b", a=3), PS[:, 0:3, 0:CH], ACT.Silu), sem("sil_done"))
            for name in ("y_ev", "hT_ev", "xgT_ev0", "xgT_ev1", "yd0", "yd1"):
                act.nop().then_inc(sem(name), 1)
            E.meet()
            turns = act.value_load(nblk[0:1, 0:1], min_val=1, max_val=NBLK // 2)
            with act.Fori(0, NBLK // 2) as i:
                with act.If(i < turns):
                    for s in range(2):
                        for hf in range(2):
                            act.wait_ge(sem(f"xgT_mm{hf}"), i * 2 + s + 1 + 2 * hf)
                            if hf == 0:
                                act.wait_ge(sem(f"gu_mm{s}"), i + 1)
                            copy(xgT[:, s, hf * 4:hf * 4 + 4, :], PS[:, hf, :].rearrange("p (k c) -> p k c", k=4)).then_inc(sem(f"xgT_ev{hf}"), 1)
                    for s in range(2):
                        act.wait_ge(sem(f"gu_mm{s}"), i + 2)
                        act.wait_ge(sem(f"gu_free{s}"), i + 1)
                        fn(hsl[:, s, :], PS[:, 2 + s, 0:DE], ACT.Silu).then_inc(sem("sl_done"), 1)
                    for s in range(2):
                        act.wait_ge(sem("hT_mm"), 2 * i + s + 1)
                        act.wait_ge(sem("y_mm"), 2 * i + s + 1)
                        copy(hT[:, s, :, :], PS[:, 4, 0:256].rearrange("p (k c) -> p k c", k=2)).then_inc(sem("hT_ev"), 1)
                        act.wait_ge(sem("y_mm"), 2 * i + s + 3)
                        act.wait_ge(sem(f"yd{s}"), 16 * i + 1)
                        copy(ysb[:, s, 512:1024], PS[:, 6, :]).then_inc(sem("y_ev"), 1)
                        act.wait_ge(sem("y_ev2"), 2 * i + s + 2)
                        act.wait_ge(sem("y_ev"), 2 * i + s + 2)
                        act.dma_start(y_dram[bass.ds(i * 2 + s, 1), :, :].rearrange("u p d -> (u p) d"), ysb[:, s, :]).then_inc(sem(f"yd{s}"), 16)
            act.wait_ge(sem("yd0"), turns * 16 + 1)
            act.wait_ge(sem("yd1"), turns * 16 + 1)
            act.nop().then_inc(sem("y_all"), 1)
            for t in range(NT):
                n = rows_of(t)
                act.wait_ge(sem("var_done"), NT + t + 1)
                fn(st[0:n, t % 2, 14:15], st[0:n, t % 2, 13:14], ACT.Sqrt).then_inc(sem("std_done"), 1)

        @block.vector
        def _(dve):
            E = Engine(dve, sem("dve_chain"), met[2], (met[0], met[1]))
            V = nc.vector
            tt, ts, stt = V.tensor_tensor, V.tensor_scalar, V.scalar_tensor_tensor
            dve.wait_ge(s_const, 32)
            E.do(V.tensor_copy(tokid[:, :], const("tokid")))
            E.do(V.memset(izero[:, :], 0))
            E.step(V.memset(ztab[:, :], 0), sem("ztab_set"))
            cosv = const("cos").rearrange("p (t c) -> p t c", c=8)
            sinv = const("sin").rearrange("p (t c) -> p t c", c=8)

            def rope(x1, x2, y1, y2, cs_, sn_, tmp):
                E.do(tt(tmp[0], x1, cs_, ALU.mult))
                E.do(tt(tmp[1], x2, sn_, ALU.mult))
                E.do(tt(tmp[2], x2, cs_, ALU.mult))
                E.step(tt(tmp[3], x1, sn_, ALU.mult))
                E.do(tt(y1, tmp[0], tmp[1], ALU.subtract))

            for t in range(NT):
                n = rows_of(t)
                dve.wait_ge(tok_ev, t + 1)
                if t >= 2:
                    dve.wait_ge(tok_turned, 3 * (t - 1))
                E.step(V.tensor_copy(qrtok[0:n, t % 2, :], qtok[0:n, t % 2, :]))
                q3 = qtok[0:n, t % 2, :].rearrange("p (h d) -> p h d", h=NH)
                r3 = qrtok[0:n, t % 2, :].rearrange("p (h d) -> p h d", h=NH)
                tm = [rt[0:n, k, :].rearrange("p (h c) -> p h c", h=8) for k in range(4)]
                c3 = cosv[0:n, t:t + 1, :].broadcast_to([n, 8, 8])
                s3 = sinv[0:n, t:t + 1, :].broadcast_to([n, 8, 8])
                rope(q3[:, :, 0:8], q3[:, :, 8:16], r3[:, :, 0:8], r3[:, :, 8:16], c3, s3, tm)
                E.step(tt(r3[:, :, 8:16], tm[2], tm[3], ALU.add))
                for j in range(2):
                    k3 = kvtok(t)[0:n, KV * (1 + j):KV * (1 + j) + P].rearrange("p (h d) -> p h d", h=2)
                    tm2 = [rt[0:n, k, 0:16].rearrange("p (h c) -> p h c", h=2) for k in range(4)]
                    c2, s2 = c3[:, 0:2, :], s3[:, 0:2, :]
                    rope(k3[:, :, 0:8], k3[:, :, 8:16], k3[:, :, 0:8], k3[:, :, 8:16], c2, s2, tm2)
                    E.step(tt(k3[:, :, 8:16], tm2[2], tm2[3], ALU.add), rope_done if j else None)
            E.meet()
            E.meet()

            def maxima(k):
                u = UNITS[k]
                i = u["i"]
                dve.wait_ge(qk_done, k + 1)
                n = (i + 1 - u["t0"]) * P
                S = PS[:, 2 * (k % 2):2 * (k % 2) + 2, :].rearrange("p a b -> p (a b)")
                E.do(tt(S[:, n - P:n], S[:, n - P:n], const("diag"), ALU.add))
                if u["kind"] == "w":
                    if i >= 4:
                        E.do(tt(S[:, 0:P], S[:, 0:P], const("edge"), ALU.add))
                    E.do(tt(S[:, 640:703], S[:, 640:703], const("cmpm")[:, i * 63:(i + 1) * 63], ALU.add))
                E.settle()
                if u["kind"] == "w":
                    E.do(V.reduce_max(mx[:, 1:2], S[:, 640:703], AX))
                E.step(V.reduce_max(mx[:, 0:1], S[:, 0:n], AX))
                if u["kind"] == "w":
                    E.do(ts(negb[:, k % 2, 1:2], mx[:, 1:2], -1e28, -SCALE, ALU.max, ALU.mult))
                E.do(ts(negb[:, k % 2, 0:1], mx[:, 0:1], -SCALE, None, ALU.mult), mx_done)

            def combine(hh):
                u = UNITS[2 * hh + 1]
                i, j, g = u["i"], u["j"], u["g"]
                h = 4 * g + j
                E.settle()
                dve.wait_ge(pv_done, u["vfirst"] + len(u["groups"]))
                E.step(ts(coef, sums[:, hh % 2, :], 1e-30, None, ALU.max))
                E.step(V.reciprocal(coef, coef))
                E.step(tt(coef, coef, gate[:, i, 3 * h + 0:3 * h + 3], ALU.mult))
                out = atok[:, i % 2, j * P + g * 64:j * P + g * 64 + 64]
                O = PS[:, 6 + hh % 2, 0:192]
                if i >= 2:
                    dve.wait_ge(pt_done, HEADS[i - 2] + 1)
                E.step(ts(out, O[:, 0:64], coef[:, 0:1], None, ALU.mult))
                E.step(stt(out, O[:, 64:128], coef[:, 1:2], out, ALU.mult, ALU.add))
                E.step(stt(out, O[:, 128:192], coef[:, 2:3], out, ALU.mult, ALU.add), o_ev)

            for t in range(NT):
                n = rows_of(t)
                g3 = gate[0:n, t, :].rearrange("p (h c) -> p h c", c=3)
                E.step(V.tensor_copy(rt[0:n, 0, 0:8], g3[:, :, 0]))
                E.step(V.tensor_copy(rt[0:n, 1, 0:16].rearrange("p (h c) -> p h c", c=2), g3[:, :, 1:3]))
                E.do(V.tensor_copy(g3[:, :, 0:2], rt[0:n, 1, 0:16].rearrange("p (h c) -> p h c", c=2)))
                E.step(V.tensor_copy(g3[:, :, 2], rt[0:n, 0, 0:8]))
            for k in range(len(UNITS)):
                maxima(k)
                if k >= 3 and k % 2:
                    combine((k - 3) // 2)
            combine(len(UNITS) // 2 - 1)
            E.step(V.memset(qz.rearrange("p a b c -> p (a b c)"), 0.0))
            for r, src in ((0, qT), (1, qrT)):
                for g in range(2):
                    v = qz[GP[g], r, :, :].rearrange("p b c -> p (b c)")
                    for j in range(4):
                        E.do(V.tensor_copy(v[:, 4 * g + j::72], src[GP[g], j, SEQ:NTOK]))
            E.meet()

            dt2 = sem("dt_ev2")
            dve.wait_ge(sem("gsel_in"), 16)
            gi = 0
            for b in range(BD):
                if gi % 2:
                    dve.wait_ge(sem("dt_done"), gi + 1)
                    if b >= 2:
                        dve.wait_ge(sem("dk_used"), b - 1)
                    E.do(V.tensor_copy(kvTb[:, b % 2, 0:512], PS[:, 5 + gi % 2, :]), dt2)
                gi += 1

            def softmax_in(n, slot):
                E.step(V.reduce_max(sm[0:64, slot, 0:1], SS[0:64, 0:n], AX))
                E.step(ts(sm[0:64, slot, 1:2], sm[0:64, slot, 0:1], -SCALE, None, ALU.mult), sem("dmx_done"))

            def inverse(slot):
                dve.wait_ge(sem("dexp_done"), slot + 1)
                E.step(V.reciprocal(sm[0:64, slot, 3:4], sm[0:64, slot, 2:3]))

            dve.wait_ge(sem("ds_done"), 1)
            E.do(V.tensor_copy(SS[0:64, 0:512], PS[0:64, 0, :]))
            E.do(V.tensor_copy(sm[0:64, 6, 0:1], PS[0:64, 4, 1:2]))
            E.step(V.tensor_copy(SS[0:64, 512:513], PS[0:64, 4, 0:1]))
            softmax_in(513, 0)
            inverse(0)
            E.step(tt(sm[0:64, 0, 4:5], sm[0:64, 0, 3:4], gsel[0:64, 1:2], ALU.mult))
            E.step(ts(SS[0:64, 0:513], SS[0:64, 0:513], sm[0:64, 0, 4:5], None, ALU.mult))
            E.step(ts(pself[0:64, 0, 0:8], const("own", 64), SS[0:64, 512:513], None, ALU.mult), sem("dp_ready"))
            gi += 1
            dve.wait_ge(sem("dt_done"), gi + 1)
            E.do(V.tensor_copy(PTb[:, 0:4, :], PS[:, 5 + gi % 2, 0:256].rearrange("p (k c) -> p k c", k=4)), dt2)
            gi += 1
            for b in range(BD):
                for t4 in range(4):
                    gi += 1
                    dve.wait_ge(sem("dt_done"), gi + 1)
                    if t4 == 0 and b:
                        dve.wait_ge(sem("dh_done"), b)
                    E.do(V.tensor_copy(kvTb[:, 1, t4 * 512:(t4 + 1) * 512], PS[:, 5 + gi % 2, :]), dt2)
                    gi += 1
            dve.wait_ge(sem("ds_done"), 2)
            dve.wait_ge(sem("win_pv"), 1)
            E.step(V.tensor_copy(SS[0:64, 0:127], PS[0:64, 2, 0:127]))
            softmax_in(127, 1)
            inverse(1)
            E.step(ts(Pc[0:64, :], SS[0:64, 0:127], sm[0:64, 1, 3:4], None, ALU.mult), sem("dp_ready"))
            E.step(ts(SS[0:64, 0:127], Pc[0:64, :], gsel[0:64, 2:3], None, ALU.mult), sem("dp_ready"))
            E.step(V.memset(zc[0:64, :], 0.0))
            dve.wait_ge(sem("ds_done"), 3)
            E.step(V.tensor_copy(zc[0:64, 1:128], PS[0:64, 4, 0:127]))
            z = zc[0:64, 0:132].rearrange("p (s c) -> p s c", c=4)
            imp = sm[0:64, 3, 0:32]
            E.step(tt(imp, z[:, 0:32, 1], z[:, 0:32, 2], ALU.add))
            E.step(tt(imp, imp, z[:, 0:32, 3], ALU.add))
            E.step(stt(imp, imp, 2.0, z[:, 0:32, 0], ALU.mult, ALU.add))
            E.step(tt(imp, imp, z[:, 1:33, 0], ALU.add))
            E.step(V.memset(sm[0:64, 3, 32:33], 0.0))
            E.step(tt(sm[0:64, 3, 0:33], sm[0:64, 3, 0:33], const("free", 64), ALU.mult))
            E.step(tt(sm[0:64, 3, 0:33], sm[0:64, 3, 0:33], const("force", 64), ALU.add))
            score = sm[0:64, 3, 0:33]
            row = sm[0:64, 3:4, 0:33].broadcast_to([64, 33, 33])
            E.do(V.tensor_copy(rank[0:64, 0, :].rearrange("p (a b) -> p a b", a=33), row))
            E.step(V.tensor_copy(rank[0:64, 1, :].rearrange("p (a b) -> p a b", a=33), score.unsqueeze(2).broadcast_to([64, 33, 33])))
            ra, rb_ = rank[0:64, 0, :], rank[0:64, 1, :]
            big = SS[0:64, 200:200 + 1089]
            E.step(tt(big, ra, rb_, ALU.is_gt))
            E.step(tt(rb_, ra, rb_, ALU.is_equal))
            E.step(tt(rb_, rb_, const("lower", 64), ALU.mult))
            E.step(tt(big, big, rb_, ALU.add))
            E.step(V.tensor_reduce(sm[0:64, 4, 0:33], big.rearrange("p (a b) -> p a b", a=33), AX, ALU.add))
            E.step(ts(selmask[0:64, :], sm[0:64, 4, 0:33], 15.5, NEG, ALU.is_gt, ALU.mult))
            gi += 1
            for b in range(BD):
                for t4 in range(4):
                    if gi % 2:
                        dve.wait_ge(sem("dt_done"), gi + 1)
                        if b >= 2:
                            dve.wait_ge(sem("dk2_used"), b - 1)
                        E.do(V.tensor_copy(kvTb[:, b % 2, t4 * 512:(t4 + 1) * 512], PS[:, 5 + gi % 2, :]), dt2)
                    gi += 1
            dve.wait_ge(sem("dk2_used"), BD)
            for c in range(4):
                E.do(tt(SS[0:64, c * 512:(c + 1) * 512].rearrange("p (a b) -> p a b", a=8),
                        PS[0:64, c, :].rearrange("p (a b) -> p a b", a=8),
                        selmask[0:64, c * 8:(c + 1) * 8].unsqueeze(2).broadcast_to([64, 8, 64]), ALU.add))
            E.step(V.tensor_copy(SS[0:64, 2048:2049], sm[0:64, 6, 0:1]))
            softmax_in(2049, 2)
            inverse(2)
            E.step(tt(sm[0:64, 2, 4:5], sm[0:64, 2, 3:4], gsel[0:64, 0:1], ALU.mult))
            E.step(ts(SS[0:64, 0:2049], SS[0:64, 0:2049], sm[0:64, 2, 4:5], None, ALU.mult))
            E.step(ts(pself[0:64, 1, 0:8], const("own", 64), SS[0:64, 2048:2049], None, ALU.mult), sem("dp_ready"))
            dve.wait_ge(sem("dt_done"), gi + 1)
            E.do(V.tensor_copy(pself[0:8, 2, 0:64], PS[0:8, 5 + gi % 2, 0:64]), dt2)
            gi += 2
            dve.wait_ge(sem("dt_done"), gi + 1)
            E.do(V.tensor_copy(PTb[:, 8:16, :], PS[:, 5 + gi % 2, :].rearrange("p (k c) -> p k c", k=8)), dt2)
            dve.wait_ge(sem("spv_used"), BD)
            for g in range(2):
                E.step(V.tensor_copy(AT[GP[g], :, SEQ:NTOK],
                                     PS[GP[g], 7, 0:64].rearrange("p (b h) -> p h b", h=8)[:, 4 * g:4 * g + 4, :]))
            E.meet()

            dve.wait_ge(sem("vec_ev"), 1)
            lm = vec[:, :, 39]
            E.step(ts(lam[:, 2, :], lm, -1.0, None, ALU.mult))
            E.step(tt(lam[:, 0, :], lam[:, 2, :], lm, ALU.max), sem("lam_step"))
            E.step(ts(lam[:, 2, :], lam[:, 2, :], 0.0, None, ALU.max))
            dve.wait_ge(sem("lam_exp"), 1)
            E.step(ts(lam[:, 5, :], lam[:, 1, :], 2.0, None, ALU.add))
            E.step(V.reciprocal(lam[:, 5, :], lam[:, 5, :]))
            E.step(tt(lam[:, 5, :], lam[:, 5, :], lam[:, 1, :], ALU.mult))
            E.step(tt(lam[:, 6, :], lam[:, 5, :], lam[:, 5, :], ALU.mult))
            E.step(V.memset(lam[:, 7, :], 1.0 / 17))
            for k in range(15, 0, -2):
                E.step(tt(lam[:, 7, :], lam[:, 7, :], lam[:, 6, :], ALU.mult))
                E.step(ts(lam[:, 7, :], lam[:, 7, :], 1.0 / k, None, ALU.add))
            E.step(tt(lam[:, 7, :], lam[:, 7, :], lam[:, 5, :], ALU.mult))
            E.step(stt(lam[:, 7, :], lam[:, 7, :], 2.0, lam[:, 2, :], ALU.mult, ALU.add))
            E.step(ts(lam[:, 3, :], lam[:, 7, :], -8.0, None, ALU.mult))
            E.step(ts(lam[:, 4, :], lam[:, 7, :], 8.0, None, ALU.mult), sem("lam_step"))
            E.step(V.memset(ucb[:, 0:3], 0.0))
            for n in range(KT):
                E.step(V.tensor_copy(ucs[:, :, 0:3], vec[:, n, 0:24].rearrange("p (b r) -> p b r", b=BD)))
                dve.wait_ge(sem("u_ev"), n + 1)
                if n:
                    dve.wait_ge(sem("i_mm"), n)
                cw = lambda k: vec[:, n, 32 + k:33 + k]
                E.do(ts(xc[:, 0:SEQ], ucb[:, 0:SEQ], cw(0), vec[:, n, 36:37], ALU.mult, ALU.add))
                E.step(ts(xc[:, SEQ:NTOK], ucs[:, :, 0], cw(0), vec[:, n, 36:37], ALU.mult, ALU.add))
                for k in range(1, 4):
                    E.do(stt(xc[:, 0:SEQ], ucb[:, k:k + SEQ], cw(k), xc[:, 0:SEQ], ALU.mult, ALU.add))
                    E.step(stt(xc[:, SEQ:NTOK], ucs[:, :, k], cw(k), xc[:, SEQ:NTOK], ALU.mult, ALU.add))
                if n:
                    dve.wait_ge(sem("stg_T"), n)
                E.do(V.tensor_copy(stg[:, 0:3], ucb[:, 1024:1027]))
                E.step(V.tensor_copy(stg[:, 3:11], ucs[:, :, 3]), sem("xc_done"))
                dve.wait_ge(sem("a_done"), n + 1)
                E.step(ts(vv, th, 1.0, None, ALU.add))
                E.step(V.reciprocal(vv, vv))
                E.step(stt(vv, th, 2.0, vv, ALU.mult, ALU.mult), sem("v_done"))
                E.step(tt(ii, ii, xc, ALU.mult))
                dve.wait_ge(sem("sq_done"), n + 1)
                E.step(tt(ii, ii, vv, ALU.mult))
                E.do(V.tensor_tensor_scan(hs[:, 0:SEQ], aa[:, 0:SEQ], ii[:, 0:SEQ], 0.0, ALU.mult, ALU.add))
                E.step(tt(hs[:, SEQ:NTOK], aa[:, SEQ:NTOK], vec[:, n, 24:32], ALU.mult))
                E.step(tt(hs[:, SEQ:NTOK], hs[:, SEQ:NTOK], ii[:, SEQ:NTOK], ALU.add))
                E.do(V.tensor_copy(stg[:, 11:20], hs[:, SEQ - 1:NTOK]))
                E.step(tt(RT[:, n, :], hs, gg[:, n % 2, :], ALU.mult), sem("stg_done"))
            E.meet()
            for n in range(KT):
                for h in range(2):
                    dve.wait_ge(w_used, 2 * KT + 4 * n + 2 * h + 2)
                    dve.wait_ge(sem("sg_done"), 2 * n + h + 1)
                    dst = m1 if h == 0 else sg[:, 1, :]
                    if h == 0:
                        E.step(tt(m1.rearrange("p (a b) -> p a b", a=3), PS[:, 3:6, 0:CH], sg[:, 0, :].rearrange("p (a b) -> p a b", a=3), ALU.mult), sem("mg_done"))
                    else:
                        E.step(tt(mT[:, n, :].rearrange("p (a b) -> p a b", a=3), PS[:, 3:6, 0:CH], sg[:, 1, :].rearrange("p (a b) -> p a b", a=3), ALU.mult))
                        E.step(tt(mT[:, n, :], mT[:, n, :], m1, ALU.add), sem("mg_done"))
            E.meet()

            def norm(y, out, n, t, gb, out_sem):
                s = st[0:n, t % 2, :]
                E.do(V.bn_stats(s[:, 0:6], y[:, 0:512]))
                E.step(V.bn_stats(s[:, 6:12], y[:, 512:1024]))
                E.step(V.bn_aggr(s[:, 12:14], s[:, 0:12]))
                E.step(ts(s[:, 13:14], s[:, 13:14], EPS, None, ALU.add), sem("var_done"))
                dve.wait_ge(sem("std_done"), t + 1 + (NT if gb else 0))
                E.step(V.reciprocal(s[:, 15:16], s[:, 14:15]))
                E.step(ts(y, y, s[:, 12:13], s[:, 15:16], ALU.subtract, ALU.mult))
                E.step(tt(y, y, lnw[0:n, gb, :], ALU.mult))
                E.step(tt(out, y, lnw[0:n, gb + 1, :], ALU.add), out_sem)

            dve.wait_ge(sem("ln_in"), 64)
            for t in range(NT):
                n = rows_of(t)
                dve.wait_ge(sem("mix_mm"), t + 1)
                dve.wait_ge(s_xin[t % 2], 16 * (3 + t // 2 + 1))
                y = yy[0:n, t % 2, :]
                E.step(stt(y.rearrange("p (a b) -> p a b", a=2), xr[0:n, t % 2, :].rearrange("p (a b) -> p a b", a=2), ALPHA,
                           PS[0:n, 2 * (t % 2):2 * (t % 2) + 2, :], ALU.mult, ALU.add), sem("xr_used"))
                norm(y, x1tok[0:n, t, :], n, t, 0, sem("x1_done"))
            E.meet()

            dve.wait_ge(sem("wrt_in"), 32)
            for t in range(NT):
                n = rows_of(t)
                dve.wait_ge(sem("lg_ev"), t + 1)
                E.step(tt(selv[0:n, :], sc[0:n, t, :], rb[0:n, :], ALU.add))
                E.step(V.max(sel8[0:n, :], selv[0:n, :]))
                E.step(V.max_index(i8[0:n, :], sel8[0:n, :], selv[0:n, :]))
                E.step(V.tensor_copy(idxf[0:n, t, :], i8[0:n, :]))
                for k in range(TOPK):
                    E.do(ts(oh[0:n, k, :], const("exp", n), idxf[0:n, t, k:k + 1], None, ALU.is_equal))
                E.settle()
                E.do(V.tensor_reduce(Mm[0:n, t, :], oh[0:n, :, :].rearrange("p k e -> p e k"), AX, ALU.add))
                E.step(tt(tmp6[0:n, :, :], oh[0:n, :, :], sc[0:n, t:t + 1, :].broadcast_to([n, TOPK, NE]), ALU.mult))
                E.step(V.tensor_reduce(wfin[0:n, t, :], tmp6[0:n, :, :], AX, ALU.add))
                E.step(V.tensor_reduce(wk[0:n, 0:1], wfin[0:n, t, :], AX, ALU.add))
                E.step(V.reciprocal(wk[0:n, 1:2], wk[0:n, 0:1]))
                E.step(ts(wfin[0:n, t, :], wfin[0:n, t, :], wk[0:n, 1:2], ROUTED_SCALE, ALU.mult, ALU.mult), sem("M_done"))
            for hb in range(2):
                dve.wait_ge(sem("sh_mm"), 2 * hb + 2)
                dve.wait_ge(sem("sil_done"), hb + 1)
                E.step(tt(shT[:, hb, :].rearrange("p (a b) -> p a b", a=3), PS[:, 3:6, 0:CH], sil.rearrange("p (a b) -> p a b", a=3), ALU.mult), sem("shT_done"))
            dve.wait_ge(sem("table_mm"), 1)
            E.step(V.tensor_copy(pos, PS[:, 6, 0:NE]))
            E.step(ts(nbl, pos, 0.5, None, ALU.is_gt))
            for k in range(1, 9):
                E.step(stt(nbl, pos, 128.0 * k + 0.5, nbl, ALU.is_gt, ALU.add))
            E.step(V.tensor_tensor_scan(cs, const("ones")[:, 0:NE], nbl, 0.0, ALU.mult, ALU.add))
            E.step(tt(base, cs, nbl, ALU.subtract))
            E.step(ts(base, base, 128.0, None, ALU.mult))
            E.step(ts(ridx[:, 0:NE], cs, const("row"), None, ALU.is_le))
            E.step(V.tensor_reduce(wk[:, 2:3], ridx[:, 0:NE], AX, ALU.add))
            E.step(ts(ridx[:, 0:1], wk[:, 2:3], float(NE - 1), None, ALU.min), sem("table_step"))
            E.step(ts(wk[0:1, 3:4], cs[0:1, NE - 1:NE], 0.5, None, ALU.mult))
            E.step(ts(ridx[0:1, 1:NE + 0], const("exp", 1)[:, 0:NE - 1], wk[0:1, 3:4], None, ALU.is_lt))
            E.step(V.tensor_reduce(wk[0:1, 4:5], ridx[0:1, 1:NE], AX, ALU.add))
            E.step(V.tensor_copy(nblk[0:1, 0:1], wk[0:1, 4:5]))
            dve.wait_ge(sem("x1_out"), 32)
            for t in range(NT):
                n = rows_of(t)
                dve.wait_ge(sem("shd_mm"), t + 1)
                x2 = x1tok[0:n, t, :].rearrange("p (a b) -> p a b", a=2)
                E.do(stt(x2, x2, ALPHA, PS[0:n, 2 * (t % 2):2 * (t % 2) + 2, :], ALU.mult, ALU.add), sem("acc_done"))
                dve.wait_ge(sem("rk_mm"), t + 1)
                E.step(tt(pos[0:n, :], PS[0:n, 4 + t % 2, 0:NE], base[0:n, :], ALU.add))
                for k in range(TOPK):
                    E.do(ts(oh[0:n, k, :], const("exp", n), idxf[0:n, t, k:k + 1], None, ALU.is_equal))
                E.settle()
                E.step(tt(tmp6[0:n, :, :], oh[0:n, :, :], pos[0:n, :].unsqueeze(1).broadcast_to([n, TOPK, NE]), ALU.mult))
                E.step(V.tensor_reduce(dstf[0:n, t, :], tmp6[0:n, :, :], AX, ALU.add))
                E.step(V.tensor_copy(dsti[0:n, t, :], dstf[0:n, t, :]), sem("dst_done"))
            dve.wait_ge(sem("table_mm"), 2)
            E.step(V.tensor_copy(blke[0:1, :], PS[0:1, 7, 0:P]))
            dve.wait_ge(sem("tab_in"), 16)
            E.step(V.tensor_copy(trow[0:NBLK, :], ztab[:, :]), sem("table_step"))
            dve.wait_ge(sem("table_mm"), 3)
            E.step(V.tensor_copy(idxall[:, 0:NBLK], PS[:, 7, 128:128 + NBLK]), sem("table_step"))
            for name in ("gu_free0", "gu_free1", "y_ev2"):
                dve.nop().then_inc(sem(name), 1)
            E.meet()
            turns = dve.value_load(nblk[0:1, 0:1], min_val=1, max_val=NBLK // 2)
            with dve.Fori(0, NBLK // 2) as i:
                with dve.If(i < turns):
                    for s in range(2):
                        dve.wait_ge(sem("sl_done"), 2 * i + s + 1)
                        tt(hh_[:, s, :], PS[:, 2 + s, DE:2 * DE], hsl[:, s, :], ALU.mult).then_inc(sem(f"gu_free{s}"), 1)
                    for s in range(2):
                        dve.wait_ge(sem("y_mm"), 2 * i + s + 3)
                        dve.wait_ge(sem(f"yd{s}"), 16 * i + 1)
                        V.tensor_copy(ysb[:, s, 0:512], PS[:, 5, :]).then_inc(sem("y_ev2"), 1)
            dve.wait_ge(sem("y_all"), 1)
            c = 0
            for t in range(NT):
                n = rows_of(t)
                acc = x1tok[0:n, t, :]
                for k in range(TOPK):
                    dve.wait_ge(sem(f"yg{c % 6}"), 16 * (c // 6 + 1))
                    E.step(stt(acc, yg[0:n, c % 6, :], wfin[0:n, t, k:k + 1], acc, ALU.mult, ALU.add), sem("yg_used"))
                    c += 1
                if t >= 2:
                    dve.wait_ge(sem(f"y_out{t % 2}"), 16 * (t // 2))
                norm(acc, fin[0:n, t % 2, :], n, t, 2, sem("fin_done"))

        @block.gpsimd
        def _(pool):
            for m in met:
                pool.wait_ge(m, 1)
            G = nc.gpsimd
            G.memset(W1.rearrange("p a b c -> p (a b c)"), 0.0)
            G.memset(zrow, 0.0)
            G.memset(W2.rearrange("p a b -> p (a b)"), 0.0).then_inc(w1_zero, 1)
            for m in met:
                pool.wait_ge(m, 3)
            pool.dma_start(gsel[0:64, 0:3], gate[0:BD, 8, :].rearrange("b (h c) -> b h c", c=3)).then_inc(sem("gsel_in"), 16)
            pool.wait_ge(sem("tab_zero"), 16)
            for t in range(NT):
                n = rows_of(t)
                pool.wait_ge(sem("dst_done"), t + 1)
                for k in range(TOPK):
                    G.indirect_dma_start(out=tab_dram, out_offset=bass.IndirectOffsetOnAxis(ap=dsti[0:n, t, k:k + 1], axis=0),
                                         in_=tokid[0:n, t:t + 1], in_offset=None).then_inc(sem("tab_full"), 16)
            pool.wait_ge(sem("table_step"), 3)
            pool.wait_ge(sem("x1_out"), 32)
            for m in met:
                pool.wait_ge(m, 8)
            turns = pool.value_load(nblk[0:1, 0:1], min_val=1, max_val=NBLK // 2)
            with pool.Fori(0, NBLK // 2) as i:
                with pool.If(i < turns):
                    for s in range(2):
                        pool.wait_ge(sem("xgT_mm1"), i * 2 + s + 1)
                        G.tensor_tensor(pause[:, 0:1], izero[:, 0:1], izero[:, 0:1], ALU.add)
                        G.tensor_tensor(idxs[:, s:s + 1], idxall[:, bass.ds(i * 2 + s, 1)], izero[:, 0:1], ALU.add).then_inc(sem(f"ix{s}"), 1)
                        pool.wait_ge(sem(f"ix{s}"), i + 1)
                        G.tensor_tensor(pause[:, 1:2], izero[:, 0:1], izero[:, 0:1], ALU.add)
                        G.indirect_dma_start(out=xg[:, s, :], out_offset=None, in_=x1_dram,
                                             in_offset=bass.IndirectOffsetOnAxis(ap=idxs[:, s:s + 1], axis=0)).then_inc(sem(f"xg{s}"), 16)
            pool.wait_ge(sem("y_all"), 1)
            c = 0
            yrows = y_dram.rearrange("b p d -> (b p) d")
            for t in range(NT):
                n = rows_of(t)
                for k in range(TOPK):
                    if c >= 6:
                        pool.wait_ge(sem("yg_used"), c - 5)
                    G.indirect_dma_start(out=yg[0:n, c % 6, :], out_offset=None, in_=yrows,
                                         in_offset=bass.IndirectOffsetOnAxis(ap=dsti[0:n, t, k:k + 1], axis=0)).then_inc(sem(f"yg{c % 6}"), 16)
                    c += 1


_OUTS = [("y_p", (SEQ, D), (1, SEQ, D)), ("y_s", (BD, D), (BD, 1, D)),
         ("cmp_p", (SEQ, KV), (1, 1, SEQ, 2, 2, HD)), ("cmp_s", (BD, KV), (1, BD, 1, 2, 2, HD)),
         ("sel_p", (SEQ, KV), (1, 1, SEQ, 2, 2, HD)), ("sel_s", (BD, KV), (1, BD, 1, 2, 2, HD)),
         ("win_p", (WINDOW, KV), (1, 1, WINDOW, 2, 2, HD)), ("win_s", (BD, WINDOW, KV), (1, BD, WINDOW, 2, 2, HD)),
         ("conv_p", (3, D), (1, 1, 3, D)), ("conv_s", (BD, 3, D), (1, BD, 3, D)),
         ("rnn_p", (1, D), (1, 1, D)), ("rnn_s", (BD, D), (1, BD, D))]


def kernel(**inputs):
    import numpy as _np
    import concourse.bacc as _bacc
    from concourse import mybir as _mybir
    from concourse.bass_utils import run_bass_kernel_spmd as _run

    v = {k: _np.asarray(x) for k, x in inputs.items()}
    shaped = {
        "x_prompt": v["x_prompt"].reshape(SEQ, D), "x_sample": v["x_sample"].reshape(BD, D),
        "cmp": v["cache_cmp_kv"].reshape(NPOOL, PAGE, KV), "sel": v["cache_sel_kv"].reshape(NPOOL, PAGE, KV),
        "win": v["cache_win_kv"].reshape(BD, WINDOW, KV), "state_conv": v["state_conv"].reshape(BD, 3, D),
        "state_rnn": v["state_rnn"].reshape(BD, D), "page_table": v["page_table"],
        "w1k": v["w_cmp_k1"].reshape(32, HD, HD), "w1v": v["w_cmp_v1"].reshape(32, HD, HD),
        "w2k": v["w_cmp_k2"].reshape(HD, HD), "w2v": v["w_cmp_v2"].reshape(HD, HD),
        "posk": v["cmp_pos_k"].reshape(32, HD), "posv": v["cmp_pos_v"].reshape(32, HD),
        "consts": CONSTS,
    }
    for name in ("w_in", "conv_w", "w_rg_a", "w_rg_i", "w_branch_attn", "w_branch_rnn", "w_out", "w_router",
                 "w_exp_gate", "w_exp_up", "w_exp_down", "w_sh_gate", "w_sh_up", "w_sh_down"):
        shaped[name] = v[name][0]
    for name in ("conv_b", "b_rg_a", "b_rg_i", "lru_lambda", "ln1_g", "ln1_b", "router_bias", "ln2_g", "ln2_b"):
        shaped[name] = v[name].reshape(1, -1)
    nc = _bacc.Bacc("TRN2", target_bir_lowering=False, num_devices=1)
    arrays, a, o = {}, {}, {}
    for name, x in shaped.items():
        x = _np.ascontiguousarray(x)
        arrays[f"in_{name}"] = x
        a[name] = nc.dram_tensor(f"in_{name}", x.shape, _mybir.dt.from_np(x.dtype), kind="ExternalInput").ap()
    for name, shape, _ in _OUTS:
        o[name] = nc.dram_tensor(f"out_{name}", shape, _mybir.dt.float32, kind="ExternalOutput").ap()
    x1_dram = nc.dram_tensor("x1_rows", (NTOK, D), _mybir.dt.float32, kind="Internal").ap()
    tab_dram = nc.dram_tensor("row_table", (NBLK * P, 1), _mybir.dt.int32, kind="Internal").ap()
    y_dram = nc.dram_tensor("expert_rows", (NBLK, P, D), _mybir.dt.float32, kind="Internal").ap()
    build(nc, a, o, x1_dram, tab_dram, y_dram)
    r = _run(nc, [arrays], core_ids=[0])
    return tuple(r.results[0][f"out_{name}"].reshape(final) for name, _, final in _OUTS)
```

```python
from contextlib import ExitStack

import numpy as np

import concourse.bass as bass
from concourse import mybir

F32 = mybir.dt.float32
I32 = mybir.dt.int32
U32 = mybir.dt.uint32
ALU = mybir.AluOpType
ACT = mybir.ActivationFunctionType
AX = mybir.AxisListType.X

P = 128
D = 1024
KT = D // P
SEQ = 1024
BD = 8
NTOK = SEQ + BD
NT = SEQ // P + 1
PAST = 2048
PAGE = 128
NPG = PAST // PAGE
NPOOL = 160
HD = 64
NH = 8
KV = 2 * 2 * HD
QW = NH * HD
TOKW = QW + 3 * KV + 3 * NH
C_U = TOKW
C_G = C_U + D
C_A = C_G + D
C_B = C_A + D
CH = NTOK // 3
WINDOW = 512
NE = 64
TOPK = 6
DE = 256
USED = NTOK * TOPK // P
NBLK = 112
SCALE = HD ** -0.5
ALPHA = 2.0 ** 0.25
EPS = 1e-5
NEG = -1e30
ROUTED_SCALE = 2.5


def constants():
    p = np.arange(P, dtype=np.float64)[:, None]
    c = np.arange(P, dtype=np.float64)[None, :]
    parts = {}
    parts["ident"] = (p == c) * 1.0
    parts["diag"] = np.where(c <= p, 0.0, NEG)
    parts["edge"] = np.where(c >= p, 0.0, NEG)
    end = 16.0 * np.arange(63)[None, None, :] + 31
    parts["cmpm"] = np.where(end <= p[:, :, None] + 128.0 * np.arange(8)[None, :, None], 0.0, NEG).reshape(P, 504)
    inv = np.float32(500000.0) ** (-(np.arange(8, dtype=np.float32) * np.float32(2.0 / 16)))
    pos = np.full((P, NT), float(PAST), np.float32)
    pos[:, :8] = (np.arange(8)[None, :] * P + np.arange(P)[:, None])
    ang = pos[:, :, None] * inv.astype(np.float32)[None, None, :]
    parts["cos"] = np.cos(ang.astype(np.float32)).reshape(P, NT * 8)
    parts["sin"] = np.sin(ang.astype(np.float32)).reshape(P, NT * 8)
    parts["before"] = (p < c) * 1.0
    parts["ones"] = np.ones((P, P))
    parts["group"] = ((p // 4) == (np.arange(64)[None, :] // 4)) * 1.0
    parts["own"] = ((p // 8) == np.arange(8)[None, :]) * 1.0
    s = np.arange(33)
    parts["lower"] = np.broadcast_to((s[None, :] < s[:, None]).reshape(1, 33 * 33), (P, 33 * 33)) * 1.0
    parts["force"] = np.broadcast_to(np.where((s == 0) | (s >= 31), 1e6, 0.0)[None, :], (P, 33))
    parts["free"] = np.broadcast_to(np.where((s == 0) | (s >= 31), 0.0, 1.0)[None, :], (P, 33))
    parts["tokid"] = p + 128.0 * np.arange(NT)[None, :]
    parts["exp"] = np.broadcast_to(np.arange(64.0)[None, :], (P, 64))
    parts["row"] = p
    parts["eighth"] = p % 8
    parts["blk"] = np.broadcast_to(np.arange(128.0)[None, :], (P, 128))
    where, at = {}, 0
    for k, v in parts.items():
        where[k] = (at, v.shape[1])
        at += v.shape[1]
    return np.ascontiguousarray(np.concatenate([np.asarray(v, np.float32) for v in parts.values()], 1)), where


CONSTS, CWHERE = constants()
NCONST = CONSTS.shape[1]


class Engine:

    def __init__(self, eng, chain, met, others):
        self.eng, self.chain, self.met, self.others = eng, chain, met, others
        self.count, self.last, self.meets = {}, None, 0

    def do(self, ins, sem=None):
        sem = self.chain if sem is None else sem
        ins.then_inc(sem, 1)
        self.count[sem.name] = self.count.get(sem.name, 0) + 1
        self.last = (sem, self.count[sem.name])

    def settle(self):
        if self.last:
            self.eng.wait_ge(*self.last)

    def step(self, ins, sem=None):
        self.do(ins, sem)
        self.settle()

    def meet(self):
        self.settle()
        self.eng.nop().then_inc(self.met, 1)
        self.meets += 1
        for o in self.others:
            self.eng.wait_ge(o, self.meets)


def attention_plan():
    units, n = [], 0
    for i in range(8):
        for j in range(4):
            for g in range(2):
                for kind in "sw":
                    if kind == "s":
                        t0 = 0
                        groups = [[("s", t, t * P) for t in range(a, min(a + 4, i + 1))] for a in range(0, i + 1, 4)]
                    else:
                        t0 = max(0, i - 4)
                        tiles = [("w", t, (t - t0) * P) for t in range(t0, i + 1)] + [("c", 0, 640)]
                        groups = [tiles[a:a + 4] for a in range(0, len(tiles), 4)]
                    units.append(dict(i=i, j=j, g=g, kind=kind, t0=t0, groups=groups, first=n))
                    n += len(groups)
    return units


UNITS = attention_plan()
NU = len(UNITS)


def build(nc, a, o, x1_dram, y_dram):
    ctx = ExitStack()
    with ctx:
        arena = ctx.enter_context(nc.sbuf_tensor("arena", [P, 52736], F32))
        PS = ctx.enter_context(nc.psum_tensor("PS", [P, 8, 512], F32))
        names = {}

        def sem(name):
            if name not in names:
                names[name] = ctx.enter_context(nc.semaphore(name))
            return names[name]

        def isb(name, shape, dt=I32):
            return ctx.enter_context(nc.sbuf_tensor(name, shape, dt))

        def at(off, *shape):
            n = int(np.prod(shape))
            assert off + n <= 52736, (off, shape)
            v = arena[:, off:off + n]
            if len(shape) == 2:
                v = v.rearrange("p (a b) -> p a b", a=shape[0])
            elif len(shape) == 3:
                v = v.rearrange("p (a b c) -> p a b c", a=shape[0], b=shape[1])
            return v

        def const(name, n=P):
            w, k = CWHERE[name]
            return arena[0:n, w:w + k]
        assert NCONST <= 3600
        ident = arena[:, 0:P]
        gate = at(3600, NT, 24)
        negb = at(3820, 2, 2)
        sums = at(3824, 2, 3)
        coef = at(3830, 2, 3)
        mx = at(3836, 4)
        posT = at(3840, 2, 32)
        cbias = at(3904, 2)
        wfin = at(3910, NT, TOPK)
        xT = at(4000, KT, NTOK)
        AT = at(12256, 4, NTOK)
        wtm = at(12256, KT, TOKW)
        TMP = 16384
        W1 = at(22688, 2, 32, P)
        W2 = at(30880, 2, P)
        assert 12256 + KT * TOKW <= 22688
        kvT = at(31136, 4, NTOK)
        kvraw = at(35264, NT, 3 * KV)
        qT = at(42176, 4, NTOK)
        qrT = at(46304, 4, NTOK)

        def kvtok(t):
            return kvraw[:, (t + 1) % NT, :]

        xin = at(22688, 8, D)
        qtok = at(50432, 2, QW)
        qrtok = at(51456, 2, QW)
        rt = at(52480, 4, 64)
        Pb = at(TMP, 3, D)
        PTs = at(50432, 3, 512)
        gh = at(TMP + 4096, 2, 127)
        kcp = at(TMP + 4352, 63)
        vcp = at(TMP + 4416, P)
        zrow = at(TMP + 4832, D)
        possb = at(TMP + 4544, 4 * HD)
        DB = 35264 + 768
        wKV = at(DB, BD, 4, KV)
        cpg = at(DB, 2, 16 * KV)
        kvTb = at(DB + 8192, 2, PAST)
        rank = at(DB + 12288, 2, 33 * 33)
        qz = at(51712, 2, BD, 64)
        assert DB + 12288 + 2178 <= 51712
        hold = at(22688, 6, 16, P)
        assert 22688 + 12288 <= 35264
        kcs = at(TMP, BD, 127)
        vcs = at(TMP + 1016, BD, P)
        SS = at(TMP + 2040, 2052)
        PTb = at(TMP + 4092, NPG, 64)
        pself = at(TMP + 5116, 3, 64)
        sm_self = at(TMP + 5308, 64)
        ghs = at(TMP + 5372, 2, 127)
        sm = at(TMP + 5626, 7, 36)
        gsel = at(TMP + 5878, 4)
        selmask = at(TMP + 5882, 36)
        zc = at(TMP + 5918, 132)
        Pc = at(TMP + 6050, 127)
        assert TMP + 6177 <= 22688
        ring = at(16384, 6, KT, P)
        EB = 16384 + 6144
        RT = at(EB, KT, NTOK)
        mT = at(EB + 8256, KT, NTOK)
        E0 = EB + 8256
        ucb = at(E0, 1028)
        ucs = at(E0 + 1028, BD, 4)
        xc = at(E0 + 1060, NTOK)
        gg = at(E0 + 2092, 2, NTOK)
        rr, aa, th, ii, vv, hs = (at(E0 + 4156 + k * NTOK, NTOK) for k in range(6))
        vec = at(E0 + 10348, KT, 40)
        vrows = at(E0 + 10668, D)
        orows = at(E0 + 11692, D)
        wra = at(E0 + 12716, KT, P)
        wri = at(E0 + 13740, KT, P)
        stg = at(E0 + 14764, 20)
        lam = at(E0 + 14784, 8, KT)
        assert E0 + 14848 <= 52400
        sg = at(E0 + 8256, 2, NTOK)
        m1 = at(E0 + 8256 + 2064, NTOK)
        x1T = at(4000, KT, NTOK)
        x1tok = at(12256, NT, D)
        xr = at(21472, 2, D)
        yy = at(23520, 2, D)
        lnw = at(25568, 4, D)
        st = at(29664, 2, 16)
        wout = at(42400, KT, D)
        assert E0 == 30784 and E0 + 8256 + 3 * NTOK <= 42400
        wrt = at(29760, KT, NE)
        wsg = at(39040, KT, DE)
        wsu = at(50592, KT, DE)
        wsd = at(42400, 2, D)
        HB = 44448
        shT = at(47300, 2, NTOK)
        sil = at(49364, NTOK)
        sc = at(HB, NT, NE)
        Mm = at(HB + 576, NT, NE)
        idxf = at(HB + 1152, NT, 8)
        oh = at(HB + 1224, TOPK, NE)
        sel8 = at(HB + 1608, 8)
        rb = at(HB + 1616, NE)
        selv = at(HB + 1680, NE)
        dstf = at(HB + 1744, NT, TOPK)
        cs = at(HB + 1800, NE)
        nbl = at(HB + 1864, NE)
        base = at(HB + 1928, NE)
        pos = at(HB + 1992, NE)
        tmp6 = at(HB + 2056, TOPK, NE)
        wk = at(HB + 2440, 8)
        ridx = at(HB + 2448, NE)
        blkf = at(HB + 2512, 2, 8)
        at_row = at(30784, 2, TOPK, P)
        at_blk = at(30784 + 1536, 2, TOPK, P)
        wexg = at(30784, 2, KT, DE)
        wexu = at(34880, 2, KT, DE)
        wexd = at(38976, 2, 2, D)
        xg = at(43072, 2, D)
        xgT = at(45120, 2, KT, P)
        hsl = at(47168, 2, DE)
        hh_ = at(47680, 2, DE)
        hT = at(48192, 2, 2, P)
        ysb = at(48704, 2, D)
        yg = at(4000, 6, D)
        fin = at(10144, 2, D)

        pgidx = isb("pgidx", [P, BD])
        i8 = isb("i8", [P, 8], U32)
        dsti = isb("dsti", [P, NT, TOPK])
        rowb = isb("rowb", [P, 2, 8])
        idxall = isb("idxall", [P, P])
        idxs = isb("idxs", [P, 2])
        izero = isb("izero", [P, 1])
        pause = isb("pause", [P, 2])
        blke = isb("blke", [1, P])
        nblk = isb("nblk", [1, 4])

        met = [sem("pe_met"), sem("act_met"), sem("dve_met")]

        s_const = sem("const_in")
        s_x = [sem(f"x_in{k}") for k in range(8)]
        s_xin = [sem("xr_in0"), sem("xr_in1")]
        s_wtm = sem("wtm_in")
        x_turned = sem("x_turned")
        xT_ready = sem("xT_ready")
        tok_mm = sem("tok_mm")
        tok_ev = sem("tok_ev")
        rope_done = sem("rope_done")
        tok_turned = sem("tok_turned")
        tokT_ready = sem("tokT_ready")
        out_done = sem("out_done")
        w1_zero = sem("w1_zero")
        s_w1 = sem("w1_in")
        cmp_mm = sem("cmp_mm")
        cmp_ev = sem("cmp_ev")
        qk_done = sem("qk_done")
        mx_done = sem("mx_done")
        exp_done = sem("exp_done")
        coef_done = sem("coef_done")
        scale_done = sem("scale_done")
        pt_done = sem("pt_done")
        pt_ev = [sem("pt_ev0"), sem("pt_ev1")]
        pv_done = sem("pv_done")
        o_ev = sem("o_ev")
        for name in ("gu_mm", "gu_free", "wex", "wexd", "xg", "xgT_mm", "xgT_ev", "yd", "ix", "pg"):
            sem(name + "0"), sem(name + "1")
        for name in ("y_zero", "y_mm", "y_ev", "y_ev2", "hT_mm", "hT_ev", "sl_done"):
            sem(name)

        block = ctx.enter_context(nc.Block())
        G_CMP = BD + 2
        G_SEL = G_CMP + 8 * BD + 1
        GP = [slice(0, 64), slice(64, 128)]

        def rows_of(t):
            return P if t < NT - 1 else BD

        stream = []
        for n in range(KT):
            stream += [("in", C_U + n * P), ("in", C_G + n * P)]
        for n in range(KT):
            stream += [("in", C_A + n * P), ("wa", n * P), ("in", C_B + n * P), ("wb", n * P)]
        RING = 6
        due, filled = [], [0] * RING
        for b, (kind, _) in enumerate(stream):
            filled[b % RING] += 32 if kind == "wa" else 16
            due.append(filled[b % RING])
        s_ring = [sem(f"ring{k}") for k in range(RING)]
        w_used = sem("w_used")

        @block.sync
        def _(sp):
            sp.dma_start(arena[:, 0:NCONST], a["consts"]).then_inc(s_const, 16)
            for r in range(8):
                sp.dma_start(pgidx[r::8, :], a["page_table"].rearrange("b j -> j b"), allow_slow_non_contiguous=True).then_inc(sem("ptab_in"), 16)
            for t in range(NT):
                n = rows_of(t)
                if t == 8:
                    sp.wait_ge(x_turned, 2)
                src = a["x_prompt"][t * P:(t + 1) * P, :] if n == P else a["x_sample"]
                sp.dma_start(xin[0:n, t % 8, :], src).then_inc(s_x[t % 8], 16)
                if t == 7:
                    for k in range(KT):
                        sp.dma_start(wtm[:, k, :], a["w_in"][k * P:(k + 1) * P, 0:TOKW]).then_inc(s_wtm, 16)
            sp.wait_ge(w1_zero, 1)
            for kv in range(2):
                for g in range(2):
                    sp.dma_start(W1[GP[g], kv, :, g * 64:g * 64 + 64],
                                 a["w1k" if kv == 0 else "w1v"].rearrange("s d f -> d s f")).then_inc(s_w1, 16)
                    sp.dma_start(W2[GP[g], kv, g * 64:g * 64 + 64], a["w2k" if kv == 0 else "w2v"]).then_inc(s_w1, 16)
            sp.dma_start(o["win_s"][:, 0:WINDOW - 1, :], a["win"][:, 1:WINDOW, :]).then_inc(out_done, 16)
            sp.dma_start(o["conv_s"][:, 0:2, :], a["state_conv"][:, 1:3, :]).then_inc(out_done, 16)
            sp.wait_ge(rope_done, NT)
            sp.dma_start(o["cmp_p"].rearrange("(t p) c -> p t c", p=P), kvraw[:, 1:9, 0:KV]).then_inc(out_done, 16)
            sp.dma_start(o["sel_p"].rearrange("(t p) c -> p t c", p=P), kvraw[:, 1:9, KV:2 * KV]).then_inc(out_done, 16)
            sp.dma_start(o["win_p"].rearrange("(t p) c -> p t c", p=P), kvraw[:, 5:9, 2 * KV:3 * KV]).then_inc(out_done, 16)
            sp.dma_start(o["cmp_s"], kvraw[0:BD, 0, 0:KV]).then_inc(out_done, 16)
            sp.dma_start(o["sel_s"], kvraw[0:BD, 0, KV:2 * KV]).then_inc(out_done, 16)
            sp.dma_start(o["win_s"][:, WINDOW - 1, :], kvraw[0:BD, 0, 2 * KV:3 * KV]).then_inc(out_done, 16)
            for m in met:
                sp.wait_ge(m, 1)
            for k in range(4):
                sp.dma_start(possb[0:32, k * HD:(k + 1) * HD], a["posk" if k < 2 else "posv"]).then_inc(s_w1, 16)
            sp.wait_ge(sem("zrow_set"), 1)
            sp.dma_start(y_dram[USED:NBLK, :, :].rearrange("b p d -> p b d"),
                         zrow.unsqueeze(1).broadcast_to([P, NBLK - USED, D])).then_inc(sem("y_zero"), 16)

            for m in met:
                sp.wait_ge(m, 3)
            sp.wait_ge(out_done, 8 * 16)
            sp.wait_ge(sem("y_zero"), 16)
            for b in range(BD):
                sp.dma_start(wKV[:, b, :, :], a["win"][b].rearrange("(t p) c -> p t c", p=P)).then_inc(sem("win_in"), 16)

            for m in met:
                sp.wait_ge(m, 4)
            sv = sem("vec_in")
            sp.dma_start(vrows[0:24, :], a["state_conv"].rearrange("b r c -> (b r) c")).then_inc(sv, 16)
            sp.dma_start(vrows[24:32, :], a["state_rnn"]).then_inc(sv, 16)
            sp.dma_start(vrows[32:36, :], a["conv_w"]).then_inc(sv, 16)
            for k, nm in enumerate(("conv_b", "b_rg_a", "b_rg_i", "lru_lambda")):
                sp.dma_start(vrows[36 + k:37 + k, :], a[nm]).then_inc(sv, 16)
            sp.dma_start(wra, a["w_rg_a"].rearrange("n c d -> c n d")).then_inc(sv, 16)
            sp.dma_start(wri, a["w_rg_i"].rearrange("n c d -> c n d")).then_inc(sv, 16)
            for b, (kind, c0) in enumerate(stream):
                if b >= RING:
                    sp.wait_ge(w_used, b - RING + 1)
                s = b % RING
                if kind == "wa":
                    for g in range(2):
                        sp.dma_start(ring[GP[g], s, 0:4, :],
                                     a["w_branch_attn"].rearrange("(g j d) n -> g d j n", g=2, j=4)[g, :, :, c0:c0 + P]).then_inc(s_ring[s], 16)
                else:
                    w = a["w_in"] if kind == "in" else a["w_branch_rnn"]
                    sp.dma_start(ring[:, s, :, :], w[:, c0:c0 + P].rearrange("(k p) n -> p k n", p=P)).then_inc(s_ring[s], 16)
                if b == 2 * KT + RING - 1:
                    sp.wait_ge(sem("rows_ready"), 1)
                    sp.dma_start(o["conv_p"], orows[0:3, :]).then_inc(out_done, 16)
                    sp.dma_start(o["conv_s"][:, 2, :], orows[3:11, :]).then_inc(out_done, 16)
                    sp.dma_start(o["rnn_p"], orows[11:12, :]).then_inc(out_done, 16)
                    sp.dma_start(o["rnn_s"], orows[12:20, :]).then_inc(out_done, 16)
                    sp.wait_ge(out_done, 12 * 16)
                if b == 2 * KT + RING + 2:
                    for m in met:
                        sp.wait_ge(m, 5)
                    sp.dma_start(wout, a["w_out"].rearrange("(k p) n -> p k n", p=P)).then_inc(sem("wout_in"), 16)

            for m in met:
                sp.wait_ge(m, 6)
            for k, nm in enumerate(("ln1_g", "ln1_b", "ln2_g", "ln2_b")):
                sp.dma_start(lnw[:, k, :], a[nm].broadcast_to([P, D])).then_inc(sem("ln_in"), 16)
            for t in range(NT):
                n = rows_of(t)
                if t >= 2:
                    sp.wait_ge(sem("xr_used"), t - 1)
                src = a["x_prompt"][t * P:(t + 1) * P, :] if n == P else a["x_sample"]
                sp.dma_start(xr[0:n, t % 2, :], src).then_inc(s_xin[t % 2], 16)
            sp.dma_start(wrt, a["w_router"].rearrange("(k p) n -> p k n", p=P)).then_inc(sem("wrt_in"), 16)
            sp.dma_start(wsg, a["w_sh_gate"].rearrange("(k p) n -> p k n", p=P)).then_inc(sem("wsh_in"), 16)
            sp.dma_start(wsu, a["w_sh_up"].rearrange("(k p) n -> p k n", p=P)).then_inc(sem("wsh_in"), 16)
            sp.wait_ge(sem("x1_done"), NT)
            sp.dma_start(x1_dram[0:SEQ, :].rearrange("(t p) d -> p t d", p=P), x1tok[:, 0:8, :]).then_inc(sem("x1_out"), 16)
            sp.dma_start(x1_dram[SEQ:NTOK, :], x1tok[0:BD, 8, :]).then_inc(sem("x1_out"), 16)
            for m in met:
                sp.wait_ge(m, 7)
            sp.dma_start(rb, a["router_bias"].broadcast_to([P, NE])).then_inc(sem("wrt_in"), 16)
            sp.dma_start(wsd, a["w_sh_down"].rearrange("(k p) n -> p k n", p=P)).then_inc(sem("wsh_in"), 16)
            for m in met:
                sp.wait_ge(m, 8)
            turns = sp.value_load(nblk[0:1, 0:1], min_val=1, max_val=NBLK // 2)
            with sp.Fori(0, NBLK // 2) as i:
                with sp.If(i < turns):
                    experts = [sp.value_load(blke[0:1, bass.ds(i * 2 + s, 1)], min_val=0, max_val=NE - 1) for s in range(2)]
                    for s, e in enumerate(experts):
                        sp.wait_ge(sem(f"gu_mm{s}"), i + 1)
                        for w, name in ((wexg, "w_exp_gate"), (wexu, "w_exp_up")):
                            sp.dma_start(w[:, s, :, :].rearrange("p k n -> p (k n)"),
                                         a[name][bass.ds(e, 1), :, :].rearrange("u (p k) n -> (u p) (k n)", p=P)).then_inc(sem(f"wex{s}"), 16)
                    for s, e in enumerate(experts):
                        sp.wait_ge(sem("y_mm"), i * 2 + s + 1)
                        sp.dma_start(wexd[:, s, :, :].rearrange("p k n -> p (k n)"),
                                     a["w_exp_down"][bass.ds(e, 1), :, :].rearrange("u (p k) n -> (u p) (k n)", p=P)).then_inc(sem(f"wexd{s}"), 16)
            for t in range(NT):
                n = rows_of(t)
                sp.wait_ge(sem("fin_done"), t + 1)
                dst = o["y_p"][t * P:(t + 1) * P, :] if n == P else o["y_s"]
                sp.dma_start(dst, fin[0:n, t % 2, :]).then_inc(sem(f"y_out{t % 2}"), 16)
            sp.wait_ge(sem("y_out0"), 16 * 5)
            sp.wait_ge(sem("y_out1"), 16 * 4)
            sp.wait_ge(out_done, 12 * 16)

        PTB = (4, 5, 7)

        def take_turned(eng, E, copy, k, odd):
            u = UNITS[k]
            for n, grp in enumerate(u["groups"]):
                gi = u["first"] + n
                if gi % 2 != odd:
                    continue
                eng.wait_ge(pt_done, gi + 1)
                if gi >= 3:
                    eng.wait_ge(pv_done, gi - 2)
                c_last = grp[-1][0] == "c"
                w = len(grp) - c_last
                if w:
                    ins = copy(PTs[:, gi % 3, 0:w * P], PS[:, PTB[gi % 3], 0:w * P])
                    if c_last:
                        E.do(ins)
                if c_last:
                    ins = copy(PTs[0:63, gi % 3, w * P:(w + 1) * P], PS[0:63, PTB[gi % 3], w * P:(w + 1) * P])
                E.do(ins, pt_ev[odd])

        @block.tensor
        def _(pe):
            E = Engine(pe, sem("pe_chain"), met[0], met[1:])
            mm = nc.tensor.matmul

            def turn(out, in_, n):
                return nc.tensor.transpose(out, in_, ident[0:n, 0:n])

            pe.wait_ge(s_const, 16)
            for t in range(NT):
                n = rows_of(t)
                pe.wait_ge(s_x[t % 8], 16 * (t // 8 + 1))
                for hf in range(2):
                    gi = 2 * t + hf
                    if gi >= 4:
                        pe.wait_ge(xT_ready, gi - 3)
                    for k in range(4):
                        ins = turn(PS[:, gi % 4, k * P:k * P + n], xin[0:n, t % 8, (hf * 4 + k) * P:(hf * 4 + k + 1) * P], n)
                    E.do(ins, x_turned)
            pe.wait_ge(s_wtm, 16 * KT)
            pe.wait_ge(xT_ready, 2 * NT)
            COLS = [(0, 512), (512, 1024), (1024, TOKW)]

            def turn_tile(t):
                n = rows_of(t)
                pe.wait_ge(rope_done, t + 1)
                for g3 in range(3):
                    gi = 3 * t + g3
                    if gi >= 2:
                        pe.wait_ge(tokT_ready, gi - 1)
                    for k in range(4):
                        if g3 < 2:
                            src = (qtok, qrtok)[g3][0:n, t % 2, k * P:(k + 1) * P]
                        else:
                            c = (0, 128, 256, 512)[k]
                            src = kvtok(t)[0:n, c:c + P]
                        ins = turn(PS[:, 6 + gi % 2, k * P:k * P + n], src, n)
                    E.do(ins, tok_turned)

            for t in range(NT):
                n = rows_of(t)
                if t >= 2:
                    pe.wait_ge(tok_ev, t - 1)
                for c, (c0, c1) in enumerate(COLS):
                    for k in range(KT):
                        ins = mm(PS[0:n, 3 * (t % 2) + c, 0:c1 - c0], xT[:, k, t * P:t * P + n], wtm[:, k, c0:c1], start=k == 0, stop=k == KT - 1)
                E.do(ins, tok_mm)
                if t:
                    turn_tile(t - 1)
            turn_tile(NT - 1)
            E.meet()

            pe.wait_ge(s_w1, 12 * 16)

            def hidden(kv, rows, ncols, bank, c0):
                for s in range(32):
                    ins = mm(PS[:, bank, c0:c0 + ncols], W1[:, kv, s, :], rows(s), start=s == 0, stop=s == 31)
                return ins

            turn(PS[:, 7, 0:32], possb[0:32, 0:128], 32)
            E.do(turn(PS[:, 7, 32:64], possb[0:32, 128:256], 32), cmp_mm)
            pe.wait_ge(cmp_ev, 1)
            for kv in range(2):
                for s in range(32):
                    ins = mm(PS[:, 7, 64 + kv:65 + kv], W1[:, kv, s, :], posT[:, kv, s:s + 1], start=s == 0, stop=s == 31)
            E.do(ins, cmp_mm)
            for kv in range(2):
                ins = hidden(kv, lambda s: kvT[:, kv, s:s + 993:16], 63, 6, 256 * kv)
            E.do(ins, cmp_mm)
            pe.wait_ge(cmp_ev, 3)
            mm(PS[:, 5, 0:63], W2[:, 0, :], gh[:, 0, 0:63], start=True, stop=True)
            E.do(mm(PS[0:63, 5, 256:384], gh[:, 1, 0:63], W2[:, 1, :], start=True, stop=True), cmp_mm)
            E.meet()
            pe.wait_ge(cmp_ev, 4)

            def scores(k):
                u = UNITS[k]
                i, j, g = u["i"], u["j"], u["g"]
                if k >= 2:
                    pe.wait_ge(exp_done, k - 1)
                q = slice(i * P, (i + 1) * P)
                end = (i + 1) * P
                for c0 in range(u["t0"] * P, end, 512):
                    c1 = min(c0 + 512, end)
                    b = 2 * (k % 2) + (c0 - u["t0"] * P) // 512
                    ins = mm(PS[:, b, 0:c1 - c0], qrT[GP[g], j, q], kvT[GP[g], 2 if u["kind"] == "s" else 3, c0:c1], start=True, stop=True)
                if u["kind"] == "w":
                    ins = mm(PS[:, 2 * (k % 2) + 1, 128:191], qT[GP[g], j, q], kcp[GP[g], :], start=True, stop=True)
                E.do(ins, qk_done)

            pend = []

            def taken(gi):
                pe.wait_ge(pt_ev[gi % 2], gi // 2 + 1)

            def values():
                k, gi, grp = pend.pop(0)
                u = UNITS[k]
                g, hh = u["g"], k // 2
                out = PS[GP[g], 6, 0:P]
                taken(gi)
                if u["kind"] == "s" and gi == u["first"] and hh >= 2:
                    pe.wait_ge(o_ev, hh - 1)
                for c, (kind, t, _) in enumerate(grp):
                    if kind == "c":
                        ins = mm(out, vcp[0:63, g * 64:g * 64 + 64], PTs[0:63, gi % 3, c * P:(c + 1) * P], start=False, stop=True)
                    else:
                        c0 = (384 if kind == "s" else 640) + g * 64
                        ins = mm(out, kvtok(t)[:, c0:c0 + 64], PTs[:, gi % 3, c * P:(c + 1) * P], start=kind == "s" and t == 0, stop=False)
                E.do(ins, pv_done)

            def turn_probs(k):
                u = UNITS[k]
                pe.wait_ge(scale_done, k + 1)
                for n, grp in enumerate(u["groups"]):
                    gi = u["first"] + n
                    if gi >= 3:
                        taken(gi - 3)
                    for c, (kind, t, off) in enumerate(grp):
                        w = 63 if kind == "c" else P
                        ins = turn(PS[0:w, PTB[gi % 3], c * P:(c + 1) * P], Pb[:, k % 3, off:off + w], P)
                    E.do(ins, pt_done)
                    if len(pend) == 2:
                        values()
                    pend.append((k, gi, grp))

            for k in range(NU + 2):
                if k < NU:
                    scores(k)
                if k >= 2:
                    turn_probs(k - 2)
            while pend:
                values()
            E.meet()

            grp_n = [0]

            def turn4(src, nparts, width, name, per=4):
                gi = grp_n[0]
                grp_n[0] += 1
                if gi >= 2:
                    pe.wait_ge(sem("dt_ev" if (gi - 2) % 2 == 0 else "dt_ev2"), (gi - 2) // 2 + 1)
                for c, s in enumerate(src):
                    ins = turn(PS[0:width, 5 + gi % 2, c * (512 // per):c * (512 // per) + nparts], s, nparts)
                E.do(ins, sem("dt_done"))
                return gi

            def turned(gi):
                pe.wait_ge(sem("dt_ev" if gi % 2 == 0 else "dt_ev2"), gi // 2 + 1)

            pe.wait_ge(sem("win_in"), 16 * BD)
            for b in range(BD):
                gi = turn4([wKV[:, b, t, 0:P] for t in range(4)], P, P, "w")
                turned(gi)
                ins = mm(PS[0:64, 0, 0:512], qz[:, 1, b, :], kvTb[:, b % 2, 0:512], start=b == 0, stop=b == BD - 1)
                E.do(ins, sem("dk_used"))
            for c, col in ((0, 3), (1, 2)):
                for b in range(BD):
                    ins = mm(PS[0:64, 4, c:c + 1], qz[:, 1, b, :], kvT[:, col, SEQ + b:SEQ + b + 1], start=b == 0, stop=b == BD - 1)
            E.do(ins, sem("ds_done"))

            def own_key(slot, cols, first):
                gi = turn4([pself[0:64, slot, 0:8]], 64, 8, "self")
                turned(gi)
                ins = mm(PS[:, 7, 0:64], kvtok(8)[0:BD, cols:cols + P], PTs_self(slot), start=first, stop=False, skip_group_check=True)
                return ins

            def PTs_self(slot):
                return pself[0:8, 2, 0:64] if slot else sm_self[0:8, :]

            pe.wait_ge(sem("dp_ready"), 1)
            own_key(0, 640, True)
            gi = turn4([SS[0:64, t * P:(t + 1) * P] for t in range(4)], 64, P, "p", per=8)
            turned(gi)
            for b in range(BD):
                for t in range(4):
                    ins = mm(PS[:, 7, b * 8:b * 8 + 8], wKV[:, b, t, P:2 * P], PTb[:, t, b * 8:b * 8 + 8], start=False, stop=False, skip_group_check=True)
            E.do(ins, sem("win_pv"))

            def compressed(b):
                pe.wait_ge(sem("dg_done"), b + 1)
                if b:
                    pe.wait_ge(sem("dkc_ev"), b)
                mm(PS[:, 3, 0:127], W2[:, 0, :], ghs[:, 0, :], start=True, stop=True)
                E.do(mm(PS[0:127, 3, 256:384], ghs[:, 1, :], W2[:, 1, :], start=True, stop=True), sem("dkc_done"))

            for b in range(BD):
                pe.wait_ge(sem(f"pg{b % 2}"), 16 * (b // 2 + 1))
                for t4 in range(4):
                    for kv in range(2):
                        gi = turn4([cpg[:, b % 2, (t4 * 4 + c) * KV + kv * P:(t4 * 4 + c) * KV + (kv + 1) * P] for c in range(4)], P, P, "c")
                if b:
                    compressed(b - 1)
                turned(gi - 1)
                turned(gi)
                if b:
                    pe.wait_ge(sem("dg_done"), b)
                hidden(0, lambda s: kvTb[:, 0, (s % 16) * P + s // 16:(s % 16) * P + s // 16 + 127], 127, 4, 0)
                E.do(hidden(1, lambda s: kvTb[:, 1, (s % 16) * P + s // 16:(s % 16) * P + s // 16 + 127], 127, 4, 256), sem("dh_done"))
            compressed(BD - 1)
            pe.wait_ge(sem("dkc_ev"), BD)
            for b in range(BD):
                ins = mm(PS[0:64, 2, 0:127], qz[:, 0, b, :], kcs[:, b, :], start=b == 0, stop=b == BD - 1)
            E.do(ins, sem("ds_done"))
            pe.wait_ge(sem("dp_ready"), 2)
            E.do(mm(PS[0:64, 4, 0:127], const("group", 64), Pc[0:64, :], start=True, stop=True), sem("ds_done"))
            pe.wait_ge(sem("dp_ready"), 3)
            gi = turn4([SS[0:64, 0:127]], 64, 127, "pc")
            turned(gi)
            for b in range(BD):
                ins = mm(PS[:, 7, b * 8:b * 8 + 8], vcs[0:127, b, :], PTb[0:127, 0, b * 8:b * 8 + 8], start=False, stop=False, skip_group_check=True)
            E.step(ins)
            for b in range(BD):
                pe.wait_ge(sem(f"pg{b % 2}"), 16 * (b // 2 + 5))
                gis = []
                for t4 in range(4):
                    gi = turn4([cpg[:, b % 2, (t4 * 4 + c) * KV:(t4 * 4 + c) * KV + P] for c in range(4)], P, P, "k")
                    gis.append(gi)
                    if t4:
                        turned(gi - 1)
                        mm(PS[0:64, t4 - 1, :], qz[:, 1, b, :], kvTb[:, b % 2, (t4 - 1) * 512:t4 * 512], start=b == 0, stop=b == BD - 1)
                turned(gi)
                E.do(mm(PS[0:64, 3, :], qz[:, 1, b, :], kvTb[:, b % 2, 1536:2048], start=b == 0, stop=b == BD - 1), sem("dk2_used"))
            pe.wait_ge(sem("dp_ready"), 4)
            own_key(1, 384, False)
            for h8 in range(2):
                gi = turn4([SS[0:64, (h8 * 8 + c) * P:(h8 * 8 + c + 1) * P] for c in range(8)], 64, P, "p", per=8)
            turned(gi - 1)
            turned(gi)
            for b in range(BD):
                if b < 6:
                    pe.wait_ge(sem("held"), b + 1)
                for t in range(NPG):
                    v = hold[:, b, t, :] if b < 6 else cpg[:, b % 2, t * KV + P:(t + 1) * KV]
                    ins = mm(PS[:, 7, b * 8:b * 8 + 8], v, PTb[:, t, b * 8:b * 8 + 8], start=False, stop=b == BD - 1 and t == NPG - 1, skip_group_check=True)
                E.do(ins, sem("spv_used"))
            E.meet()

            pe.wait_ge(sem("vec_in"), 9 * 16)
            for n in range(KT):
                ins = turn(PS[:, 7, n * 40:(n + 1) * 40], vrows[0:40, n * P:(n + 1) * P], 40)
            E.do(ins, sem("vec_T"))

            def product(b, bank, rhs, kts):
                s = b % RING
                pe.wait_ge(s_ring[s], due[b])
                for c in range(3):
                    for k in range(kts):
                        ins = mm(PS[:, bank + c, 0:CH], ring[:, s, k, :], rhs[:, k, c * CH:(c + 1) * CH], start=k == 0, stop=k == kts - 1)
                E.do(ins, w_used)

            for n in range(KT):
                if n:
                    pe.wait_ge(sem("r_ev"), n)
                product(2 * n, 0, xT, KT)
                if n:
                    pe.wait_ge(sem("i_ev"), n)
                product(2 * n + 1, 3, xT, KT)
                if n:
                    pe.wait_ge(sem("stg_done"), n)
                    if n > 1:
                        pe.wait_ge(sem("stg_ev"), n - 1)
                    E.do(turn(PS[0:20, 6, 0:P], stg[:, :], P), sem("stg_T"))
                pe.wait_ge(sem("xc_done"), n + 1)
                for c in range(3):
                    ins = mm(PS[:, c, 0:CH], wra[:, n, :], xc[:, c * CH:(c + 1) * CH], start=True, stop=True)
                E.do(ins, sem("r_mm"))
                pe.wait_ge(sem("g_ev"), n + 1)
                for c in range(3):
                    ins = mm(PS[:, 3 + c, 0:CH], wri[:, n, :], xc[:, c * CH:(c + 1) * CH], start=True, stop=True)
                E.do(ins, sem("i_mm"))
            pe.wait_ge(sem("r_ev"), KT)
            product(2 * KT, 0, xT, KT)
            pe.wait_ge(sem("i_ev"), KT)
            product(2 * KT + 1, 3, AT, 4)
            pe.wait_ge(sem("stg_done"), KT)
            pe.wait_ge(sem("stg_ev"), KT - 1)
            E.do(turn(PS[0:20, 6, 0:P], stg[:, :], P), sem("stg_T"))
            E.meet()

            for n in range(KT):
                b = 2 * KT + 4 * n
                if n:
                    pe.wait_ge(sem("sg_done"), 2 * n)
                    product(b, 0, xT, KT)
                    pe.wait_ge(sem("mg_done"), 2 * n)
                    product(b + 1, 3, AT, 4)
                pe.wait_ge(sem("sg_done"), 2 * n + 1)
                product(b + 2, 0, xT, KT)
                pe.wait_ge(sem("mg_done"), 2 * n + 1)
                product(b + 3, 3, RT, KT)
            E.meet()

            pe.wait_ge(sem("wout_in"), 16)

            def turn_x1(t):
                n = rows_of(t)
                pe.wait_ge(sem("x1_done"), t + 1)
                for hf in range(2):
                    gi = 2 * t + hf
                    if gi >= 2:
                        pe.wait_ge(sem("x1T_ev"), gi - 1)
                    for k in range(4):
                        ins = turn(PS[:, 4 + gi % 2, k * P:k * P + n], x1tok[0:n, t, (hf * 4 + k) * P:(hf * 4 + k + 1) * P], n)
                    E.do(ins, sem("x1_T"))

            for t in range(NT):
                n = rows_of(t)
                if t >= 2:
                    pe.wait_ge(sem("xr_used"), t - 1)
                for c in range(2):
                    for k in range(KT):
                        ins = mm(PS[0:n, 2 * (t % 2) + c, :], mT[:, k, t * P:t * P + n], wout[:, k, c * 512:(c + 1) * 512], start=k == 0, stop=k == KT - 1)
                E.do(ins, sem("mix_mm"))
                if t >= 2:
                    turn_x1(t - 2)
            turn_x1(NT - 2)
            turn_x1(NT - 1)
            E.meet()
            pe.wait_ge(sem("wrt_in"), 32)
            for t in range(NT):
                n = rows_of(t)
                if t >= 2:
                    pe.wait_ge(sem("lg_ev"), t - 1)
                for k in range(KT):
                    ins = mm(PS[0:n, 6 + t % 2, 0:NE], x1T[:, k, t * P:t * P + n], wrt[:, k, :], start=k == 0, stop=k == KT - 1)
                E.do(ins, sem("lg_mm"))
            pe.wait_ge(sem("wsh_in"), 48)
            for hb in range(2):
                for bank, w in ((0, wsg), (3, wsu)):
                    if hb:
                        pe.wait_ge(sem("sil_done" if bank == 0 else "shT_done"), 1)
                    for c in range(3):
                        for k in range(KT):
                            ins = mm(PS[:, bank + c, 0:CH], w[:, k, hb * P:(hb + 1) * P], x1T[:, k, c * CH:(c + 1) * CH], start=k == 0, stop=k == KT - 1)
                    E.do(ins, sem("sh_mm"))
            pe.wait_ge(sem("M_done"), NT)
            pe.wait_ge(sem("lg_ev"), NT)
            for t in range(NT):
                n = rows_of(t)
                ins = mm(PS[:, 6, 0:NE], const("ones", n), Mm[0:n, t, :], start=t == 0, stop=t == NT - 1)
            E.do(ins, sem("table_mm"))
            def hot(t):
                n = rows_of(t)
                pe.wait_ge(sem("hot_done"), t + 1)
                for k in range(TOPK):
                    ins = mm(PS[:, 6, 0:P], at_row[0:n, t % 2, k, :], at_blk[0:n, t % 2, k, :], start=t == 0 and k == 0, stop=t == NT - 1 and k == TOPK - 1)
                E.do(ins, sem("hot_mm"))

            pe.wait_ge(sem("shT_done"), 2)
            for t in range(NT):
                n = rows_of(t)
                if t >= 2:
                    pe.wait_ge(sem("acc_done"), t - 1)
                for c in range(2):
                    for hb in range(2):
                        ins = mm(PS[0:n, 2 * (t % 2) + c, :], shT[:, hb, t * P:t * P + n], wsd[:, hb, c * 512:(c + 1) * 512], start=hb == 0, stop=hb == 1)
                E.do(ins, sem("shd_mm"))
                if t >= 2:
                    pe.wait_ge(sem("dst_done"), t - 1)
                ins = mm(PS[0:n, 4 + t % 2, 0:NE], const("before", n)[:, 0:n], Mm[0:n, t, :], start=True, stop=t == 0)
                for u in range(t):
                    ins = mm(PS[0:n, 4 + t % 2, 0:NE], const("ones")[:, 0:n], Mm[:, u, :], start=False, stop=u == t - 1)
                E.do(ins, sem("rk_mm"))
                if t >= 2:
                    hot(t - 2)
            hot(NT - 2)
            hot(NT - 1)
            pe.wait_ge(sem("table_step"), 1)
            E.do(turn(PS[0:1, 7, 0:P], ridx[:, 0:1], P), sem("table_mm"))
            for name, n in (("gu_mm0", 1), ("gu_mm1", 1), ("y_mm", 2), ("xgT_mm1", 2)):
                pe.nop().then_inc(sem(name), n)
            E.meet()
            turns = pe.value_load(nblk[0:1, 0:1], min_val=1, max_val=NBLK // 2)
            with pe.Fori(0, NBLK // 2) as i:
                with pe.If(i < turns):
                    for s in range(2):
                        pe.wait_ge(sem(f"xg{s}"), 16 * i + 16)
                        for hf in range(2):
                            pe.wait_ge(sem(f"xgT_ev{hf}"), 2 * i + s + 1)
                            for k in range(4):
                                ins = turn(PS[:, hf, k * P:(k + 1) * P], xg[:, s, hf * 4 + k::8], P)
                            ins.then_inc(sem(f"xgT_mm{hf}"), 1)
                    def gate_up(s, h, w):
                        for k in range(KT):
                            ins = mm(PS[:, 2 + s, h * DE:(h + 1) * DE], xgT[:, s, k, :], w[:, s, k, :], start=k == 0, stop=k == KT - 1)
                        return ins

                    def turn_hidden(s):
                        pe.wait_ge(sem(f"gu_free{s}"), i + 2)
                        for k in range(2):
                            ins = turn(PS[:, s, k * P:(k + 1) * P], hh_[:, s, k::2], P)
                        ins.then_inc(sem("hT_mm"), 1)

                    def down(s, c):
                        for k in range(2):
                            ins = mm(PS[:, 4 + 2 * s + c, :], hT[:, s, k, :], wexd[:, s, k, c * 512:(c + 1) * 512], start=k == 0, stop=k == 1)
                        return ins

                    for s in range(2):
                        pe.wait_ge(sem("xgT_ev0"), 2 * i + s + 2)
                        pe.wait_ge(sem("xgT_ev1"), 2 * i + s + 2)
                        pe.wait_ge(sem(f"wex{s}"), 32 * i + 32)
                        pe.wait_ge(sem(f"gu_free{s}"), i + 1)
                        gate_up(s, 0, wexg)
                        if s:
                            turn_hidden(0)
                        gate_up(s, 1, wexu).then_inc(sem(f"gu_mm{s}"), 1)
                    for s in range(2):
                        pe.wait_ge(sem("hT_ev"), 2 * i + s + 2)
                        pe.wait_ge(sem(f"wexd{s}"), 16 * i + 16)
                        pe.wait_ge(sem("y_ev"), 2 * i + s + 1)
                        pe.wait_ge(sem("y_ev2"), 2 * i + s + 1)
                        down(s, 0)
                        if s == 0:
                            turn_hidden(1)
                        down(s, 1).then_inc(sem("y_mm"), 1)

        @block.scalar
        def _(act):
            E = Engine(act, sem("act_chain"), met[1], (met[0], met[2]))
            fn = nc.scalar.activation

            def copy(out, in_):
                return fn(out, in_, ACT.Copy)

            for t in range(NT):
                n = rows_of(t)
                for hf in range(2):
                    gi = 2 * t + hf
                    act.wait_ge(x_turned, gi + 1)
                    E.do(copy(xT[:, hf * 4:hf * 4 + 4, t * P:t * P + n],
                              PS[:, gi % 4, :].rearrange("p (k c) -> p k c", k=4)[:, :, 0:n]), xT_ready)

            def tok_T(t):
                n = rows_of(t)
                for g3 in range(3):
                    gi = 3 * t + g3
                    act.wait_ge(tok_turned, gi + 1)
                    E.do(copy((qT, qrT, kvT)[g3][:, :, t * P:t * P + n],
                              PS[:, 6 + gi % 2, :].rearrange("p (k c) -> p k c", k=4)[:, :, 0:n]), tokT_ready)

            for t in range(NT):
                n = rows_of(t)
                b0 = 3 * (t % 2)
                act.wait_ge(tok_mm, t + 1)
                if t >= 2:
                    act.wait_ge(tok_turned, 3 * (t - 1))
                E.do(copy(qtok[0:n, t % 2, :].rearrange("p (j g d) -> p g j d", j=4, g=2),
                          PS[0:n, b0, :].rearrange("p (g j d) -> p g j d", g=2, j=4)))
                E.do(copy(kvtok(t)[0:n, 0:512], PS[0:n, b0 + 1, :]))
                E.do(copy(kvtok(t)[0:n, 512:768], PS[0:n, b0 + 2, 0:256]))
                E.do(fn(gate[0:n, t, :], PS[0:n, b0 + 2, 256:280], ACT.Sigmoid), tok_ev)
                if t:
                    tok_T(t - 1)
            tok_T(NT - 1)
            E.meet()
            act.wait_ge(cmp_mm, 1)
            E.do(copy(posT.rearrange("p a b -> p (a b)"), PS[:, 7, 0:64]), cmp_ev)
            act.wait_ge(cmp_mm, 2)
            E.step(copy(cbias, PS[:, 7, 64:66]), cmp_ev)
            act.wait_ge(cmp_mm, 3)
            E.do(fn(gh[:, 0, 0:63], PS[:, 6, 0:63], ACT.Gelu_apprx_tanh, bias=cbias[:, 0:1]))
            E.do(fn(gh[:, 1, 0:63], PS[:, 6, 256:319], ACT.Gelu_apprx_tanh, bias=cbias[:, 1:2]), cmp_ev)
            act.wait_ge(cmp_mm, 4)
            E.do(copy(kcp, PS[:, 5, 0:63]))
            E.do(copy(vcp[0:63, :], PS[0:63, 5, 256:384]), cmp_ev)
            E.meet()

            def exps(k):
                u = UNITS[k]
                hh = k // 2
                act.wait_ge(mx_done, k + 1)
                if k >= 3:
                    act.wait_ge(pt_done, UNITS[k - 2]["first"])
                n = (u["i"] + 1 - u["t0"]) * P
                S = PS[:, 2 * (k % 2):2 * (k % 2) + 2, :].rearrange("p a b -> p (a b)")
                if u["kind"] == "s":
                    E.do(fn(Pb[:, k % 3, 0:n], S[:, 0:n], ACT.Exp, bias=negb[:, k % 2, 0:1], scale=SCALE, accum_out=sums[:, hh % 2, 0:1]), exp_done)
                else:
                    E.do(fn(Pb[:, k % 3, 640:703], S[:, 640:703], ACT.Exp, bias=negb[:, k % 2, 1:2], scale=SCALE, accum_out=sums[:, hh % 2, 2:3]))
                    E.do(fn(Pb[:, k % 3, 0:n], S[:, 0:n], ACT.Exp, bias=negb[:, k % 2, 0:1], scale=SCALE, accum_out=sums[:, hh % 2, 1:2]), exp_done)

            def scaled(k):
                u = UNITS[k]
                n = (u["i"] + 1 - u["t0"]) * P
                act.wait_ge(coef_done, k + 1)
                if u["kind"] == "w":
                    E.do(fn(Pb[:, k % 3, 640:703], Pb[:, k % 3, 640:703], ACT.Copy, scale=coef[:, k % 2, 2:3]))
                c = "sw".index(u["kind"])
                E.do(fn(Pb[:, k % 3, 0:n], Pb[:, k % 3, 0:n], ACT.Copy, scale=coef[:, k % 2, c:c + 1]), scale_done)

            for k in range(NU + 2):
                if k < NU:
                    exps(k)
                if k >= 2:
                    take_turned(act, E, copy, k - 2, 1)
                if k < NU:
                    scaled(k)
            E.meet()

            dt_ev = sem("dt_ev")
            gi = 0
            for b in range(BD):
                if gi % 2 == 0:
                    act.wait_ge(sem("dt_done"), gi + 1)
                    if b >= 2:
                        act.wait_ge(sem("dk_used"), b - 1)
                    E.do(copy(kvTb[:, b % 2, 0:512], PS[:, 5 + gi % 2, :]), dt_ev)
                gi += 1

            def softmax_exp(n, slot):
                act.wait_ge(sem("dmx_done"), slot + 1)
                E.step(fn(SS[0:64, 0:n], SS[0:64, 0:n], ACT.Exp, bias=sm[0:64, slot, 1:2], scale=SCALE, accum_out=sm[0:64, slot, 2:3]), sem("dexp_done"))

            softmax_exp(513, 0)
            act.wait_ge(sem("dt_done"), gi + 1)
            E.do(copy(sm_self[0:8, :], PS[0:8, 5 + gi % 2, 0:64]), dt_ev)
            gi += 2
            for b in range(BD):
                for t4 in range(4):
                    act.wait_ge(sem("dt_done"), gi + 1)
                    if t4 == 0 and b:
                        act.wait_ge(sem("dh_done"), b)
                    E.do(copy(kvTb[:, 0, t4 * 512:(t4 + 1) * 512], PS[:, 5 + gi % 2, :]), dt_ev)
                    gi += 2
                act.wait_ge(sem("dh_done"), b + 1)
                if b:
                    act.wait_ge(sem("dkc_done"), b)
                for kv in range(2):
                    E.do(fn(ghs[:, kv, :], PS[:, 4, 256 * kv:256 * kv + 127], ACT.Gelu_apprx_tanh, bias=cbias[:, kv:kv + 1]), sem("dg_done") if kv else None)
                if b:
                    E.do(copy(kcs[:, b - 1, :], PS[:, 3, 0:127]))
                    E.do(copy(vcs[0:127, b - 1, :], PS[0:127, 3, 256:384]), sem("dkc_ev"))
            act.wait_ge(sem("dkc_done"), BD)
            E.do(copy(kcs[:, BD - 1, :], PS[:, 3, 0:127]))
            E.do(copy(vcs[0:127, BD - 1, :], PS[0:127, 3, 256:384]), sem("dkc_ev"))
            softmax_exp(127, 1)
            act.wait_ge(sem("dt_done"), gi + 1)
            E.do(copy(PTb[0:127, 0, :], PS[0:127, 5 + gi % 2, 0:64]), dt_ev)
            gi += 1
            for b in range(BD):
                for t4 in range(4):
                    if gi % 2 == 0:
                        act.wait_ge(sem("dt_done"), gi + 1)
                        if b >= 2:
                            act.wait_ge(sem("dk2_used"), b - 1)
                        E.do(copy(kvTb[:, b % 2, t4 * 512:(t4 + 1) * 512], PS[:, 5 + gi % 2, :]), dt_ev)
                    gi += 1
            softmax_exp(2049, 2)
            gi += 1
            act.wait_ge(sem("dt_done"), gi + 1)
            E.do(copy(PTb[:, 0:8, :], PS[:, 5 + gi % 2, :].rearrange("p (k c) -> p k c", k=8)), dt_ev)
            E.meet()

            act.wait_ge(sem("vec_T"), 1)
            E.step(copy(vec.rearrange("p a b -> p (a b)"), PS[:, 7, 0:320]), sem("vec_ev"))
            act.wait_ge(sem("lam_step"), 1)
            E.do(fn(lam[:, 1, :], lam[:, 0, :], ACT.Exp, scale=-1.0), sem("lam_exp"))
            act.wait_ge(sem("lam_step"), 2)

            def rows_T(n):
                act.wait_ge(sem("stg_T"), n + 1)
                E.do(copy(orows[0:20, n * P:(n + 1) * P], PS[0:20, 6, 0:P]), sem("stg_ev"))

            for n in range(KT):
                act.wait_ge(w_used, 2 * n + 1)
                if n:
                    act.wait_ge(sem("xc_done"), n)
                E.do(copy(ucb[:, 3:691].rearrange("p (a b) -> p a b", a=2), PS[:, 0:2, 0:CH]))
                E.do(copy(ucb[:, 691:1027], PS[:, 2, 0:336]))
                E.do(copy(ucs[:, :, 3], PS[:, 2, 336:344]), sem("u_ev"))
                act.wait_ge(w_used, 2 * n + 2)
                if n >= 2:
                    act.wait_ge(sem("stg_done"), n - 1)
                E.do(fn(gg[:, n % 2, :].rearrange("p (a b) -> p a b", a=3), PS[:, 3:6, 0:CH], ACT.Gelu_apprx_tanh), sem("g_ev"))
                act.wait_ge(sem("r_mm"), n + 1)
                if n:
                    act.wait_ge(sem("stg_done"), n)
                E.step(fn(rr.rearrange("p (a b) -> p a b", a=3), PS[:, 0:3, 0:CH], ACT.Sigmoid, bias=vec[:, n, 37:38]), sem("r_ev"))
                act.wait_ge(sem("i_mm"), n + 1)
                E.do(fn(ii.rearrange("p (a b) -> p a b", a=3), PS[:, 3:6, 0:CH], ACT.Sigmoid, bias=vec[:, n, 38:39]), sem("i_ev"))
                E.do(fn(aa, rr, ACT.Exp, scale=lam[:, 3, n:n + 1]))
                E.do(fn(th, rr, ACT.Tanh, scale=lam[:, 4, n:n + 1]), sem("a_done"))
                act.wait_ge(sem("v_done"), n + 1)
                E.do(fn(vv, vv, ACT.Sqrt), sem("sq_done"))
                if n:
                    rows_T(n - 1)
            rows_T(KT - 1)
            E.settle()
            act.nop().then_inc(sem("rows_ready"), 1)
            E.meet()
            for n in range(KT):
                for h in range(2):
                    act.wait_ge(w_used, 2 * KT + 4 * n + 2 * h + 1)
                    if n:
                        act.wait_ge(sem("mg_done"), 2 * (n - 1) + h + 1)
                    E.do(fn(sg[:, h, :].rearrange("p (a b) -> p a b", a=3), PS[:, 0:3, 0:CH], ACT.Sigmoid), sem("sg_done"))
            E.meet()

            def x1_T(t):
                n = rows_of(t)
                for hf in range(2):
                    gi = 2 * t + hf
                    act.wait_ge(sem("x1_T"), gi + 1)
                    E.do(copy(x1T[:, hf * 4:hf * 4 + 4, t * P:t * P + n],
                              PS[:, 4 + gi % 2, :].rearrange("p (k c) -> p k c", k=4)[:, :, 0:n]), sem("x1T_ev"))

            for t in range(NT):
                n = rows_of(t)
                act.wait_ge(sem("var_done"), t + 1)
                E.do(fn(st[0:n, t % 2, 14:15], st[0:n, t % 2, 13:14], ACT.Sqrt), sem("std_done"))
                if t >= 2:
                    x1_T(t - 2)
            x1_T(NT - 2)
            x1_T(NT - 1)
            E.meet()
            for t in range(NT):
                n = rows_of(t)
                act.wait_ge(sem("lg_mm"), t + 1)
                E.do(fn(sc[0:n, t, :], PS[0:n, 6 + t % 2, 0:NE], ACT.Sigmoid), sem("lg_ev"))
            for hb in range(2):
                act.wait_ge(sem("sh_mm"), 2 * hb + 1)
                if hb:
                    act.wait_ge(sem("shT_done"), 1)
                E.do(fn(sil.rearrange("p (a b) -> p a b", a=3), PS[:, 0:3, 0:CH], ACT.Silu), sem("sil_done"))
            for name, n in (("y_ev", 2), ("hT_ev", 1), ("xgT_ev0", 1), ("yd0", 1), ("yd1", 1)):
                act.nop().then_inc(sem(name), n)
            E.meet()
            turns = act.value_load(nblk[0:1, 0:1], min_val=1, max_val=NBLK // 2)

            def block_out(s, b, n):
                act.wait_ge(sem("y_ev2"), n)
                act.wait_ge(sem("y_ev"), n)
                act.dma_start(y_dram[bass.ds(b, 1), :, :].rearrange("u p d -> (u p) d"), ysb[:, s, :]).then_inc(sem(f"yd{s}"), 16)

            def act_turn(i, first):
                for s in range(2):
                    act.wait_ge(sem("xgT_mm0"), i * 2 + s + 1)
                    act.wait_ge(sem(f"gu_mm{s}"), i + 1)
                    copy(xgT[:, s, 0:4, :], PS[:, 0, :].rearrange("p (k c) -> p k c", k=4)).then_inc(sem("xgT_ev0"), 1)
                if not first:
                    block_out(1, i * 2 - 1, 2 * i + 2)
                for s in range(2):
                    act.wait_ge(sem(f"gu_mm{s}"), i + 2)
                    act.wait_ge(sem(f"gu_free{s}"), i + 1)
                    fn(hsl[:, s, :], PS[:, 2 + s, 0:DE], ACT.Silu).then_inc(sem("sl_done"), 1)
                    if s == 0:
                        hidden_T(i, 0)
                hidden_T(i, 1)
                for s in range(2):
                    act.wait_ge(sem("y_mm"), 2 * i + s + 3)
                    act.wait_ge(sem(f"yd{s}"), 16 * i + 1)
                    copy(ysb[:, s, 512:1024], PS[:, 5 + 2 * s, :]).then_inc(sem("y_ev"), 1)
                    if s == 0:
                        block_out(0, i * 2, 2 * i + 3)

            def hidden_T(i, s):
                act.wait_ge(sem("hT_mm"), 2 * i + s + 1)
                act.wait_ge(sem("y_mm"), 2 * i + s + 1)
                copy(hT[:, s, :, :], PS[:, s, 0:256].rearrange("p (k c) -> p k c", k=2)).then_inc(sem("hT_ev"), 1)

            act_turn(0, True)
            with act.Fori(1, NBLK // 2) as i:
                with act.If(i < turns):
                    act_turn(i, False)
            block_out(1, turns * 2 - 1, turns * 2 + 2)
            act.wait_ge(sem("yd0"), turns * 16 + 1)
            act.wait_ge(sem("yd1"), turns * 16 + 1)
            act.nop().then_inc(sem("y_all"), 1)
            for t in range(NT):
                n = rows_of(t)
                act.wait_ge(sem("var_done"), NT + t + 1)
                fn(st[0:n, t % 2, 14:15], st[0:n, t % 2, 13:14], ACT.Sqrt).then_inc(sem("std_done"), 1)
                act.wait_ge(sem("shift_done"), t + 1)
                y = x1tok[0:n, t, :]
                fn(y, y, ACT.Identity, bias=st[0:n, t % 2, 12:13], scale=st[0:n, t % 2, 15:16]).then_inc(sem("normed"), 1)

        @block.vector
        def _(dve):
            E = Engine(dve, sem("dve_chain"), met[2], (met[0], met[1]))
            V = nc.vector
            tt, ts, stt = V.tensor_tensor, V.tensor_scalar, V.scalar_tensor_tensor
            dve.wait_ge(s_const, 16)
            E.do(V.memset(izero[:, :], 0))
            dve.wait_ge(sem("ptab_in"), 8 * 16)
            E.step(ts(pgidx[:, :], pgidx[:, :], 8.0, const("eighth"), ALU.mult, ALU.add), sem("pg_ready"))
            cosv = const("cos").rearrange("p (t c) -> p t c", c=8)
            sinv = const("sin").rearrange("p (t c) -> p t c", c=8)

            def rope(x1, x2, y1, y2, cs_, sn_, tmp):
                E.do(tt(tmp[0], x1, cs_, ALU.mult))
                E.do(tt(tmp[1], x2, sn_, ALU.mult))
                E.do(tt(tmp[2], x2, cs_, ALU.mult))
                E.step(tt(tmp[3], x1, sn_, ALU.mult))
                E.do(tt(y1, tmp[0], tmp[1], ALU.subtract))

            for t in range(NT):
                n = rows_of(t)
                dve.wait_ge(tok_ev, t + 1)
                if t >= 2:
                    dve.wait_ge(tok_turned, 3 * (t - 1))
                E.step(V.tensor_copy(qrtok[0:n, t % 2, :], qtok[0:n, t % 2, :]))
                q3 = qtok[0:n, t % 2, :].rearrange("p (h d) -> p h d", h=NH)
                r3 = qrtok[0:n, t % 2, :].rearrange("p (h d) -> p h d", h=NH)
                tm = [rt[0:n, k, :].rearrange("p (h c) -> p h c", h=8) for k in range(4)]
                c3 = cosv[0:n, t:t + 1, :].broadcast_to([n, 8, 8])
                s3 = sinv[0:n, t:t + 1, :].broadcast_to([n, 8, 8])
                rope(q3[:, :, 0:8], q3[:, :, 8:16], r3[:, :, 0:8], r3[:, :, 8:16], c3, s3, tm)
                E.step(tt(r3[:, :, 8:16], tm[2], tm[3], ALU.add))
                for j in range(2):
                    k3 = kvtok(t)[0:n, KV * (1 + j):KV * (1 + j) + P].rearrange("p (h d) -> p h d", h=2)
                    tm2 = [rt[0:n, k, 0:16].rearrange("p (h c) -> p h c", h=2) for k in range(4)]
                    c2, s2 = c3[:, 0:2, :], s3[:, 0:2, :]
                    rope(k3[:, :, 0:8], k3[:, :, 8:16], k3[:, :, 0:8], k3[:, :, 8:16], c2, s2, tm2)
                    E.step(tt(k3[:, :, 8:16], tm2[2], tm2[3], ALU.add), rope_done if j else None)
            E.meet()
            E.meet()

            def maxima(k):
                u = UNITS[k]
                i = u["i"]
                dve.wait_ge(qk_done, k + 1)
                n = (i + 1 - u["t0"]) * P
                S = PS[:, 2 * (k % 2):2 * (k % 2) + 2, :].rearrange("p a b -> p (a b)")
                E.do(tt(S[:, n - P:n], S[:, n - P:n], const("diag"), ALU.add))
                if u["kind"] == "w":
                    if i >= 4:
                        E.do(tt(S[:, 0:P], S[:, 0:P], const("edge"), ALU.add))
                    E.do(tt(S[:, 640:703], S[:, 640:703], const("cmpm")[:, i * 63:(i + 1) * 63], ALU.add))
                E.settle()
                if u["kind"] == "w":
                    E.do(V.reduce_max(mx[:, 1:2], S[:, 640:703], AX))
                E.step(V.reduce_max(mx[:, 0:1], S[:, 0:n], AX))
                if u["kind"] == "w":
                    E.do(ts(negb[:, k % 2, 1:2], mx[:, 1:2], -1e28, -SCALE, ALU.max, ALU.mult))
                E.do(ts(negb[:, k % 2, 0:1], mx[:, 0:1], -SCALE, None, ALU.mult), mx_done)

            def coefs(k):
                u = UNITS[k]
                h = 4 * u["g"] + u["j"]
                c = slice(0, 1) if u["kind"] == "s" else slice(1, 3)
                v = coef[:, k % 2, c]
                dve.wait_ge(exp_done, k + 1)
                if k >= 2:
                    dve.wait_ge(scale_done, k - 1)
                E.step(ts(v, sums[:, (k // 2) % 2, c], 1e-30, None, ALU.max))
                E.step(V.reciprocal(v, v))
                E.do(tt(v, v, gate[:, u["i"], 3 * h + c.start:3 * h + c.stop], ALU.mult), coef_done)

            def head_out(hh):
                u = UNITS[2 * hh + 1]
                dve.wait_ge(pv_done, u["first"] + len(u["groups"]))
                E.do(V.tensor_copy(AT[GP[u["g"]], u["j"], u["i"] * P:(u["i"] + 1) * P], PS[GP[u["g"]], 6, 0:P]), o_ev)

            for t in range(NT):
                n = rows_of(t)
                g3 = gate[0:n, t, :].rearrange("p (h c) -> p h c", c=3)
                E.step(V.tensor_copy(rt[0:n, 0, 0:8], g3[:, :, 0]))
                E.step(V.tensor_copy(rt[0:n, 1, 0:16].rearrange("p (h c) -> p h c", c=2), g3[:, :, 1:3]))
                E.do(V.tensor_copy(g3[:, :, 0:2], rt[0:n, 1, 0:16].rearrange("p (h c) -> p h c", c=2)))
                E.step(V.tensor_copy(g3[:, :, 2], rt[0:n, 0, 0:8]))
            for k in range(NU + 2):
                if k < NU:
                    maxima(k)
                if k >= 2:
                    take_turned(dve, E, V.tensor_copy, k - 2, 0)
                if k < NU:
                    coefs(k)
                if k >= 6 and k % 2 == 0:
                    head_out(k // 2 - 3)
            head_out(NU // 2 - 2)
            head_out(NU // 2 - 1)
            E.step(V.memset(qz.rearrange("p a b c -> p (a b c)"), 0.0))
            for r, src in ((0, qT), (1, qrT)):
                for g in range(2):
                    v = qz[GP[g], r, :, :].rearrange("p b c -> p (b c)")
                    for j in range(4):
                        E.do(V.tensor_copy(v[:, 4 * g + j::72], src[GP[g], j, SEQ:NTOK]))
            E.meet()

            dt2 = sem("dt_ev2")
            dve.wait_ge(sem("gsel_in"), 16)
            gi = 0
            for b in range(BD):
                if gi % 2:
                    dve.wait_ge(sem("dt_done"), gi + 1)
                    if b >= 2:
                        dve.wait_ge(sem("dk_used"), b - 1)
                    E.do(V.tensor_copy(kvTb[:, b % 2, 0:512], PS[:, 5 + gi % 2, :]), dt2)
                gi += 1

            def softmax_in(n, slot):
                E.step(V.reduce_max(sm[0:64, slot, 0:1], SS[0:64, 0:n], AX))
                E.step(ts(sm[0:64, slot, 1:2], sm[0:64, slot, 0:1], -SCALE, None, ALU.mult), sem("dmx_done"))

            def inverse(slot):
                dve.wait_ge(sem("dexp_done"), slot + 1)
                E.step(V.reciprocal(sm[0:64, slot, 3:4], sm[0:64, slot, 2:3]))

            dve.wait_ge(sem("ds_done"), 1)
            E.do(V.tensor_copy(SS[0:64, 0:512], PS[0:64, 0, :]))
            E.do(V.tensor_copy(sm[0:64, 5, 0:1], PS[0:64, 4, 1:2]))
            E.step(V.tensor_copy(SS[0:64, 512:513], PS[0:64, 4, 0:1]))
            softmax_in(513, 0)
            inverse(0)
            E.step(tt(sm[0:64, 0, 4:5], sm[0:64, 0, 3:4], gsel[0:64, 1:2], ALU.mult))
            E.step(ts(SS[0:64, 0:513], SS[0:64, 0:513], sm[0:64, 0, 4:5], None, ALU.mult))
            E.step(ts(pself[0:64, 0, 0:8], const("own", 64), SS[0:64, 512:513], None, ALU.mult), sem("dp_ready"))
            gi += 1
            dve.wait_ge(sem("dt_done"), gi + 1)
            E.do(V.tensor_copy(PTb[:, 0:4, :], PS[:, 5 + gi % 2, 0:256].rearrange("p (k c) -> p k c", k=4)), dt2)
            gi += 1
            for b in range(BD):
                for t4 in range(4):
                    gi += 1
                    dve.wait_ge(sem("dt_done"), gi + 1)
                    if t4 == 0 and b:
                        dve.wait_ge(sem("dh_done"), b)
                    E.do(V.tensor_copy(kvTb[:, 1, t4 * 512:(t4 + 1) * 512], PS[:, 5 + gi % 2, :]), dt2)
                    gi += 1
            dve.wait_ge(sem("ds_done"), 2)
            dve.wait_ge(sem("win_pv"), 1)
            E.step(V.tensor_copy(SS[0:64, 0:127], PS[0:64, 2, 0:127]))
            softmax_in(127, 1)
            inverse(1)
            E.step(ts(Pc[0:64, :], SS[0:64, 0:127], sm[0:64, 1, 3:4], None, ALU.mult), sem("dp_ready"))
            E.step(ts(SS[0:64, 0:127], Pc[0:64, :], gsel[0:64, 2:3], None, ALU.mult), sem("dp_ready"))
            E.step(V.memset(zc[0:64, :], 0.0))
            dve.wait_ge(sem("ds_done"), 3)
            E.step(V.tensor_copy(zc[0:64, 1:128], PS[0:64, 4, 0:127]))
            z = zc[0:64, 0:132].rearrange("p (s c) -> p s c", c=4)
            imp = sm[0:64, 3, 0:32]
            E.step(tt(imp, z[:, 0:32, 1], z[:, 0:32, 2], ALU.add))
            E.step(tt(imp, imp, z[:, 0:32, 3], ALU.add))
            E.step(stt(imp, imp, 2.0, z[:, 0:32, 0], ALU.mult, ALU.add))
            E.step(tt(imp, imp, z[:, 1:33, 0], ALU.add))
            E.step(V.memset(sm[0:64, 3, 32:33], 0.0))
            E.step(tt(sm[0:64, 3, 0:33], sm[0:64, 3, 0:33], const("free", 64), ALU.mult))
            E.step(tt(sm[0:64, 3, 0:33], sm[0:64, 3, 0:33], const("force", 64), ALU.add))
            score = sm[0:64, 3, 0:33]
            row = sm[0:64, 3:4, 0:33].broadcast_to([64, 33, 33])
            E.do(V.tensor_copy(rank[0:64, 0, :].rearrange("p (a b) -> p a b", a=33), row))
            E.step(V.tensor_copy(rank[0:64, 1, :].rearrange("p (a b) -> p a b", a=33), score.unsqueeze(2).broadcast_to([64, 33, 33])))
            ra, rb_ = rank[0:64, 0, :], rank[0:64, 1, :]
            big = SS[0:64, 200:200 + 1089]
            E.step(tt(big, ra, rb_, ALU.is_gt))
            E.step(tt(rb_, ra, rb_, ALU.is_equal))
            E.step(tt(rb_, rb_, const("lower", 64), ALU.mult))
            E.step(tt(big, big, rb_, ALU.add))
            E.step(V.tensor_reduce(sm[0:64, 4, 0:33], big.rearrange("p (a b) -> p a b", a=33), AX, ALU.add))
            E.step(ts(selmask[0:64, 0:33], sm[0:64, 4, 0:33], 15.5, NEG, ALU.is_gt, ALU.mult))
            gi += 1
            for b in range(BD):
                for t4 in range(4):
                    if gi % 2:
                        dve.wait_ge(sem("dt_done"), gi + 1)
                        if b >= 2:
                            dve.wait_ge(sem("dk2_used"), b - 1)
                        E.do(V.tensor_copy(kvTb[:, b % 2, t4 * 512:(t4 + 1) * 512], PS[:, 5 + gi % 2, :]), dt2)
                    gi += 1
            dve.wait_ge(sem("dk2_used"), BD)
            for c in range(4):
                E.do(tt(SS[0:64, c * 512:(c + 1) * 512].rearrange("p (a b c) -> p a b c", a=4, c=4),
                        PS[0:64, c, :].rearrange("p (a b c) -> p a b c", a=4, c=4),
                        selmask[0:64, 0:32].unsqueeze(1).unsqueeze(3).broadcast_to([64, 4, 32, 4]), ALU.add))
            E.step(V.tensor_copy(SS[0:64, 2048:2049], sm[0:64, 5, 0:1]))
            softmax_in(2049, 2)
            inverse(2)
            E.step(tt(sm[0:64, 2, 4:5], sm[0:64, 2, 3:4], gsel[0:64, 0:1], ALU.mult))
            E.step(ts(SS[0:64, 0:2049], SS[0:64, 0:2049], sm[0:64, 2, 4:5], None, ALU.mult))
            E.step(ts(pself[0:64, 1, 0:8], const("own", 64), SS[0:64, 2048:2049], None, ALU.mult), sem("dp_ready"))
            dve.wait_ge(sem("dt_done"), gi + 1)
            E.do(V.tensor_copy(pself[0:8, 2, 0:64], PS[0:8, 5 + gi % 2, 0:64]), dt2)
            gi += 2
            dve.wait_ge(sem("dt_done"), gi + 1)
            E.do(V.tensor_copy(PTb[:, 8:16, :], PS[:, 5 + gi % 2, :].rearrange("p (k c) -> p k c", k=8)), dt2)
            dve.wait_ge(sem("spv_used"), BD)
            for g in range(2):
                E.step(V.tensor_copy(AT[GP[g], :, SEQ:NTOK],
                                     PS[GP[g], 7, 0:64].rearrange("p (b h) -> p h b", h=8)[:, 4 * g:4 * g + 4, :]))
            E.meet()

            dve.wait_ge(sem("vec_ev"), 1)
            lm = vec[:, :, 39]
            E.step(ts(lam[:, 2, :], lm, -1.0, None, ALU.mult))
            E.step(tt(lam[:, 0, :], lam[:, 2, :], lm, ALU.max), sem("lam_step"))
            E.step(ts(lam[:, 2, :], lam[:, 2, :], 0.0, None, ALU.max))
            dve.wait_ge(sem("lam_exp"), 1)
            E.step(ts(lam[:, 5, :], lam[:, 1, :], 2.0, None, ALU.add))
            E.step(V.reciprocal(lam[:, 5, :], lam[:, 5, :]))
            E.step(tt(lam[:, 5, :], lam[:, 5, :], lam[:, 1, :], ALU.mult))
            E.step(tt(lam[:, 6, :], lam[:, 5, :], lam[:, 5, :], ALU.mult))
            E.step(V.memset(lam[:, 7, :], 1.0 / 17))
            for k in range(15, 0, -2):
                E.step(tt(lam[:, 7, :], lam[:, 7, :], lam[:, 6, :], ALU.mult))
                E.step(ts(lam[:, 7, :], lam[:, 7, :], 1.0 / k, None, ALU.add))
            E.step(tt(lam[:, 7, :], lam[:, 7, :], lam[:, 5, :], ALU.mult))
            E.step(stt(lam[:, 7, :], lam[:, 7, :], 2.0, lam[:, 2, :], ALU.mult, ALU.add))
            E.step(ts(lam[:, 3, :], lam[:, 7, :], -8.0, None, ALU.mult))
            E.step(ts(lam[:, 4, :], lam[:, 7, :], 8.0, None, ALU.mult), sem("lam_step"))
            E.step(V.memset(ucb[:, 0:3], 0.0))
            for n in range(KT):
                E.step(V.tensor_copy(ucs[:, :, 0:3], vec[:, n, 0:24].rearrange("p (b r) -> p b r", b=BD)))
                dve.wait_ge(sem("u_ev"), n + 1)
                if n:
                    dve.wait_ge(sem("i_mm"), n)
                cw = lambda k: vec[:, n, 32 + k:33 + k]
                E.do(ts(xc[:, 0:SEQ], ucb[:, 0:SEQ], cw(0), vec[:, n, 36:37], ALU.mult, ALU.add))
                E.step(ts(xc[:, SEQ:NTOK], ucs[:, :, 0], cw(0), vec[:, n, 36:37], ALU.mult, ALU.add))
                for k in range(1, 4):
                    E.do(stt(xc[:, 0:SEQ], ucb[:, k:k + SEQ], cw(k), xc[:, 0:SEQ], ALU.mult, ALU.add))
                    E.step(stt(xc[:, SEQ:NTOK], ucs[:, :, k], cw(k), xc[:, SEQ:NTOK], ALU.mult, ALU.add))
                if n:
                    dve.wait_ge(sem("stg_T"), n)
                E.do(V.tensor_copy(stg[:, 0:3], ucb[:, 1024:1027]))
                E.step(V.tensor_copy(stg[:, 3:11], ucs[:, :, 3]), sem("xc_done"))
                dve.wait_ge(sem("a_done"), n + 1)
                E.step(ts(vv, th, 1.0, None, ALU.add))
                E.step(V.reciprocal(vv, vv))
                E.step(stt(vv, th, 2.0, vv, ALU.mult, ALU.mult), sem("v_done"))
                E.step(tt(ii, ii, xc, ALU.mult))
                dve.wait_ge(sem("sq_done"), n + 1)
                E.step(tt(ii, ii, vv, ALU.mult))
                E.do(V.tensor_tensor_scan(hs[:, 0:SEQ], aa[:, 0:SEQ], ii[:, 0:SEQ], 0.0, ALU.mult, ALU.add))
                E.step(tt(hs[:, SEQ:NTOK], aa[:, SEQ:NTOK], vec[:, n, 24:32], ALU.mult))
                E.step(tt(hs[:, SEQ:NTOK], hs[:, SEQ:NTOK], ii[:, SEQ:NTOK], ALU.add))
                E.do(V.tensor_copy(stg[:, 11:20], hs[:, SEQ - 1:NTOK]))
                E.step(tt(RT[:, n, :], hs, gg[:, n % 2, :], ALU.mult), sem("stg_done"))
            E.meet()
            for n in range(KT):
                for h in range(2):
                    dve.wait_ge(w_used, 2 * KT + 4 * n + 2 * h + 2)
                    dve.wait_ge(sem("sg_done"), 2 * n + h + 1)
                    dst = m1 if h == 0 else sg[:, 1, :]
                    if h == 0:
                        E.step(tt(m1.rearrange("p (a b) -> p a b", a=3), PS[:, 3:6, 0:CH], sg[:, 0, :].rearrange("p (a b) -> p a b", a=3), ALU.mult), sem("mg_done"))
                    else:
                        E.step(tt(mT[:, n, :].rearrange("p (a b) -> p a b", a=3), PS[:, 3:6, 0:CH], sg[:, 1, :].rearrange("p (a b) -> p a b", a=3), ALU.mult))
                        E.step(tt(mT[:, n, :], mT[:, n, :], m1, ALU.add), sem("mg_done"))
            E.meet()

            def stats(y, s):
                E.do(V.bn_stats(s[:, 0:6], y[:, 0:512]))
                E.step(V.bn_stats(s[:, 6:12], y[:, 512:1024]))
                E.step(V.bn_aggr(s[:, 12:14], s[:, 0:12]))
                E.step(ts(s[:, 13:14], s[:, 13:14], EPS, None, ALU.add), sem("var_done"))

            def norm(y, out, n, t):
                s = st[0:n, t % 2, :]
                stats(y, s)
                dve.wait_ge(sem("std_done"), t + 1)
                E.step(V.reciprocal(s[:, 15:16], s[:, 14:15]))
                E.step(ts(y, y, s[:, 12:13], s[:, 15:16], ALU.subtract, ALU.mult))
                E.step(tt(y, y, lnw[0:n, 0, :], ALU.mult))
                E.step(tt(out, y, lnw[0:n, 1, :], ALU.add), sem("x1_done"))

            dve.wait_ge(sem("ln_in"), 64)
            for t in range(NT):
                n = rows_of(t)
                dve.wait_ge(sem("mix_mm"), t + 1)
                dve.wait_ge(s_xin[t % 2], 16 * (t // 2 + 1))
                y = yy[0:n, t % 2, :]
                E.step(stt(y.rearrange("p (a b) -> p a b", a=2), xr[0:n, t % 2, :].rearrange("p (a b) -> p a b", a=2), ALPHA,
                           PS[0:n, 2 * (t % 2):2 * (t % 2) + 2, :], ALU.mult, ALU.add), sem("xr_used"))
                norm(y, x1tok[0:n, t, :], n, t)
            E.meet()

            dve.wait_ge(sem("wrt_in"), 32)
            for t in range(NT):
                n = rows_of(t)
                dve.wait_ge(sem("lg_ev"), t + 1)
                E.step(tt(selv[0:n, :], sc[0:n, t, :], rb[0:n, :], ALU.add))
                E.step(V.max(sel8[0:n, :], selv[0:n, :]))
                E.step(V.max_index(i8[0:n, :], sel8[0:n, :], selv[0:n, :]))
                E.step(V.tensor_copy(idxf[0:n, t, :], i8[0:n, :]))
                for k in range(TOPK):
                    E.do(ts(oh[0:n, k, :], const("exp", n), idxf[0:n, t, k:k + 1], None, ALU.is_equal))
                E.settle()
                E.do(V.tensor_reduce(Mm[0:n, t, :], oh[0:n, :, :].rearrange("p k e -> p e k"), AX, ALU.add))
                E.step(tt(tmp6[0:n, :, :], oh[0:n, :, :], sc[0:n, t:t + 1, :].broadcast_to([n, TOPK, NE]), ALU.mult))
                E.step(V.tensor_reduce(wfin[0:n, t, :], tmp6[0:n, :, :], AX, ALU.add))
                E.step(V.tensor_reduce(wk[0:n, 0:1], wfin[0:n, t, :], AX, ALU.add))
                E.step(V.reciprocal(wk[0:n, 1:2], wk[0:n, 0:1]))
                E.step(ts(wfin[0:n, t, :], wfin[0:n, t, :], wk[0:n, 1:2], ROUTED_SCALE, ALU.mult, ALU.mult), sem("M_done"))
            for hb in range(2):
                dve.wait_ge(sem("sh_mm"), 2 * hb + 2)
                dve.wait_ge(sem("sil_done"), hb + 1)
                E.step(tt(shT[:, hb, :].rearrange("p (a b) -> p a b", a=3), PS[:, 3:6, 0:CH], sil.rearrange("p (a b) -> p a b", a=3), ALU.mult), sem("shT_done"))
            dve.wait_ge(sem("table_mm"), 1)
            E.step(V.tensor_copy(pos, PS[:, 6, 0:NE]))
            E.step(ts(nbl, pos, 0.5, None, ALU.is_gt))
            for k in range(1, 9):
                E.step(stt(nbl, pos, 128.0 * k + 0.5, nbl, ALU.is_gt, ALU.add))
            E.step(V.tensor_tensor_scan(cs, const("ones")[:, 0:NE], nbl, 0.0, ALU.mult, ALU.add))
            E.step(tt(base, cs, nbl, ALU.subtract))
            E.step(ts(base, base, 128.0, None, ALU.mult))
            E.step(ts(ridx[:, 0:NE], cs, const("row"), None, ALU.is_le))
            E.step(V.tensor_reduce(wk[:, 2:3], ridx[:, 0:NE], AX, ALU.add))
            E.step(ts(ridx[:, 0:1], wk[:, 2:3], float(NE - 1), None, ALU.min), sem("table_step"))
            E.step(ts(wk[0:1, 3:4], cs[0:1, NE - 1:NE], 0.5, None, ALU.mult))
            E.step(ts(ridx[0:1, 1:NE + 0], const("exp", 1)[:, 0:NE - 1], wk[0:1, 3:4], None, ALU.is_lt))
            E.step(V.tensor_reduce(wk[0:1, 4:5], ridx[0:1, 1:NE], AX, ALU.add))
            E.step(V.tensor_copy(nblk[0:1, 0:1], wk[0:1, 4:5]))
            dve.wait_ge(sem("x1_out"), 32)
            for t in range(NT):
                n = rows_of(t)
                dve.wait_ge(sem("shd_mm"), t + 1)
                x2 = x1tok[0:n, t, :].rearrange("p (a b) -> p a b", a=2)
                E.do(stt(x2, x2, ALPHA, PS[0:n, 2 * (t % 2):2 * (t % 2) + 2, :], ALU.mult, ALU.add), sem("acc_done"))
                dve.wait_ge(sem("rk_mm"), t + 1)
                E.step(tt(pos[0:n, :], PS[0:n, 4 + t % 2, 0:NE], base[0:n, :], ALU.add))
                for k in range(TOPK):
                    E.do(ts(oh[0:n, k, :], const("exp", n), idxf[0:n, t, k:k + 1], None, ALU.is_equal))
                E.settle()
                E.step(tt(tmp6[0:n, :, :], oh[0:n, :, :], pos[0:n, :].unsqueeze(1).broadcast_to([n, TOPK, NE]), ALU.mult))
                E.step(V.tensor_reduce(dstf[0:n, t, :], tmp6[0:n, :, :], AX, ALU.add))
                E.step(V.tensor_copy(dsti[0:n, t, :], dstf[0:n, t, :]), sem("dst_done"))
                E.do(ts(rowb[0:n, 0, 0:TOPK], dsti[0:n, t, :], P - 1, None, ALU.bitwise_and))
                E.step(ts(rowb[0:n, 1, 0:TOPK], dsti[0:n, t, :], 7, None, ALU.logical_shift_right))
                E.step(V.tensor_copy(blkf[0:n, :, 0:TOPK], rowb[0:n, :, 0:TOPK]))
                if t >= 2:
                    dve.wait_ge(sem("hot_mm"), t - 1)
                for k in range(TOPK):
                    E.do(ts(at_row[0:n, t % 2, k, :], const("blk", n), blkf[0:n, 0, k:k + 1], None, ALU.is_equal))
                    E.do(ts(at_blk[0:n, t % 2, k, :], const("blk", n), blkf[0:n, 1, k:k + 1], const("tokid", n)[:, t:t + 1], ALU.is_equal, ALU.mult),
                         sem("hot_done") if k == TOPK - 1 else None)
                E.settle()
            dve.wait_ge(sem("table_mm"), 2)
            E.step(V.tensor_copy(blke[0:1, :], PS[0:1, 7, 0:P]))
            dve.wait_ge(sem("hot_mm"), NT)
            E.step(V.tensor_copy(idxall[:, :], PS[:, 6, 0:P]), sem("table_step"))
            for name, n in (("gu_free0", 1), ("gu_free1", 1), ("xgT_ev1", 1), ("y_ev2", 2)):
                dve.nop().then_inc(sem(name), n)
            E.meet()
            turns = dve.value_load(nblk[0:1, 0:1], min_val=1, max_val=NBLK // 2)
            with dve.Fori(0, NBLK // 2) as i:
                with dve.If(i < turns):
                    for s in range(2):
                        dve.wait_ge(sem("xgT_mm1"), i * 2 + s + 3)
                        dve.wait_ge(sem(f"gu_mm{s}"), i + 1)
                        V.tensor_copy(xgT[:, s, 4:8, :], PS[:, 1, :].rearrange("p (k c) -> p k c", k=4)).then_inc(sem("xgT_ev1"), 1)
                    for s in range(2):
                        dve.wait_ge(sem("sl_done"), 2 * i + s + 1)
                        tt(hh_[:, s, :], PS[:, 2 + s, DE:2 * DE], hsl[:, s, :], ALU.mult).then_inc(sem(f"gu_free{s}"), 1)
                    for s in range(2):
                        dve.wait_ge(sem("y_mm"), 2 * i + s + 3)
                        dve.wait_ge(sem(f"yd{s}"), 16 * i + 1)
                        V.tensor_copy(ysb[:, s, 0:512], PS[:, 4 + 2 * s, :]).then_inc(sem("y_ev2"), 1)
            dve.wait_ge(sem("y_all"), 1)
            def finish(t):
                n = rows_of(t)
                y = x1tok[0:n, t, :]
                dve.wait_ge(sem("normed"), t + 1)
                E.step(tt(y, y, lnw[0:n, 2, :], ALU.mult))
                if t >= 2:
                    dve.wait_ge(sem(f"y_out{t % 2}"), 16 * (t // 2))
                E.do(tt(fin[0:n, t % 2, :], y, lnw[0:n, 3, :], ALU.add), sem("fin_done"))

            c = 0
            for t in range(NT):
                n = rows_of(t)
                acc = x1tok[0:n, t, :]
                s = st[0:n, t % 2, :]
                for k in range(TOPK):
                    dve.wait_ge(sem(f"yg{c % 6}"), 16 * (c // 6 + 1))
                    E.step(stt(acc, yg[0:n, c % 6, :], wfin[0:n, t, k:k + 1], acc, ALU.mult, ALU.add), sem("yg_used"))
                    c += 1
                stats(acc, s)
                dve.wait_ge(sem("std_done"), NT + t + 1)
                E.step(V.reciprocal(s[:, 15:16], s[:, 14:15]))
                E.do(stt(s[:, 12:13], s[:, 12:13], -1.0, s[:, 15:16], ALU.mult, ALU.mult), sem("shift_done"))
                if t:
                    finish(t - 1)
            finish(NT - 1)

        @block.gpsimd
        def _(pool):
            G = nc.gpsimd
            pool.wait_ge(x_turned, 2 * NT)
            G.memset(W1.rearrange("p a b c -> p (a b c)"), 0.0)
            G.memset(W2.rearrange("p a b -> p (a b)"), 0.0).then_inc(w1_zero, 1)
            for m in met:
                pool.wait_ge(m, 1)
            G.memset(zrow, 0.0).then_inc(sem("zrow_set"), 1)
            for m in met:
                pool.wait_ge(m, 3)
            pool.wait_ge(sem("y_zero"), 16)
            pool.dma_start(gsel[0:64, 0:3], gate[0:BD, 8, :].rearrange("b (h c) -> b h c", c=3)).then_inc(sem("gsel_in"), 16)

            def pages(cache, b):
                G.indirect_dma_start(out=cpg[:, b % 2, :], out_offset=None, in_=cache.rearrange("n (q s) c -> (n q) (s c)", s=16),
                                     in_offset=bass.IndirectOffsetOnAxis(ap=pgidx[:, b:b + 1], axis=0)).then_inc(sem(f"pg{b % 2}"), 16)

            pool.wait_ge(sem("pg_ready"), 1)
            pool.wait_ge(sem("win_pv"), 1)
            for b in range(BD):
                if b >= 2:
                    pool.wait_ge(sem("dt_done"), G_CMP + 8 * (b - 1))
                pages(a["cmp"], b)
            for b in range(BD):
                if b < 2:
                    pool.wait_ge(sem("dt_done"), G_CMP + 8 * (BD - 1 + b))
                else:
                    pool.wait_ge(sem("dh_done"), BD)
                    pool.wait_ge(sem("ds_done"), 1)
                    pool.wait_ge(sem(f"pg{b % 2}"), 16 * ((b - 2) // 2 + 5))
                    G.tensor_copy(hold[:, b - 2, :, :], cpg[:, b % 2, :].rearrange("p (s c) -> p s c", s=16)[:, :, P:2 * P]).then_inc(sem("held"), 1)
                    pool.wait_ge(sem("held"), b - 1)
                    pool.wait_ge(sem("dt_done"), G_SEL + 4 * (b - 1))
                pages(a["sel"], b)
            pool.wait_ge(sem("table_step"), 2)
            pool.wait_ge(sem("x1_out"), 32)
            for m in met:
                pool.wait_ge(m, 8)
            turns = pool.value_load(nblk[0:1, 0:1], min_val=1, max_val=NBLK // 2)
            with pool.Fori(0, NBLK // 2) as i:
                with pool.If(i < turns):
                    for s in range(2):
                        pool.wait_ge(sem("xgT_mm1"), i * 2 + s + 1)
                        G.tensor_tensor(pause[:, 0:1], izero[:, 0:1], izero[:, 0:1], ALU.add)
                        G.tensor_tensor(idxs[:, s:s + 1], idxall[:, bass.ds(i * 2 + s, 1)], izero[:, 0:1], ALU.add).then_inc(sem(f"ix{s}"), 1)
                        pool.wait_ge(sem(f"ix{s}"), i + 1)
                        G.tensor_tensor(pause[:, 1:2], izero[:, 0:1], izero[:, 0:1], ALU.add)
                        G.indirect_dma_start(out=xg[:, s, :], out_offset=None, in_=x1_dram,
                                             in_offset=bass.IndirectOffsetOnAxis(ap=idxs[:, s:s + 1], axis=0)).then_inc(sem(f"xg{s}"), 16)
            pool.wait_ge(sem("y_all"), 1)
            c = 0
            yrows = y_dram.rearrange("b p d -> (b p) d")
            for t in range(NT):
                n = rows_of(t)
                for k in range(TOPK):
                    if c >= 6:
                        pool.wait_ge(sem("yg_used"), c - 5)
                    G.indirect_dma_start(out=yg[0:n, c % 6, :], out_offset=None, in_=yrows,
                                         in_offset=bass.IndirectOffsetOnAxis(ap=dsti[0:n, t, k:k + 1], axis=0)).then_inc(sem(f"yg{c % 6}"), 16)
                    c += 1


_OUTS = [("y_p", (SEQ, D), (1, SEQ, D)), ("y_s", (BD, D), (BD, 1, D)),
         ("cmp_p", (SEQ, KV), (1, 1, SEQ, 2, 2, HD)), ("cmp_s", (BD, KV), (1, BD, 1, 2, 2, HD)),
         ("sel_p", (SEQ, KV), (1, 1, SEQ, 2, 2, HD)), ("sel_s", (BD, KV), (1, BD, 1, 2, 2, HD)),
         ("win_p", (WINDOW, KV), (1, 1, WINDOW, 2, 2, HD)), ("win_s", (BD, WINDOW, KV), (1, BD, WINDOW, 2, 2, HD)),
         ("conv_p", (3, D), (1, 1, 3, D)), ("conv_s", (BD, 3, D), (1, BD, 3, D)),
         ("rnn_p", (1, D), (1, 1, D)), ("rnn_s", (BD, D), (1, BD, D))]


def kernel(**inputs):
    import numpy as _np
    import concourse.bacc as _bacc
    from concourse import mybir as _mybir
    from concourse.bass_utils import run_bass_kernel_spmd as _run

    v = {k: _np.asarray(x) for k, x in inputs.items()}
    shaped = {
        "x_prompt": v["x_prompt"].reshape(SEQ, D), "x_sample": v["x_sample"].reshape(BD, D),
        "cmp": v["cache_cmp_kv"].reshape(NPOOL, PAGE, KV), "sel": v["cache_sel_kv"].reshape(NPOOL, PAGE, KV),
        "win": v["cache_win_kv"].reshape(BD, WINDOW, KV), "state_conv": v["state_conv"].reshape(BD, 3, D),
        "state_rnn": v["state_rnn"].reshape(BD, D), "page_table": v["page_table"],
        "w1k": v["w_cmp_k1"].reshape(32, HD, HD), "w1v": v["w_cmp_v1"].reshape(32, HD, HD),
        "w2k": v["w_cmp_k2"].reshape(HD, HD), "w2v": v["w_cmp_v2"].reshape(HD, HD),
        "posk": v["cmp_pos_k"].reshape(32, HD), "posv": v["cmp_pos_v"].reshape(32, HD),
        "consts": CONSTS,
    }
    for name in ("w_in", "conv_w", "w_rg_a", "w_rg_i", "w_branch_attn", "w_branch_rnn", "w_out", "w_router",
                 "w_exp_gate", "w_exp_up", "w_exp_down", "w_sh_gate", "w_sh_up", "w_sh_down"):
        shaped[name] = v[name][0]
    for name in ("conv_b", "b_rg_a", "b_rg_i", "lru_lambda", "ln1_g", "ln1_b", "router_bias", "ln2_g", "ln2_b"):
        shaped[name] = v[name].reshape(1, -1)
    nc = _bacc.Bacc("TRN2", target_bir_lowering=False, num_devices=1)
    arrays, a, o = {}, {}, {}
    for name, x in shaped.items():
        x = _np.ascontiguousarray(x)
        arrays[f"in_{name}"] = x
        a[name] = nc.dram_tensor(f"in_{name}", x.shape, _mybir.dt.from_np(x.dtype), kind="ExternalInput").ap()
    for name, shape, _ in _OUTS:
        o[name] = nc.dram_tensor(f"out_{name}", shape, _mybir.dt.float32, kind="ExternalOutput").ap()
    x1_dram = nc.dram_tensor("x1_rows", (NTOK, D), _mybir.dt.float32, kind="Internal").ap()
    y_dram = nc.dram_tensor("expert_rows", (NBLK, P, D), _mybir.dt.float32, kind="Internal").ap()
    build(nc, a, o, x1_dram, y_dram)
    r = _run(nc, [arrays], core_ids=[0])
    return tuple(r.results[0][f"out_{name}"].reshape(final) for name, _, final in _OUTS)
```
